# Optimizing a Trainium2 kernel written in Bass

```python
import functools
import jax, jax.numpy as jnp
from jax import lax
import numpy as np

D_MODEL = 1024
BATCH = 1
SEQ = 512
DEPTH = 2
DEC_BATCH = 8
DEC_SEQ = 4
PAST_LEN = 1024
PAGE_SIZE = 128

D_MIX = D_MODEL
A_WIDTH = D_MIX // 2
A_HD = 64
A_HEADS = A_WIDTH // A_HD
A_KV = 2
A_G = A_HEADS // A_KV
CMP_BLOCK = 64
TOPK = 16
WINDOW = 512
Q_BLOCK = 64
ROPE_THETA = 10000.0
FORCE = float(A_G + 1)
M_WIDTH = D_MIX - A_WIDTH
M_HEADS = 4
M_DV = M_WIDTH // M_HEADS
M_DK = M_DV // 2
M_CHUNK = 64
D_FF = ((8 * D_MODEL) // 3 + 127) // 128 * 128
CONV_W = 3
EPS = 1e-6
IN_SPLITS = (A_HEADS * A_HD, 2 * A_KV * A_HD, 2 * A_KV * A_HD, 2 * A_KV * A_HD, 3 * A_HEADS,
             M_HEADS * M_DK, M_HEADS * M_DK, M_WIDTH, M_WIDTH, 2 * M_HEADS)
IN_WIDTH = sum(IN_SPLITS)

kernel_name = 'nsa_mlstm_convffn_hybrid_step'

F32 = jnp.float32

def rmsnorm(x, g):
    xf = x.astype(F32)
    y = xf * lax.rsqrt(jnp.mean(xf * xf, axis=-1, keepdims=True) + EPS)
    return (y * g.astype(F32)).astype(x.dtype)

def adaln(c, w, b):
    mod = jax.nn.silu(c) @ w + b
    return [m[:, None, :] for m in jnp.split(mod, 6, axis=-1)]

def rope(x, pos):
    d = x.shape[-1]
    half = d // 2
    freq = ROPE_THETA ** (-2.0 * jnp.arange(half, dtype=F32) / d)
    ang = pos.astype(F32)[:, None] * freq[None, :]
    cos = jnp.cos(ang)[None, :, None, :]
    sin = jnp.sin(ang)[None, :, None, :]
    x1 = x[..., :half].astype(F32)
    x2 = x[..., half:].astype(F32)
    return jnp.concatenate([x1 * cos - x2 * sin, x1 * sin + x2 * cos], axis=-1).astype(x.dtype)

def make_kv(z, pos):
    bt, t = z.shape[:2]
    kv = z.reshape(bt, t, 2, A_KV, A_HD)
    return jnp.stack([rope(kv[:, :, 0], pos), kv[:, :, 1]], axis=2)

def block_view(kv):
    bt, length = kv.shape[:2]
    nb = -(-length // CMP_BLOCK)
    kv = jnp.pad(kv, ((0, 0), (0, nb * CMP_BLOCK - length), (0, 0), (0, 0), (0, 0)))
    return kv.reshape(bt, nb, CMP_BLOCK, 2, A_KV, A_HD)

def cmp_means(kv):
    return block_view(kv).astype(F32).mean(axis=2)

def sel_blocks(kv):
    return block_view(kv).transpose(0, 4, 1, 2, 3, 5)

def nsa_cmp_sel(q, cm, sb, q_pos):
    bt, tq = q.shape[:2]
    nb = cm.shape[1]
    scale = A_HD ** -0.5
    qg = q.reshape(bt, tq, A_KV, A_G, A_HD)
    s = jnp.einsum('btkgd,bnkd->btkgn', qg.astype(F32), cm[:, :, 0]) * scale
    blk = jnp.arange(nb)
    cmp_ok = (blk[None, :] + 1) * CMP_BLOCK <= q_pos[:, None] + 1
    s = jnp.where(cmp_ok[None, :, None, None, :], s, -jnp.inf)
    s_max = s.max(axis=-1, keepdims=True)
    e = jnp.exp(s - jnp.where(jnp.isfinite(s_max), s_max, 0.0))
    den = e.sum(axis=-1, keepdims=True)
    p = e / jnp.where(den > 0, den, 1.0)
    o_cmp = jnp.einsum('btkgn,bnkd->btkgd', p, cm[:, :, 1]).reshape(bt, tq, A_HEADS, A_HD).astype(q.dtype)
    imp = p.sum(axis=3)
    cur = q_pos // CMP_BLOCK
    forced = (blk[None, :] == cur[:, None]) | (blk[None, :] == 0)
    allowed = blk[None, :] <= cur[:, None]
    score = jnp.where(forced[None, :, None, :], FORCE, jnp.where(allowed[None, :, None, :], imp, -1.0))
    top_val, top_idx = lax.top_k(score, min(TOPK, nb))
    idx_t = top_idx.transpose(0, 2, 1, 3)
    ok_blk = (top_val >= 0).transpose(0, 2, 1, 3)
    bi = jnp.arange(bt)[:, None, None, None]
    ki = jnp.arange(A_KV)[None, :, None, None]
    g = sb[bi, ki, idx_t]
    kpos = idx_t[..., None] * CMP_BLOCK + jnp.arange(CMP_BLOCK)
    ok = (kpos <= q_pos[None, None, :, None, None]) & ok_blk[..., None]
    qt = qg.transpose(0, 2, 1, 3, 4)
    s2 = jnp.einsum('bktgd,bktsjd->bktgsj', qt, g[..., 0, :]).astype(F32) * scale
    s2 = jnp.where(ok[:, :, :, None], s2, -jnp.inf)
    kk = top_idx.shape[-1]
    p2 = jax.nn.softmax(s2.reshape(bt, A_KV, tq, A_G, kk * CMP_BLOCK), axis=-1).reshape(s2.shape)
    o_sel = jnp.einsum('bktgsj,bktsjd->bktgd', p2.astype(q.dtype), g[..., 1, :])
    o_sel = o_sel.transpose(0, 2, 1, 3, 4).reshape(bt, tq, A_HEADS, A_HD)
    return o_cmp, o_sel

def window_attn(q, kv, q_pos, k_pos):
    bt, tq = q.shape[:2]
    qg = q.reshape(bt, tq, A_KV, A_G, A_HD)
    s = jnp.einsum('btkgd,bskd->btkgs', qg, kv[:, :, 0]).astype(F32) * A_HD ** -0.5
    ok = (k_pos[None, :] <= q_pos[:, None]) & (k_pos[None, :] > q_pos[:, None] - WINDOW) & (k_pos[None, :] >= 0)
    s = jnp.where(ok[None, :, None, None, :], s, -jnp.inf)
    p = jax.nn.softmax(s, axis=-1)
    o = jnp.einsum('btkgs,bskd->btkgd', p.astype(q.dtype), kv[:, :, 1])
    return o.reshape(bt, tq, A_HEADS, A_HD)

def nsa_attend_prompt(q, kv_c, kv_s, kv_w):
    bt, t = q.shape[:2]
    cm = cmp_means(kv_c)
    sb = sel_blocks(kv_s)
    kvw_pad = jnp.pad(kv_w, ((0, 0), (WINDOW, 0), (0, 0), (0, 0), (0, 0)))

    def body(i):
        start = i * Q_BLOCK
        qb = lax.dynamic_slice_in_dim(q, start, Q_BLOCK, axis=1)
        q_pos = start + jnp.arange(Q_BLOCK)
        o_c, o_s = nsa_cmp_sel(qb, cm, sb, q_pos)
        kb = lax.dynamic_slice_in_dim(kvw_pad, start, WINDOW + Q_BLOCK, axis=1)
        k_pos = start - WINDOW + jnp.arange(WINDOW + Q_BLOCK)
        return o_c, o_s, window_attn(qb, kb, q_pos, k_pos)

    outs = lax.map(body, jnp.arange(t // Q_BLOCK))
    o_c, o_s, o_w = [jnp.moveaxis(o, 0, 1).reshape(bt, t, A_HEADS, A_HD) for o in outs]
    return o_c, o_s, o_w, kv_w[:, -min(WINDOW, t):]

def nsa_attend_sample(q, kv_c, kv_s, kv_w, past_c, past_s, win_buf):
    t = q.shape[1]
    wb = win_buf.shape[1]
    q_pos = PAST_LEN + jnp.arange(t)
    full_c = jnp.concatenate([past_c.astype(kv_c.dtype), kv_c], axis=1)
    full_s = jnp.concatenate([past_s.astype(kv_s.dtype), kv_s], axis=1)
    o_c, o_s = nsa_cmp_sel(q, cmp_means(full_c), sel_blocks(full_s), q_pos)
    kw = jnp.concatenate([win_buf.astype(kv_w.dtype), kv_w], axis=1)
    k_pos = PAST_LEN - wb + jnp.arange(wb + t)
    return o_c, o_s, window_attn(q, kw, q_pos, k_pos), kw[:, -wb:]

def mlstm_chunk(state, inp):
    C, n, m = [s.astype(F32) for s in state]
    q, k, v, ig, lf = inp
    L = q.shape[1]
    b = jnp.cumsum(lf, axis=1)
    a = b + m[:, None, :]
    d = b[:, :, None, :] - b[:, None, :, :] + ig[:, None, :, :]
    causal = jnp.tril(jnp.ones((L, L), dtype=bool))
    d = jnp.where(causal[None, :, :, None], d, -jnp.inf)
    m_t = jnp.maximum(a, d.max(axis=2))
    w = jnp.einsum('btnd,bsnd->btsn', q, k) * jnp.exp(d - m_t[:, :, None, :])
    aw = jnp.exp(a - m_t)
    num = jnp.einsum('btsn,bsnv->btnv', w, v) + aw[..., None] * jnp.einsum('btnd,bndv->btnv', q, C)
    den = w.sum(axis=2) + aw * jnp.einsum('btnd,bnd->btn', q, n)
    h = num / jnp.maximum(jnp.abs(den), jnp.exp(-m_t))[..., None]
    b_end = b[:, -1]
    wl = b_end[:, None, :] - b + ig
    m_new = jnp.maximum(b_end + m, wl.max(axis=1))
    decay = jnp.exp(b_end + m - m_new)
    ws = jnp.exp(wl - m_new[:, None, :])
    C_new = decay[:, :, None, None] * C + jnp.einsum('bsn,bsnd,bsnv->bndv', ws, k, v)
    n_new = decay[:, :, None] * n + jnp.einsum('bsn,bsnd->bnd', ws, k)
    return (C_new, n_new, m_new), h

def mlstm_prompt(q, k, v, ig, lf):
    bt, t = q.shape[:2]
    nc = t // M_CHUNK

    def chunks(z):
        return jnp.moveaxis(z.reshape((bt, nc, M_CHUNK) + z.shape[2:]), 1, 0)

    init = (jnp.zeros((bt, M_HEADS, M_DK, M_DV), F32), jnp.zeros((bt, M_HEADS, M_DK), F32),
            jnp.zeros((bt, M_HEADS), F32))
    state, h = lax.scan(mlstm_chunk, init, (chunks(q), chunks(k), chunks(v), chunks(ig), chunks(lf)))
    return jnp.moveaxis(h, 0, 1).reshape(bt, t, M_HEADS, M_DV), state

def mlstm_sample(q, k, v, ig, lf, C, n, m):
    state, h = mlstm_chunk((C, n, m), (q, k, v, ig, lf))
    return h, state

def conv_ffn(xn, buf, w_up, w_conv, b_conv, w_down):
    u, gt = jnp.split(xn @ w_up, 2, axis=-1)
    t = u.shape[1]
    up = jnp.concatenate([buf.astype(u.dtype), u], axis=1)
    conv = b_conv
    for j in range(CONV_W):
        conv = conv + w_conv[j] * up[:, j:j + t]
    y = (jax.nn.silu(conv) * gt) @ w_down
    return y, up[:, -(CONV_W - 1):]

def trunk_layer(x, c, pos, conv_buf, attend, recur, lw):
    n1, n2, wm, bm, wi, bif, mng, wo, wu, wc, bc, wd = lw
    sh1, sc1, g1, sh2, sc2, g2 = adaln(c, wm, bm)
    bt, t = x.shape[:2]
    xn = rmsnorm(x, n1) * (1 + sc1) + sh1
    points = [int(s) for s in np.cumsum(IN_SPLITS)[:-1]]
    a_q, a_kc, a_ks, a_kw, a_g, m_q, m_k, m_v, m_o, m_if = jnp.split(xn @ wi, points, axis=-1)
    q = rope(a_q.reshape(bt, t, A_HEADS, A_HD), pos)
    kv_c, kv_s, kv_w = make_kv(a_kc, pos), make_kv(a_ks, pos), make_kv(a_kw, pos)
    o_c, o_s, o_w, win_state = attend(q, kv_c, kv_s, kv_w)
    gate = jax.nn.sigmoid(a_g.astype(F32)).reshape(bt, t, A_HEADS, 3, 1).astype(x.dtype)
    a_out = (gate[:, :, :, 0] * o_c + gate[:, :, :, 1] * o_s + gate[:, :, :, 2] * o_w).reshape(bt, t, A_WIDTH)
    ifg = (m_if + bif).astype(F32).reshape(bt, t, 2, M_HEADS)
    mq = m_q.astype(F32).reshape(bt, t, M_HEADS, M_DK)
    mk = m_k.astype(F32).reshape(bt, t, M_HEADS, M_DK) * M_DK ** -0.5
    mv = m_v.astype(F32).reshape(bt, t, M_HEADS, M_DV)
    h, mstate = recur(mq, mk, mv, ifg[:, :, 0], jax.nn.log_sigmoid(ifg[:, :, 1]))
    h = h * lax.rsqrt(jnp.mean(h * h, axis=-1, keepdims=True) + EPS) * mng.astype(F32).reshape(M_HEADS, M_DV)
    m_out = jax.nn.sigmoid(m_o) * h.reshape(bt, t, M_WIDTH).astype(x.dtype)
    x = x + g1 * (jnp.concatenate([a_out, m_out], axis=-1) @ wo)
    xn2 = rmsnorm(x, n2) * (1 + sc2) + sh2
    f, new_buf = conv_ffn(xn2, conv_buf, wu, wc, bc, wd)
    x = x + g2 * f
    return x, kv_c, kv_s, win_state, mstate, new_buf

def setup_inputs(seed: int = 0) -> dict:
    key = jax.random.key(seed)
    ks = jax.random.split(key, 26)

    def nrm(k, shape, s=1.0):
        return s * jax.random.normal(k, shape, F32)

    n_pages = PAST_LEN // PAGE_SIZE
    n_used = DEC_BATCH * n_pages
    n_phys = n_used + max(1, n_used // 4)
    win_buf = min(WINDOW, PAST_LEN)
    page_table = jax.random.permutation(ks[0], n_phys)[:n_used].reshape(DEC_BATCH, n_pages).astype(jnp.int32)
    kv_row = (2, A_KV, A_HD)
    kb1, kb2 = jax.random.split(ks[17])
    b_if = jnp.concatenate([nrm(kb1, (DEPTH, M_HEADS), 0.1),
                            jnp.linspace(3.0, 6.0, M_HEADS, dtype=F32)[None, :] + nrm(kb2, (DEPTH, M_HEADS), 0.1)], axis=-1)
    return {
        'x_prompt': nrm(ks[1], (BATCH, SEQ, D_MODEL)),
        'x_sample': nrm(ks[2], (DEC_BATCH, DEC_SEQ, D_MODEL)),
        'cache_cmp_kv': nrm(ks[3], (DEPTH, n_phys, PAGE_SIZE) + kv_row),
        'cache_sel_kv': nrm(ks[4], (DEPTH, n_phys, PAGE_SIZE) + kv_row),
        'cache_win_kv': nrm(ks[5], (DEPTH, DEC_BATCH, win_buf) + kv_row),
        'state_mlstm_C': nrm(ks[6], (DEPTH, DEC_BATCH, M_HEADS, M_DK, M_DV), 0.3),
        'state_mlstm_n': nrm(ks[7], (DEPTH, DEC_BATCH, M_HEADS, M_DK), 0.3),
        'state_mlstm_m': nrm(ks[8], (DEPTH, DEC_BATCH, M_HEADS), 0.5),
        'state_ffn_conv': nrm(ks[9], (DEPTH, DEC_BATCH, CONV_W - 1, D_FF)),
        'page_table': page_table,
        'c_prompt': nrm(ks[10], (BATCH, D_MODEL)),
        'c_sample': nrm(ks[11], (DEC_BATCH, D_MODEL)),
        'norm1_g': 1.0 + nrm(ks[12], (DEPTH, D_MODEL), 0.1),
        'norm2_g': 1.0 + nrm(ks[13], (DEPTH, D_MODEL), 0.1),
        'w_mod': nrm(ks[14], (DEPTH, D_MODEL, 6 * D_MODEL), 0.5 * D_MODEL ** -0.5),
        'b_mod': nrm(ks[15], (DEPTH, 6 * D_MODEL), 0.02),
        'w_in': nrm(ks[16], (DEPTH, D_MODEL, IN_WIDTH), D_MODEL ** -0.5),
        'b_if': b_if,
        'mlstm_norm_g': 1.0 + nrm(ks[18], (DEPTH, M_WIDTH), 0.1),
        'w_out': nrm(ks[19], (DEPTH, D_MIX, D_MODEL), D_MIX ** -0.5),
        'w_up': nrm(ks[20], (DEPTH, D_MODEL, 2 * D_FF), D_MODEL ** -0.5),
        'w_conv': nrm(ks[21], (DEPTH, CONV_W, D_FF), CONV_W ** -0.5),
        'b_conv': nrm(ks[22], (DEPTH, D_FF), 0.02),
        'w_down': nrm(ks[23], (DEPTH, D_FF, D_MODEL), D_FF ** -0.5),
        'final_g': 1.0 + nrm(ks[24], (D_MODEL,), 0.1),
    }

def reference(x_prompt, x_sample, cache_cmp_kv, cache_sel_kv, cache_win_kv, state_mlstm_C, state_mlstm_n,
              state_mlstm_m, state_ffn_conv, page_table, c_prompt, c_sample, norm1_g, norm2_g, w_mod, b_mod,
              w_in, b_if, mlstm_norm_g, w_out, w_up, w_conv, b_conv, w_down, final_g):
    pos_p = jnp.arange(SEQ)
    pos_s = PAST_LEN + jnp.arange(DEC_SEQ)
    xp, xs = x_prompt, x_sample
    conv0 = jnp.zeros((BATCH, CONV_W - 1, D_FF), x_prompt.dtype)
    outs_p = [[] for _ in range(7)]
    outs_s = [[] for _ in range(7)]
    for l in range(DEPTH):
        lw = (norm1_g[l], norm2_g[l], w_mod[l], b_mod[l], w_in[l], b_if[l], mlstm_norm_g[l], w_out[l],
              w_up[l], w_conv[l], b_conv[l], w_down[l])
        xp, kc, ksl, kw, (mc, mn, mm), cb = trunk_layer(xp, c_prompt, pos_p, conv0, nsa_attend_prompt,
                                                        mlstm_prompt, lw)
        for lst, arr in zip(outs_p, (kc, ksl, kw, mc, mn, mm, cb)):
            lst.append(arr)
        past_c = cache_cmp_kv[l][page_table].reshape(DEC_BATCH, -1, 2, A_KV, A_HD)
        past_s = cache_sel_kv[l][page_table].reshape(DEC_BATCH, -1, 2, A_KV, A_HD)
        attend_s = functools.partial(nsa_attend_sample, past_c=past_c, past_s=past_s, win_buf=cache_win_kv[l])
        recur_s = functools.partial(mlstm_sample, C=state_mlstm_C[l], n=state_mlstm_n[l], m=state_mlstm_m[l])
        xs, kc, ksl, kw, (mc, mn, mm), cb = trunk_layer(xs, c_sample, pos_s, state_ffn_conv[l], attend_s,
                                                        recur_s, lw)
        for lst, arr in zip(outs_s, (kc, ksl, kw, mc, mn, mm, cb)):
            lst.append(arr)
    y_prompt = rmsnorm(xp, final_g)
    y_sample = rmsnorm(xs, final_g)
    p_cmp, p_sel, p_win, p_C, p_n, p_m, p_conv = [jnp.stack(a, axis=0) for a in outs_p]
    s_cmp, s_sel, s_win, s_C, s_n, s_m, s_conv = [jnp.stack(a, axis=0) for a in outs_s]
    return (y_prompt, y_sample, p_cmp, p_sel, p_win, p_C, p_n, p_m, p_conv,
            s_cmp, s_sel, s_win, s_C, s_n, s_m, s_conv)


_drawn_inputs = setup_inputs


def setup_inputs(seed=0):
    import zlib

    import numpy as np

    out = dict(_drawn_inputs(seed))
    spreads = {}
    factors = {'cache_cmp_kv': 8.0, 'cache_sel_kv': 5.781, 'mlstm_norm_g': 2.926, 'b_conv': 8.0}
    for name, (base, spread) in spreads.items():
        noise = np.random.default_rng([zlib.crc32(name.encode()), seed]).standard_normal(out[name].shape)
        drawn = base * np.exp(spread * noise) if base else spread * noise
        out[name] = __import__('jax').numpy.asarray(drawn.astype(out[name].dtype))
    for name, factor in factors.items():
        out[name] = (out[name] * factor).astype(out[name].dtype)
    return out
```

```python
import numpy as np
import concourse.bass as bass
from concourse import mybir
from contextlib import ExitStack

D = 1024
SEQ = 512
DEPTH = 2
NB = 8
NT = 4
PAST = 1024
PAGE = 128
N_PHYS = 80
HD = 64
AH = 8
KV = 2
AG = AH // KV
BLK = 64
WINDOW = 512
MH = 4
DK = 64
DV = 128
FF = 2816
EPS = 1e-6
KC = D // 128
TS = NB * NT
TT = SEQ + TS
HALF = TT // 2
PT_ = SEQ // 128
NPG = PAST // PAGE
NEG = -1e30
C_Q, C_KC, C_KS, C_KW, C_G = 0, 512, 768, 1024, 1280
C_MQ, C_MK, C_MV, C_MO, C_IF = 1304, 1560, 1816, 2328, 2840
IN_W = 2848
IN_SLABS = [(512 * i, min(512, IN_W - 512 * i)) for i in range(6)]
FC = FF // 128
U = 16
UPW = 2 + SEQ + NB * (NT + 2)

_NAMES = ["ident", "ones", "causal", "causalT", "cos", "sin", "cmpadd", "cmp01", "ind8", "ind64", "hmask",
          "ind2", "slide", "sum32", "samegroup", "iota", "newadd", "winadd", "tokrow", "hsel", "rowtok",
          "onehot", "samebatch", "inbatch", "inbatchT", "lastT"]
_SEQ_NAMES = ["seg", "pen"]


def shape_constants():
    f = np.float32
    p = np.arange(128)
    c = {}
    c["ident"] = np.eye(128, dtype=f)
    c["ones"] = np.ones((128, 128), f)
    c["causal"] = np.where(p[None, :] <= p[:, None], 0, NEG).astype(f)
    c["causalT"] = np.where(p[None, :] >= p[:, None], 0, NEG).astype(f)
    half = HD // 2
    freq = np.power(f(10000.0), (f(-2.0) * np.arange(half, dtype=f) / f(HD))).astype(f)
    pos = np.concatenate([np.arange(SEQ).reshape(PT_, 128), (PAST + p % NT)[None]]).astype(f)
    ang = (pos.T[:, :, None] * freq[None, None, :]).astype(f)
    c["cos"] = np.cos(ang).astype(f)
    c["sin"] = np.sin(ang).astype(f)
    tok = np.arange(SEQ).reshape(PT_, 128).T
    ok = (np.arange(8)[None, None, :] + 1) * BLK <= tok[:, :, None] + 1
    c["cmpadd"] = np.where(ok, 0, NEG).astype(f)
    c["cmp01"] = ok.astype(f)
    ind8 = (tok[:, :, None] // BLK == np.arange(8)[None, None, :]) / f(BLK)
    c["ind8"] = ind8.astype(f)
    c["ind64"] = np.tile(ind8[:, :, None, :], (1, 1, 8, 1)).astype(f)
    c["hmask"] = (p[:, None] // 8 == np.arange(8)[None, :]).astype(f)
    c["ind2"] = ((p[:, None] // BLK == np.arange(2)[None, :]) / f(BLK)).astype(f)
    slide = np.zeros((128, 126), f)
    slide[:, 62:64] = c["ind2"]
    c["slide"] = slide
    c["sum32"] = (p[:, None] % 32 == np.arange(32)[None, :]).astype(f)
    rb, rk, rg, rt = p // 32, p // 16 % 2, p // 4 % 4, p % 4
    key = rb * 8 + rk * 4 + rt
    c["samegroup"] = (key[:, None] == key[None, :]).astype(f)
    c["iota"] = np.tile(np.arange(1, 16, dtype=f), (128, 1))
    tb, tt = np.arange(TS) // NT, np.arange(TS) % NT
    grp = np.arange(2)
    same = (grp[None, :, None] * 4 + rb[:, None, None]) == tb[None, None, :]
    c["newadd"] = np.where(same & (tt[None, None, :] <= rt[:, None, None]), 0, NEG).astype(f)
    c["winadd"] = np.where(np.arange(4)[None, :] > rt[:, None], 0, NEG).astype(f)
    match = same & (tt[None, None, :] == rt[:, None, None])
    t32 = np.zeros((128, 2, 128), f)
    t32[:TS] = match.transpose(2, 1, 0)
    c["tokrow"] = t32
    head = rk * 4 + rg
    c["hsel"] = (head[:, None] == np.arange(8)[None, :]).astype(f)
    c["rowtok"] = (match[:, :, None, :] * c["hsel"][:, None, :, None]).astype(f)
    oh = np.zeros((128, MH, 128), f)
    for h in range(MH):
        oh[h, h] = 1
    c["onehot"] = oh
    seg = np.ones(TT, f)
    seg[SEQ::NT] = 0
    c["seg"] = np.tile(seg, (128, 1))
    c["pen"] = np.tile(np.where(seg == 0, NEG, 0).astype(f), (128, 1))
    sb = np.full((128, TS), NEG, f)
    sb[:TS] = np.where((tb[:, None] == tb[None, :]) & (tt[None, :] >= tt[:, None]), 0, NEG)
    c["samebatch"] = sb
    c["inbatch"] = np.tile((np.arange(NB)[:, None] == tb[None, :]).astype(f)[None], (128, 1, 1))
    it = np.zeros((128, NB), f)
    it[:TS] = tb[:, None] == np.arange(NB)[None, :]
    c["inbatchT"] = it
    lt = np.zeros((128, NB), f)
    lt[:TS] = (tb[:, None] == np.arange(NB)[None, :]) & (tt[:, None] == NT - 1)
    c["lastT"] = lt
    return [np.ascontiguousarray(c[n].reshape(128, -1), dtype=f) for n in _NAMES + _SEQ_NAMES]


_WIDTHS = [a.shape[1] for a in shape_constants()][:len(_NAMES)]


def trunk_program(nc, A, O):
    F = mybir.dt.float32
    I32 = mybir.dt.int32
    ACT = mybir.ActivationFunctionType
    ALU = mybir.AluOpType
    X = mybir.AxisListType.X
    (y_p, y_s, p_cmp, p_sel, p_win, p_C, p_n, p_m, p_conv,
     s_cmp, s_sel, s_win, s_C, s_n, s_m, s_conv) = O
    ctx = ExitStack()
    with ctx:
        def sb(name, shape, dt=F):
            return ctx.enter_context(nc.sbuf_tensor(name, shape, dt))

        cst = sb("shape_constants", [128, sum(_WIDTHS)])
        at, K = 0, {}
        for n, w in zip(_NAMES, _WIDTHS):
            K[n] = cst[:, at:at + w]
            at += w
        ident, ones = K["ident"], K["ones"]

        def view(name, pattern, **kw):
            return K[name].rearrange(pattern, **kw)

        cos, sin = view("cos", "p (t d) -> p t d", t=5), view("sin", "p (t d) -> p t d", t=5)
        xT = sb("xT", [128, KC, TT])
        xnT = sb("xnT", [128, KC, TT])
        NSLAB = 3
        slab = [sb(f"slab{i}", [128, 4096]) for i in range(NSLAB)]
        big = sb("big", [128, 12288])
        proj = big[:, 0:PT_ * IN_W].rearrange("p (t n) -> p t n", t=PT_)
        hT = big[:, 0:FC * TT].rearrange("p (c n) -> p c n", c=FC)
        proj_s = sb("proj_s", [TS, IN_W])
        work = sb("work", [128, 10496])
        cT = sb("cT", [128, KC, 32])
        modT = sb("modT", [128, 48, 9])
        scale_n = sb("scale_n", [128, KC, 9])
        colsA = sb("colsA", [128, 64])
        colsB = sb("colsB", [128, 96])
        rows_bc = sb("rows_bc", [128, 512 + 8])
        rstd = sb("rstd", [128, TT])
        gates = sb("gates", [128, PT_, 24])
        gates_s = sb("gates_s", [TS, 24])
        aTs = sb("aTs", [128, 4, TS])
        RT = sb("RT", [128, 5, 4, MH])
        ybuf = big[:, 0:5120].rearrange("p (n d) -> p n d", n=10)
        pages_sb = sb("pages_sb", [1, NB * NPG], I32)
        seqc = work[0:MH, 9216:9216 + 2 * TT].rearrange("p (a n) -> p a n", a=2)
        ps = [ctx.enter_context(nc.psum_tensor(f"ps{i}", [128, 512], F)) for i in range(8)]

        class carve:
            def __init__(self, region):
                self.r, self.at = region, 0

            def __call__(self, *shape):
                n = int(np.prod(shape))
                a = self.r[:, self.at:self.at + n]
                self.at += n
                assert self.at <= self.r.shape[1], (self.at, self.r.shape)
                if len(shape) == 1:
                    return a
                names = "abcd"[:len(shape)]
                return a.rearrange(f"p ({' '.join(names)}) -> p {' '.join(names)}",
                                   **{names[i]: shape[i] for i in range(1, len(shape))})

        w = carve(work)
        modp, rowsA, rowsB = w(NSLAB, 512), w(128), w(128)
        crow, crow2 = w(D), w(D)
        xrow = w(4, D)
        w = carve(work)
        sq = w(2, TT)
        dpart = w(2, 512)
        w = carve(work)
        mqk = w(8, SEQ)
        kw = w(PT_, MH * DK)
        E, W = w(1280), w(1280)
        Cp = w(MH, DV + 1)
        hden, hvar = w(4), w(16)
        rope_t = w(4, 256)
        rr = xnT[0:MH, :, :]
        row8 = big[0:MH, PT_ * IN_W:PT_ * IN_W + TT]
        negG_s = sb("neg_g_decode", [MH, TS])
        m0s = sb("m0s", [MH, NB])
        mqks = sb("mqks", [64, 8, TS])
        w = carve(work)
        TH = w(12, SEQ)
        qs, Pb, PTb = w(2, SEQ), w(2, SEQ), w(2, SEQ)
        cS = w(256)
        KmT, VmBD = w(16), w(512)
        sm = w(96)
        gnow = w(PT_, 2, 2)
        nmax, den = w(U), w(U)
        rg = w(2)
        w = carve(work)
        KT = w(2, 1024)
        Ssb, PTs = w(1024 + TS), w(9, 128)
        qTs, Qbd, KN = w(4, TS), w(4, 32), w(2, TS)
        cmb, imp, rownow = w(128), w(96), w(8, TS)
        P4 = imp[:, 32:96]
        small = w(64)
        PTc = w(128)
        KmTd, Vmd = sb("decode_k_means", [128, NB, 16]), sb("decode_v_means", [64, 2, 128])
        paged = lambda a: a.rearrange("p (n c) -> p n c", c=256)
        cpg = [paged(slab[0][:, 2048 * i:2048 * i + 2048]) for i in range(2)]
        spg = [paged((slab[1], slab[2], slab[0], big)[b // 2][:, 2048 * (b % 2):2048 * (b % 2) + 2048]) for b in range(NB)]
        wpg = [paged(big[:, 4096 + 1024 * b:4096 + 1024 * b + 1024]) for b in range(NB)]
        w = carve(big)
        Cst, nst, Cnew = w(NB * MH, DV), w(NB * MH), w(NB * MH, DV)
        nnew, decayb = w(NB * MH), w(NB * MH)
        w = carve(work)
        Qm, kwb, Es, Ws = w(NB, TS), w(NB, DK), w(TS), w(TS)
        hs, hs2, h_small = w(512), w(512), w(32)
        nd = w(DV + 1)
        kws = w(MH * DK)[0:TS, :]
        awl = w(NB, MH)
        gq = sb("gq", [128, 2, 3])
        gq_now = sb("gq_now", [128, 3])
        w = carve(work)
        w.at = 2 * TT
        convS = w(FC, 16)
        uLast = w(FC, 18)
        up, cv = w(2, UPW), w(2, UPW)
        cwt, cbias = w(6), w(2)
        ulrow = w(FF)
        csrow = w(FF)

        passed = ctx.enter_context(nc.semaphore("register_waits_passed"))

        def stand_alone(eng):
            eng.sem_inc(passed, 1)

        class Signal:
            def __init__(self, name, per_iter, trips=1, credit=0):
                self.sem = ctx.enter_context(nc.semaphore(name))
                self.name, self.per_iter, self.trips, self.credit = name, per_iter, trips, credit

            def at(self, k, L=0, j=0):
                k = k + self.credit
                assert not isinstance(k, int) or k >= 1, self.name
                return L * (self.per_iter * self.trips) + j * self.per_iter + k

        sig = Signal

        N_FENCE = 15

        stage_done = ctx.enter_context(nc.semaphore("stage_done"))

        def stage_end(n, L):
            return L * (4 * N_FENCE) + 4 * n

        PRO_LOADS = 16 * 6
        pro_silu, pro_ct = ctx.enter_context(nc.semaphore("c_silu")), ctx.enter_context(nc.semaphore("c_transposed"))
        pro_xt = ctx.enter_context(nc.semaphore("x_transposed"))
        pro_copy_p, pro_copy_s = ctx.enter_context(nc.semaphore("x_copied_prompt")), ctx.enter_context(nc.semaphore("x_copied_decode"))
        load_in = ctx.enter_context(nc.semaphore("prologue_loaded"))
        final_sq, final_used = sig("final_squared", KC), sig("final_square_summed", KC)
        final_sum, final_var, final_sqrt, final_rstd = (sig("final_sum", 1), sig("final_var", 1),
                                                        sig("final_sqrt", 1), sig("final_rstd", 1))
        final_tr, final_copy, final_xn = sig("final_transposed", 10), sig("final_copied", 10), sig("final_scaled", KC)
        stored = ctx.enter_context(nc.semaphore("outputs_stored"))

        STAGES = [("mod", 12), ("in", 6), ("pages", 3), ("out", 2), ("up", 11), ("down", 8)]
        PARTS = {"mod": 1, "in": 1, "pages": 0, "out": 1, "up": 2, "down": 1}
        uses, dmas = [0] * NSLAB, [0] * NSLAB
        first_use, first_dma = {}, {}
        for name, n in STAGES:
            for s in range(NSLAB):
                first_use[name, s], first_dma[name, s] = uses[s], dmas[s]
                uses[s] += len(range(s, n, NSLAB))
                dmas[s] += PARTS[name] * len(range(s, n, NSLAB))
        slab_in = [ctx.enter_context(nc.semaphore(f"slab{s}_loaded")) for s in range(NSLAB)]
        slab_out = [ctx.enter_context(nc.semaphore(f"slab{s}_used")) for s in range(NSLAB)]

        def slab_loads(stage, i, L, j=0):
            s, m = i % NSLAB, PARTS[stage]
            return L * (16 * dmas[s]) + j * (16 * m) + 16 * (first_dma[stage, s] + m * (i // NSLAB + 1))


        mod_acc, mod_copy = sig("mod_accumulated", 3, 4), sig("mod_part_copied", 3, 4)
        rows_in = ctx.enter_context(nc.semaphore("layer_rows_loaded"))
        ROWS_PER_LAYER = 16 * 10
        rows_tr = sig("rows_transposed", 1)
        NRM = {}
        for nm in ("n1", "n2"):
            NRM[nm] = dict(sq=sig(nm + "_squared", KC), used=sig(nm + "_square_summed", KC), sum=sig(nm + "_sum", 1),
                           var=sig(nm + "_var", 1), root=sig(nm + "_sqrt", 1), xr=sig(nm + "_scaled", KC))
        N_IN = 6 * 5
        IN_ORDER = [n for i in range(6) for n in ([5 * i, 5 * i - 1] if i else [0]) + [5 * i + t for t in (1, 2, 3)]] + [N_IN - 1]
        dp_acc, dp_copy = sig("decode_parts_accumulated", 6), sig("decode_parts_copied", 6)
        in_acc = sig("in_accumulated", N_IN)
        in_act, in_dve = sig("in_copied_act", N_IN // 2), sig("in_copied_dve", N_IN // 2)
        if_ready, if_tr = sig("if_gates_ready", 1), sig("if_gates_transposed", 1)
        ml_abs, ml_ln = sig("forget_abs", 1), sig("forget_ln", 1)
        ml_rows, ml_exp, ml_colt, ml_col = sig("mlstm_rows_ready", 1), sig("mlstm_rows_exp", 1), sig("mlstm_cols_transposed", 1), sig("mlstm_cols_ready", 1)
        mt_tr, mt_cp = sig("mlstm_heads_transposed", 9), sig("mlstm_heads_copied", 9)
        ml_g, ml_qk = sig("neg_g_spread", MH), sig("mlstm_qk", MH * 4)
        ml_diag, ml_E, ml_W = sig("mlstm_diag_masked", MH), sig("mlstm_decay_ready", MH * 4), sig("mlstm_w_ready", MH * 4)
        ml_num, ml_numc = sig("mlstm_num", MH), sig("mlstm_num_copied", MH)
        ml_kw, k_scaled, roped = sig("mlstm_kw_ready", 1), sig("mlstm_k_scaled", 1), sig("roped", 1)
        h_var, h_root = sig("head_var", 1), sig("head_sqrt", 1)
        hs_var, hs_root = sig("dec_head_var", 1), sig("dec_head_sqrt", 1)
        ms_kq, ms_q = sig("dec_keys_weighted", 1), sig("dec_q_spread", MH)
        ml_Cc = sig("mlstm_state_copied", MH)
        th_tr, th_act, th_dve = sig("heads_transposed", 12), sig("heads_copied_act", 6), sig("heads_copied_dve", 6)
        cm_mean, cm_meanc = sig("block_means", 1), sig("block_means_copied", 1)
        cm_s, cm_sub, cm_exp, cm_p = sig("cmp_scores", 1), sig("cmp_shifted", 1), sig("cmp_exp", 1), sig("cmp_probs", 1)
        cm_t, cm_tc, cm_o = sig("cmp_probs_transposed", 1), sig("cmp_probsT_copied", 1), sig("cmp_out", 1)
        q_stage, g_stage = sig("q_staged", 1, 4), sig("gates_staged", 1, 4)
        a_s, a_max, a_exp = sig("attn_scores", U, 4), sig("attn_max", U, 4), sig("attn_exp", U, 4)
        a_t, a_tc, a_pv, a_acc = (sig("attn_probs_transposed", U, 4), sig("attn_probsT_copied", U, 4),
                                  sig("attn_pv", U, 4), sig("attn_added", U, 4))
        mx_t, mx_c = sig("mix_transposed", 8), sig("mix_copied", 8)
        d_pair = sig("dec_q_paired", 1)
        d_tr = sig("dec_heads_transposed", 1)
        cpg_in = [ctx.enter_context(nc.semaphore(f"cmp_pages{s}_loaded")) for s in range(2)]
        spg_in = [ctx.enter_context(nc.semaphore(f"sel_pages{g}_loaded")) for g in range(NB // 2)]
        wpg_in = [ctx.enter_context(nc.semaphore(f"win_rows{j}_loaded")) for j in range(2)]
        d_cm = sig("dec_means", NB)
        d_q = sig("dec_q_ready", 1, 2)
        d_cs = sig("dec_cmp_scores", 1, 2)
        d_csub, d_cexp, d_cp = sig("dec_cmp_shifted", 1, 2), sig("dec_cmp_exp", 1, 2), sig("dec_cmp_probs", 1, 2)
        d_imp = sig("dec_importance", 1, 2)
        d_ct, d_ctc, d_co = sig("dec_cmp_probs_transposed", 1, 2), sig("dec_cmp_probsT_copied", 1, 2), sig("dec_cmp_out", 1, 2)
        d_kt, d_ktc = sig("dec_k_transposed", 12, 2), sig("dec_k_copied", 12, 2)
        d_s, d_max, d_exp = sig("dec_scores", 2, 2), sig("dec_max", 2, 2), sig("dec_exp", 2, 2)
        d_pt, d_ptc, d_pv = sig("dec_probs_transposed", 2, 2), sig("dec_probsT_copied", 2, 2), sig("dec_pv", 2, 2)
        d_cmb, d_out, d_add = sig("dec_combined", 1, 2), sig("dec_out", 1, 2), sig("dec_added", 1, 2)
        st_in = ctx.enter_context(nc.semaphore("decode_state_loaded"))
        ms_g, ms_E, ms_W = sig("dec_neg_g_spread", MH), sig("dec_decay_masked", MH), sig("dec_decay_exp", MH)
        ms_Wd, ms_num, ms_numc = sig("dec_w_ready", MH), sig("dec_num", MH), sig("dec_num_copied", MH)
        ms_C, ms_Cc = sig("dec_state", MH * 2), sig("dec_state_copied", MH * 2)
        ms_dec = sig("dec_decay_spread", 1)
        ms_t, ms_tc = sig("dec_mix_transposed", 1), sig("dec_mix_copied", 1)
        o_acc, o_add = sig("out_accumulated", 8), sig("out_added", 8)
        cv_in, cv_t = ctx.enter_context(nc.semaphore("conv_history_loaded")), sig("history_transposed", 1)
        u_acc, u_cp, u_cv, u_si, u_h = (sig("up_accumulated", 22), sig("u_copied", 22), sig("conv_done", 22, credit=2),
                                        sig("silu_done", 22), sig("hidden_done", 22, credit=2))
        y_acc, y_add = sig("down_accumulated", 8), sig("down_added", 8, credit=3)
        ul_t, ul_c = sig("tail_transposed", FC), sig("tail_copied", FC)

        block = ctx.enter_context(nc.Block())

        @block.sync
        def _(sp):
            wmod = A["w_mod"].rearrange("l (k p) n -> l p k n", p=128)
            win = A["w_in"].rearrange("l (k p) n -> l p k n", p=128)
            wout = A["w_out"].rearrange("l (k p) n -> l p k n", p=128)
            wup = A["w_up"].rearrange("l (k p) (h n) -> l p k h n", p=128, h=2)
            wdn = A["w_down"].rearrange("l (k p) n -> l p k n", p=128)

            sp.wait_ge(load_in, PRO_LOADS)
            flat = lambda a: a.rearrange("l n p a k d -> (l n) p (a k d)")
            cmp_pool, sel_pool = flat(A["cache_cmp_kv"]), flat(A["cache_sel_kv"])

            with sp.Fori(0, DEPTH) as L:
                def pages(dst, src, b, sem):
                    for p in range(NPG):
                        pg = sp.value_load(pages_sb[0:1, NPG * b + p:NPG * b + p + 1], min_val=0, max_val=N_PHYS - 1)
                        sp.dma_start(dst[:, p, :], src[bass.ds(pg + L * N_PHYS, 1)].squeeze(0)).then_inc(sem, 16)

                def load(stage, i, copies, j=0):
                    s = i % NSLAB
                    sp.wait_ge(slab_out[s], L * uses[s] + j + (first_use[stage, s] + i // NSLAB) + 1)
                    for dst, src in copies:
                        sp.dma_start(dst, src).then_inc(slab_in[s], 16)

                def sl(i, n, wd):
                    return slab[i % NSLAB][:, 0:n * wd].rearrange("p (k n) -> p k n", k=n)

                with sp.Fori(0, 4) as j:
                    for i in range(3):
                        load("mod", i, [(sl(i, 8, 512), wmod[L, :, :, bass.ds(j * 1536 + 512 * i, 512)])], j)
                for i, (c0, cw) in enumerate(IN_SLABS):
                    load("in", i, [(sl(i, 8, cw), win[L, :, :, c0:c0 + cw])])
                for b in range(NB):
                    if b in (0, 2, 4):
                        load("pages", b // 2, [])
                        stand_alone(sp)
                    if b in (2, 4):
                        for bb in (b - 2, b - 1):
                            pages(spg[bb], sel_pool, bb, spg_in[bb // 2])
                    if b >= 2:
                        sp.wait_ge(d_cm.sem, d_cm.at(b - 1, L))
                        stand_alone(sp)
                    pages(cpg[b % 2], cmp_pool, b, cpg_in[b % 2])
                for b in (4, 5):
                    sp.wait_ge(d_cm.sem, d_cm.at(b + 3, L))
                    stand_alone(sp)
                    pages(spg[b], sel_pool, b, spg_in[b // 2])
                sp.wait_ge(mx_t.sem, mx_t.at(8, L))
                stand_alone(sp)
                for b in (6, 7):
                    pages(spg[b], sel_pool, b, spg_in[b // 2])
                for i in range(2):
                    load("out", i, [(sl(i, 8, 512), wout[L, :, :, 512 * i:512 * i + 512])])
                for i in range(11):
                    dst = slab[i % NSLAB][:, :].rearrange("p (k h n) -> p k h n", k=8, h=2)
                    load("up", i, [(dst[:, :, h, :], wup[L, :, :, h, 256 * i:256 * i + 256]) for h in range(2)])
                for i in range(8):
                    load("down", i, [(sl(i, FC, 128), wdn[L, :, :, 128 * i:128 * i + 128])])

        @block.tensor
        def _(pe):
            mm, tr = nc.tensor.matmul, nc.tensor.transpose

            def idn(n):
                return ident[0:n, 0:n]

            for s in range(NSLAB):
                pe.sem_inc(slab_out[s], 1)
            pe.wait_ge(load_in, PRO_LOADS)
            pe.wait_ge(pro_silu, 1)
            for k in range(KC):
                ins = tr(ps[7][:, 9 * k:9 * k + 9], crow[0:9, 128 * k:128 * k + 128], idn(9))
            ins.then_inc(pro_ct, 1)
            for k in range(KC):
                if k >= 3:
                    pe.wait_ge(pro_copy_p, k - 2)
                    pe.wait_ge(pro_copy_s, k - 2)
                for t in range(PT_):
                    tr(ps[2 * (k % 3)][:, 128 * t:128 * t + 128], xrow[:, t, 128 * k:128 * k + 128], ident)
                tr(ps[2 * (k % 3) + 1][:, 0:TS], crow2[0:TS, 128 * k:128 * k + 128], idn(TS)).then_inc(pro_xt, 1)

            def norm_sums(S, L=0, frees=None):
                for k in range(KC):
                    pe.wait_ge(S["sq"].sem, S["sq"].at(k + 1, L))
                    for b in range(2):
                        ins = mm(ps[b][:, 0:HALF], ones, sq[:, k % 2, HALF * b:HALF * b + HALF],
                                 start=k == 0, stop=k == KC - 1)
                        if frees is not None and k == 0 and b == 0:
                            ins.then_inc(slab_out[frees], 1)
                    ins.then_inc(S["used"].sem, 1)

            with pe.Fori(0, DEPTH) as L:
                pe.drain().then_inc(stage_done, 1)
                pe.wait_ge(stage_done, stage_end(1, L))
                stand_alone(pe)
                pe.wait_ge(rows_in, L * ROWS_PER_LAYER + ROWS_PER_LAYER)
                stand_alone(pe)
                tr(ps[6][:, 0:64], rowsA[0:64, :], idn(64))
                tr(ps[6][:, 64:160], rowsB[0:96, :], idn(96)).then_inc(rows_tr.sem, 1)
                sel9 = K["sum32"][:, 0:9]
                with pe.Fori(0, 4) as j:
                    def part(i):
                        pe.wait_ge(slab_in[i % NSLAB], slab_loads("mod", i, L, j))
                        wv = slab[i][:, :].rearrange("p (k n) -> p k n", k=8)
                        for r in range(2):
                            for q in range(4):
                                k = 4 * r + q
                                ins = mm(ps[i][32 * q:32 * q + 32, :], cT[:, k, :], wv[:, k, :], start=r == 0,
                                         stop=r == 1, tile_position=(0, 32 * q), skip_group_check=True)
                                if k == 0 and i == 1:
                                    ins.then_inc(slab_out[0], 1)
                        ins.then_inc(mod_acc.sem, 1)

                    def gather(i):
                        pe.wait_ge(mod_copy.sem, mod_copy.at(i + 1, L, j))
                        for c in range(4):
                            ins = mm(ps[7][:, bass.ds(j * 108 + 36 * i + 9 * c, 9)], modp[:, i, 128 * c:128 * c + 128],
                                     sel9, start=True, stop=True)
                        if i < 2:
                            ins.then_inc(slab_out[i + 1], 1)
                    part(0)
                    part(1)
                    gather(0)
                    part(2)
                    gather(1)
                    gather(2)
                pe.drain().then_inc(stage_done, 1)
                pe.wait_ge(stage_done, stage_end(2, L))
                stand_alone(pe)
                norm_sums(NRM["n1"], L)
                pe.drain().then_inc(stage_done, 1)
                pe.wait_ge(stage_done, stage_end(3, L))
                stand_alone(pe)
                def bank_free(n):
                    if n >= 8:
                        m = n - 8
                        copied = in_act if m % 2 == 0 else in_dve
                        pe.wait_ge(copied.sem, copied.at(m // 2 + 1, L))

                def sum_parts(i):
                    n, cw = 5 * i + 4, IN_SLABS[i][1]
                    pe.wait_ge(dp_copy.sem, dp_copy.at(i + 1, L))
                    mm(ps[n % 8][0:TS, 0:cw], K["sum32"], dpart[:, i % 2, 0:cw], start=True, stop=True).then_inc(in_acc.sem, 1)

                for i, (c0, cw) in enumerate(IN_SLABS):
                    pe.wait_ge(slab_in[i % NSLAB], slab_loads("in", i, L))
                    wv = slab[i % NSLAB][:, 0:8 * cw].rearrange("p (k n) -> p k n", k=8)
                    for t in range(4):
                        n = 5 * i + t
                        bank_free(n)
                        for k in range(KC):
                            ins = mm(ps[n % 8][:, 0:cw], xnT[:, k, 128 * t:128 * t + 128], wv[:, k, :],
                                     start=k == 0, stop=k == KC - 1)
                            if i and t == 0 and k == 0:
                                ins.then_inc(slab_out[(i - 1) % NSLAB], 1)
                        ins.then_inc(in_acc.sem, 1)
                        if i and t == 0:
                            sum_parts(i - 1)
                    bank_free(5 * i + 4)
                    for r in range(2):
                        for q in range(4):
                            ins = mm(ps[(5 * i + 4) % 8][32 * q:32 * q + 32, 0:cw], xnT[:, 4 * r + q, SEQ:TT],
                                     wv[:, 4 * r + q, :], start=r == 0, stop=r == 1, tile_position=(0, 32 * q),
                                     skip_group_check=True)
                    ins.then_inc(dp_acc.sem, 1)
                sum_parts(5)
                pe.drain().then_inc(stage_done, 1)
                pe.wait_ge(stage_done, stage_end(4, L))
                stand_alone(pe)
                def block_means(b):
                    pe.wait_ge(cpg_in[b % 2], L * (4 * 16 * NPG) + 16 * NPG * (b // 2 + 1))
                    for p in range(NPG):
                        mm(ps[6][:, 16 * b + 2 * p:16 * b + 2 * p + 2], cpg[b % 2][:, p, 0:128], K["ind2"], start=True, stop=True)
                    for p in range(NPG):
                        r = 16 * (b % 4) + 2 * p
                        ins = mm(ps[7][0:64, 256 + 128 * (b // 4):384 + 128 * (b // 4)], K["slide"][:, 62 - r:126 - r],
                                 cpg[b % 2][:, p, 128:256], start=b % 4 == 0 and p == 0, stop=b % 4 == 3 and p == NPG - 1)
                    ins.then_inc(d_cm.sem, 1)

                pe.wait_ge(if_ready.sem, if_ready.at(1, L))
                for half in range(2):
                    c = C_IF + MH * half
                    for t in range(PT_):
                        ins = tr(ps[half][0:MH, 128 * t:128 * t + 128], proj[:, t, c:c + MH], ident)
                        if half == 0 and t == 0:
                            ins.then_inc(slab_out[5 % NSLAB], 1)
                    ins = tr(ps[2][0:MH, 32 * half:32 * half + TS], proj_s[:, c:c + MH], idn(TS))
                ins.then_inc(if_tr.sem, 1)
                pe.wait_ge(k_scaled.sem, k_scaled.at(1, L))
                stand_alone(pe)
                for n in range(8):
                    c = (C_MQ if n < 4 else C_MK) + DK * (n % 4)
                    b = 4 + n % 2
                    if n >= 2:
                        pe.wait_ge(mt_cp.sem, mt_cp.at(n - 1, L))
                        stand_alone(pe)
                    for t in range(PT_):
                        ins = tr(ps[b][0:64, 128 * t:128 * t + 128], proj[:, t, c:c + DK], ident)
                    ins.then_inc(mt_tr.sem, 1)
                pe.wait_ge(mt_cp.sem, mt_cp.at(7, L))
                stand_alone(pe)
                for n in range(8):
                    c = (C_MQ if n < 4 else C_MK) + DK * (n % 4)
                    ins = tr(ps[4][0:64, TS * n:TS * n + TS], proj_s[:, c:c + DK], idn(TS))
                ins.then_inc(mt_tr.sem, 1)
                block_means(0)
                block_means(1)
                pe.wait_ge(ml_exp.sem, ml_exp.at(1, L))
                stand_alone(pe)
                for t in range(5):
                    M = 128 if t < 4 else TS
                    for q in range(4):
                        ins = tr(ps[3][0:M, 16 * t + 4 * q:16 * t + 4 * q + 4], rr[:, q, 128 * t:128 * t + M], idn(MH))
                ins.then_inc(ml_colt.sem, 1)
                pe.drain().then_inc(stage_done, 1)
                pe.wait_ge(stage_done, stage_end(5, L))
                stand_alone(pe)
                pe.wait_ge(ml_kw.sem, ml_kw.at(1, L))
                for h in range(MH):
                    if h:
                        pe.wait_ge(ml_E.sem, ml_E.at(4 * h, L))
                    mm(ps[0][:, :], view("onehot", "p (h n) -> p h n", h=MH)[0:MH, h, :], rr[:, 7, 0:SEQ],
                                start=True, stop=True).then_inc(ml_g.sem, 1)
                    for i in range(PT_):
                        n = 128 * (PT_ - i)
                        if h * 4 + i >= 2:
                            pe.wait_ge(ml_W.sem, ml_W.at(h * 4 + i - 1, L))
                        mm(ps[1 + i % 2][:, 0:n], mqk[0:64, 4 + h, 128 * i:128 * i + 128],
                                     mqk[0:64, h, 128 * i:SEQ], start=True, stop=True).then_inc(ml_qk.sem, 1)
                    if h:
                        block_means(2 * h)
                    pe.wait_ge(ml_W.sem, ml_W.at(4 * h + 4, L))
                    if h:
                        pe.wait_ge(ml_numc.sem, ml_numc.at(h, L))
                        pe.wait_ge(ml_Cc.sem, ml_Cc.at(h, L))
                    wo = [0, 512, 896, 1152]
                    for t in range(PT_):
                        for i in range(t + 1):
                            mm(ps[3][:, 128 * t:128 * t + 128], W[:, wo[i] + 128 * (t - i):wo[i] + 128 * (t - i) + 128],
                               proj[:, i, C_MV + DV * h:C_MV + DV * h + DV], start=i == 0, stop=i == t)
                        for i in range(t + 1):
                            ins = mm(ps[4][:, t:t + 1], W[:, wo[i] + 128 * (t - i):wo[i] + 128 * (t - i) + 128],
                                     ones[:, 0:1], start=i == 0, stop=i == t)
                    for i in range(PT_):
                        kh = kw[:, i, DK * h:DK * h + DK]
                        mm(ps[5][0:64, 0:DV], kh, proj[:, i, C_MV + DV * h:C_MV + DV * h + DV],
                           start=i == 0, stop=i == PT_ - 1)
                    for i in range(PT_):
                        ins = mm(ps[5][0:64, DV:DV + 1], kw[:, i, DK * h:DK * h + DK], ones[:, 0:1],
                                 start=i == 0, stop=i == PT_ - 1)
                    ins.then_inc(ml_num.sem, 1)
                    if h:
                        block_means(2 * h + 1)
                pe.drain().then_inc(stage_done, 1)
                pe.wait_ge(stage_done, stage_end(6, L))
                stand_alone(pe)
                for n in range(12):
                    c = C_Q + HD * n if n < 8 else (C_KS if n < 10 else C_KW) + HD * (n % 2)
                    b = n % 4
                    if n >= 4:
                        m = n - 4
                        copied = th_act if m % 2 == 0 else th_dve
                        pe.wait_ge(copied.sem, copied.at(m // 2 + 1, L))
                        stand_alone(pe)
                    for t in range(PT_):
                        ins = tr(ps[b][0:64, 128 * t:128 * t + 128], proj[:, t, c:c + HD], ident)
                    ins.then_inc(th_tr.sem, 1)
                ind8, ind64 = view("ind8", "p (t n) -> p t n", t=4), view("ind64", "p (t n) -> p t n", t=4)
                for kv in range(KV):
                    for t in range(PT_):
                        mm(ps[4][0:64, 8 * kv:8 * kv + 8], proj[:, t, C_KC + HD * kv:C_KC + HD * kv + HD], ind8[:, t, :],
                           start=t == 0, stop=t == PT_ - 1)
                for t in range(PT_):
                    ins = mm(ps[5][0:64, 0:128], ind64[:, t, :], proj[:, t, C_KC + 128:C_KC + 256],
                             start=t == 0, stop=t == PT_ - 1)
                ins.then_inc(cm_mean.sem, 1)
                pe.wait_ge(cm_meanc.sem, cm_meanc.at(1, L))
                pe.wait_ge(th_act.sem, th_act.at(6, L))
                pe.wait_ge(th_dve.sem, th_dve.at(6, L))
                for t in range(PT_):
                    for h in range(AH):
                        ins = mm(ps[6][:, 64 * t + 8 * h:64 * t + 8 * h + 8], TH[0:64, h, 128 * t:128 * t + 128],
                                 KmT[0:64, 8 * (h // AG):8 * (h // AG) + 8], start=True, stop=True)
                ins.then_inc(cm_s.sem, 1)
                pe.wait_ge(cm_p.sem, cm_p.at(1, L))
                stand_alone(pe)
                for t in range(PT_):
                    ins = tr(ps[7][0:64, 128 * t:128 * t + 128], cS[:, 64 * t:64 * t + 64], ident)
                ins.then_inc(cm_t.sem, 1)
                pe.wait_ge(cm_tc.sem, cm_tc.at(1, L))
                for t in range(PT_):
                    ins = mm(ps[t][:, :], PTb[0:64, 0, 128 * t:128 * t + 128], VmBD[0:64, :], start=True, stop=True)
                ins.then_inc(cm_o.sem, 1)
                pe.drain().then_inc(stage_done, 1)
                pe.wait_ge(stage_done, stage_end(7, L))
                stand_alone(pe)
                with pe.Fori(0, 4) as j:
                    units = [(hh, br, t) for hh in range(2) for br in range(2) for t in range(PT_)]

                    def scores(u):
                        hh, br, t = units[u]
                        mm(ps[u % 3][:, 0:128 * t + 128], qs[0:64, hh, 128 * t:128 * t + 128],
                                   TH[0:64, 8 + 2 * br + hh, 0:128 * t + 128], start=True, stop=True).then_inc(a_s.sem, 1)

                    def turn(u):
                        t = units[u][2]
                        pe.wait_ge(a_exp.sem, a_exp.at(u + 1, L, j))
                        for i in range(t + 1):
                            ins = tr(ps[3 + u % 2][:, 128 * i:128 * i + 128], Pb[:, u % 2, 128 * i:128 * i + 128], ident)
                        ins.then_inc(a_t.sem, 1)

                    def values(u):
                        hh, br, t = units[u]
                        pe.wait_ge(a_tc.sem, a_tc.at(u + 1, L, j))
                        if u >= 2:
                            pe.wait_ge(a_acc.sem, a_acc.at(u - 1, L, j))
                        c = (C_KS, C_KW)[br] + 128 + HD * hh
                        for i in range(t + 1):
                            ins = mm(ps[5 + u % 2][:, 0:HD], PTb[:, u % 2, 128 * i:128 * i + 128], proj[:, i, c:c + HD],
                                     start=i == 0, stop=i == t)
                        ins.then_inc(a_pv.sem, 1)

                    pe.wait_ge(q_stage.sem, q_stage.at(1, L, j))
                    pe.wait_ge(g_stage.sem, g_stage.at(1, L, j))
                    scores(0)
                    scores(1)
                    for u in range(U):
                        turn(u)
                        if u + 2 < U:
                            scores(u + 2)
                        if u >= 1:
                            values(u - 1)
                    values(U - 1)
                pe.drain().then_inc(stage_done, 1)
                pe.wait_ge(stage_done, stage_end(8, L))
                stand_alone(pe)
                for n in range(8):
                    c = C_Q + 128 * n if n < 4 else C_MO + 128 * (n - 4)
                    if n >= 4:
                        pe.wait_ge(mx_c.sem, mx_c.at(n - 3, L))
                    for t in range(PT_):
                        ins = tr(ps[n % 4][:, 128 * t:128 * t + 128], proj[:, t, c:c + 128], ident)
                    ins.then_inc(mx_t.sem, 1)
                pe.wait_ge(d_pair.sem, d_pair.at(1, L))
                stand_alone(pe)
                for g in range(AG):
                    tr(ps[4][:, TS * g:TS * g + TS],
                       Ssb[0:TS, 128 * g:128 * g + 128], idn(TS))
                for b_, c in enumerate((C_KS, C_KW)):
                    tr(ps[4][:, 128 + TS * b_:128 + TS * b_ + TS], proj_s[:, c:c + 128], idn(TS))
                for g in range(2):
                    ins = mm(ps[5][:, 24 * g:24 * g + 24], view("tokrow", "p (g n) -> p g n", g=2)[0:TS, g, :], gates_s[:, :],
                             start=True, stop=True)
                ins.then_inc(d_tr.sem, 1)
                pe.drain().then_inc(stage_done, 1)
                pe.wait_ge(stage_done, stage_end(9, L))
                stand_alone(pe)
                for j in range(2):
                    pe.wait_ge(d_q.sem, d_q.at(1, L, j))
                    for b in range(4):
                        ins = mm(ps[4][32 * b:32 * b + 32, 0:16], Qbd[:, b, :], KmTd[:, 4 * j + b, :], start=True, stop=True,
                                 tile_position=(0, 32 * b), skip_group_check=True)
                    ins.then_inc(d_cs.sem, 1)
                    nkt = 0
                    for br in range(2):
                        for b in range(4):
                            kv_ = (spg, wpg)[br][4 * j + b]
                            if br == 0 and b % 2 == 0:
                                pe.wait_ge(spg_in[2 * j + b // 2], L * (32 * NPG) + 32 * NPG)
                            if br == 1 and b == 0:
                                pe.wait_ge(wpg_in[j], L * 64 + 64)
                            for half in range(2 - br):
                                if nkt >= 2:
                                    pe.wait_ge(d_ktc.sem, d_ktc.at(nkt - 1, L, j))
                                for i in range(4):
                                    src = kv_[:, 4 * half + i, 0:128]
                                    ins = tr(ps[nkt % 2][:, 128 * i:128 * i + 128], src, ident)
                                    if br == 1 and b == 0 and i < 2 - j:
                                        ins.then_inc(slab_out[0 if j else 1 + i], 1)
                                ins.then_inc(d_kt.sem, 1)
                                nkt += 1
                            for half in range(2 - br):
                                pe.wait_ge(d_ktc.sem, d_ktc.at(nkt - (1 - br) + half, L, j))
                                if br == 1 and b == 0:
                                    pe.wait_ge(d_max.sem, d_max.at(1, L, j))
                                mm(ps[5 + half][32 * b:32 * b + 32, :], Qbd[:, b, :], KT[:, b % 2, 512 * half:512 * half + 512],
                                   start=True, stop=True, tile_position=(0, 32 * b), skip_group_check=True)
                            ins = mm(ps[7][32 * b:32 * b + 32, 0:TS], Qbd[:, b, :], KN[:, br, :], start=True, stop=True,
                                     tile_position=(0, 32 * b), skip_group_check=True)
                        ins.then_inc(d_s.sem, 1)
                        if br == 0:
                            pe.wait_ge(d_cp.sem, d_cp.at(1, L, j))
                            mm(ps[2][:, 0:16], K["samegroup"], imp[:, 0:16], start=True, stop=True).then_inc(d_imp.sem, 1)
                            tr(ps[3][0:64, 0:128], P4, ident).then_inc(d_ct.sem, 1)
                            pe.wait_ge(d_ctc.sem, d_ctc.at(1, L, j))
                            stand_alone(pe)
                            ins = mm(ps[4][:, 128:256], PTc[0:64, :], Vmd[:, j, :], start=True, stop=True)
                            ins.then_inc(d_co.sem, 1)
                        pe.wait_ge(d_exp.sem, d_exp.at(br + 1, L, j))
                        nt = (8, 4)[br]
                        for i in range(nt):
                            tr(ps[i // 4][:, 128 * (i % 4):128 * (i % 4) + 128], Ssb[:, 128 * i:128 * i + 128], ident)
                        tr(ps[3][0:TS, 128:256], Ssb[:, 128 * nt:128 * nt + TS], ident).then_inc(d_pt.sem, 1)
                        pe.wait_ge(d_ptc.sem, d_ptc.at(br + 1, L, j))
                        cn = (C_KS, C_KW)[br] + 128
                        for i in range(nt + 1):
                            for b in range(4):
                                o_ = ps[4][32 * b:32 * b + 32, 256:384] if br == 0 else ps[2][32 * b:32 * b + 32, 128:256]
                                if i < nt:
                                    lt, rh = PTs[:, i, 32 * b:32 * b + 32], (spg, wpg)[br][4 * j + b][:, i, 128:256]
                                else:
                                    lt, rh = PTs[0:TS, 8, 32 * b:32 * b + 32], proj_s[:, cn:cn + 128]
                                ins = mm(o_, lt, rh, start=i == 0, stop=i == nt, tile_position=(0, 32 * b),
                                         skip_group_check=True)
                        ins.then_inc(d_pv.sem, 1)
                    pe.wait_ge(d_cmb.sem, d_cmb.at(1, L, j))
                    for h in range(AH):
                        kv = h // AG
                        q = 64 * (h % 2)
                        ins = mm(ps[3][q:q + 64, 256 + TS * (h // 2):256 + TS * (h // 2) + TS], cmb[:, 64 * kv:64 * kv + 64],
                                 rownow[:, h, :], start=True, stop=True, tile_position=(0, q), skip_group_check=True)
                    ins.then_inc(d_out.sem, 1)
                    pe.wait_ge(d_add.sem, d_add.at(1, L, j))
                    stand_alone(pe)
                pe.drain().then_inc(stage_done, 1)
                pe.wait_ge(stage_done, stage_end(10, L))
                stand_alone(pe)
                oh = view("onehot", "p (h n) -> p h n", h=MH)
                pe.wait_ge(st_in, L * (16 * 2) + 32)
                pe.wait_ge(ms_kq.sem, ms_kq.at(1, L))
                stand_alone(pe)
                mm(ps[6][0:64, 0:NB * MH], ones[0:TS, 0:64], awl[0:TS, :, :].rearrange("p b h -> p (b h)"),
                              start=True, stop=True).then_inc(ms_dec.sem, 1)
                for h in range(MH):
                    if h:
                        pe.wait_ge(ms_numc.sem, ms_numc.at(h, L))
                        pe.wait_ge(ms_W.sem, ms_W.at(h, L))
                        stand_alone(pe)
                    mm(ps[1][0:TS, 0:TS], mqks[:, 4 + h, :], mqks[:, h, :], start=True, stop=True)
                    mm(ps[0][0:TS, 0:TS], oh[0:MH, h, 0:TS], negG_s[:, :], start=True, stop=True).then_inc(ms_g.sem, 1)
                    pe.wait_ge(ms_Wd.sem, ms_Wd.at(h + 1, L))
                    stand_alone(pe)
                    v = proj_s[:, C_MV + DV * h:C_MV + DV * h + DV]
                    mm(ps[2][0:TS, 0:DV], Ws[0:TS, :], v, start=True, stop=True)
                    mm(ps[2][0:TS, DV:DV + 1], Ws[0:TS, :], ones[0:TS, 0:1], start=True, stop=True)
                    pe.wait_ge(ms_q.sem, ms_q.at(h + 1, L))
                    stand_alone(pe)
                    for b in range(NB):
                        mm(ps[3][0:TS, 0:DV], Qm[0:64, b, :], Cst[0:64, b * MH + h, :], start=b == 0, stop=b == NB - 1)
                    for b in range(NB):
                        ins = mm(ps[3][0:TS, DV:DV + 1], Qm[0:64, b, :], nst[0:64, b * MH + h:b * MH + h + 1],
                                 start=b == 0, stop=b == NB - 1)
                    ins.then_inc(ms_num.sem, 1)
                    for half in range(2):
                        if h or half:
                            pe.wait_ge(ms_Cc.sem, ms_Cc.at(2 * h + half, L))
                            stand_alone(pe)
                        for bb in range(4):
                            b = 4 * half + bb
                            mm(ps[4][0:64, DV * bb:DV * bb + DV], kwb[0:TS, b, :], v, start=True, stop=True)
                            ins = mm(ps[5][0:64, bb:bb + 1], kwb[0:TS, b, :], ones[0:TS, 0:1], start=True, stop=True)
                        ins.then_inc(ms_C.sem, 1)
                pe.drain().then_inc(stage_done, 1)
                pe.wait_ge(stage_done, stage_end(11, L))
                stand_alone(pe)
                for c in range(4):
                    ins = tr(ps[0][:, TS * c:TS * c + TS], hs[0:TS, 128 * c:128 * c + 128], idn(TS))
                ins.then_inc(ms_t.sem, 1)
                pe.drain().then_inc(stage_done, 1)
                pe.wait_ge(stage_done, stage_end(12, L))
                stand_alone(pe)
                for c in range(8):
                    i = c // 4
                    if c % 4 == 0:
                        pe.wait_ge(slab_in[i % NSLAB], slab_loads("out", i, L))
                    if c >= 4:
                        pe.wait_ge(o_add.sem, o_add.at(c - 3, L))
                    wv = slab[i][:, :].rearrange("p (k n) -> p k n", k=8)
                    for k in range(KC):
                        for b in range(2):
                            ins = mm(ps[2 * (c % 4) + b][:, 0:HALF], wv[:, k, 128 * (c % 4):128 * (c % 4) + 128],
                                     xnT[:, k, HALF * b:HALF * b + HALF], start=k == 0, stop=k == KC - 1)
                            if c == 4 and k == 0 and b == 0:
                                ins.then_inc(slab_out[0], 1)
                    ins.then_inc(o_acc.sem, 1)
                pe.drain().then_inc(stage_done, 1)
                pe.wait_ge(stage_done, stage_end(13, L))
                stand_alone(pe)
                norm_sums(NRM["n2"], L, frees=1)
                pe.wait_ge(cv_in, L * 16 + 16)
                stand_alone(pe)
                for c in range(FC):
                    ins = tr(ps[2][:, 16 * c:16 * c + 16], csrow[0:16, 128 * c:128 * c + 128], idn(16))
                ins.then_inc(cv_t.sem, 1)
                pe.drain().then_inc(stage_done, 1)
                pe.wait_ge(stage_done, stage_end(14, L))
                stand_alone(pe)
                def up_slab(i, j=0):
                    pe.wait_ge(slab_in[i % NSLAB], slab_loads("up", i, L, j))
                    wv = slab[i % NSLAB][:, :].rearrange("p (k h n) -> p k h n", k=8, h=2)
                    for cc in range(2):
                        c = 2 * i + cc
                        pe.wait_ge(u_h.sem, u_h.at(c - 1 + j * 6, L))
                        for h in range(2):
                            for k in range(KC):
                                for b in range(2):
                                    ins = mm(ps[4 * (c % 2) + 2 * h + b][:, 0:HALF], wv[:, k, h, 128 * cc:128 * cc + 128],
                                             xnT[:, k, HALF * b:HALF * b + HALF], start=k == 0, stop=k == KC - 1)
                                    if i not in (0, 9) and cc == 0 and h == 0 and k == 0 and b == 0:
                                        ins.then_inc(slab_out[(i - 1) % NSLAB], 1)
                        ins.then_inc(u_acc.sem, 1)

                with pe.Fori(0, 3) as j:
                    for i in range(3):
                        up_slab(i, j)
                    pe.drain().then_inc(slab_out[2], 1)
                for i in (9, 10):
                    up_slab(i)
                pe.wait_ge(u_h.sem, u_h.at(FC, L))
                stand_alone(pe)
                pe.drain().then_inc(slab_out[10 % NSLAB], 1)

                def down_slab(c, j=0):
                    pe.wait_ge(slab_in[c % NSLAB], slab_loads("down", c, L, j))
                    pe.wait_ge(y_add.sem, y_add.at(c - 2 + j * 3, L))
                    wv = slab[c % NSLAB][:, 0:FC * 128].rearrange("p (k n) -> p k n", k=FC)
                    for k in range(FC):
                        for b in range(2):
                            ins = mm(ps[2 * (c % 3) + b][:, 0:HALF], wv[:, k, :], hT[:, k, HALF * b:HALF * b + HALF],
                                     start=k == 0, stop=k == FC - 1)
                            if c not in (0, 6) and k == 0 and b == 0:
                                ins.then_inc(slab_out[(c - 1) % NSLAB], 1)
                    ins.then_inc(y_acc.sem, 1)

                with pe.Fori(0, 2) as j:
                    for c in range(3):
                        down_slab(c, j)
                    pe.drain().then_inc(slab_out[2], 1)
                for c in (6, 7):
                    down_slab(c)
                pe.drain().then_inc(slab_out[7 % NSLAB], 1)
                for c in range(FC):
                    if c >= 2:
                        pe.wait_ge(ul_c.sem, ul_c.at(c - 1, L))
                    tr(ps[6 + c % 2][0:18, 0:128], uLast[:, c, :], ident).then_inc(ul_t.sem, 1)
                pe.drain().then_inc(stage_done, 1)
                pe.wait_ge(stage_done, stage_end(15, L))
                stand_alone(pe)

            norm_sums(dict(sq=final_sq, used=final_used))
            pe.wait_ge(final_xn.sem, final_xn.at(KC))
            for n in range(10):
                t, hf = n // 2, n % 2
                M = 128 if t < 4 else TS
                if n >= 4:
                    pe.wait_ge(final_copy.sem, final_copy.at(n - 3))
                for k in range(4):
                    ins = tr(ps[4 + n % 4][0:M, 128 * k:128 * k + 128], xnT[:, 4 * hf + k, 128 * t:128 * t + M], ident)
                ins.then_inc(final_tr.sem, 1)

        def bc(ap, axis, n):
            a = ap.unsqueeze(axis)
            shape = list(a.shape)
            shape[axis] = n
            return a.to_broadcast(shape)

        modA = modT[:, :, :]
        convw = colsB[:, 0:66]

        @block.scalar
        def _(act):
            A_ = nc.scalar.activation
            drain = act.drain
            act.wait_ge(load_in, PRO_LOADS)
            A_(crow[0:9, :], crow[0:9, :], ACT.Silu).then_inc(pro_silu, 1)
            for k in range(KC):
                act.wait_ge(pro_xt, k + 1)
                A_(xT[:, k, 0:SEQ], ps[2 * (k % 3)][:, :], ACT.Copy).then_inc(pro_copy_p, 1)

            def norm_act(S, L=0):
                for k in range(KC):
                    if k >= 2:
                        act.wait_ge(S["used"].sem, S["used"].at(k - 1, L))
                    A_(sq[:, k % 2, :], xT[:, k, :], ACT.Square).then_inc(S["sq"].sem, 1)
                act.wait_ge(S["var"].sem, S["var"].at(1, L))
                A_(rstd[:, :], rstd[:, :], ACT.Sqrt).then_inc(S["root"].sem, 1)

            def modulate(S, shift, L):
                for k in range(KC):
                    act.wait_ge(S["xr"].sem, S["xr"].at(k + 1, L))
                    A_(xnT[:, k, 0:SEQ], xnT[:, k, 0:SEQ], ACT.Identity, bias=modT[:, shift + k, 0:1],
                       scale=scale_n[:, k, 0:1])

            with act.Fori(0, DEPTH) as L:
                act.drain().then_inc(stage_done, 1)
                act.wait_ge(stage_done, stage_end(1, L))
                stand_alone(act)
                with act.Fori(0, 4) as j:
                    for i in range(3):
                        act.wait_ge(mod_acc.sem, mod_acc.at(i + 1, L, j))
                        A_(modp[:, i, :], ps[i][:, :], ACT.Copy).then_inc(mod_copy.sem, 1)
                act.drain().then_inc(stage_done, 1)
                act.wait_ge(stage_done, stage_end(2, L))
                stand_alone(act)
                norm_act(NRM["n1"], L)
                modulate(NRM["n1"], 0, L)
                act.drain().then_inc(stage_done, 1)
                act.wait_ge(stage_done, stage_end(3, L))
                stand_alone(act)
                for at, n in enumerate(IN_ORDER):
                    i, t = divmod(n, 5)
                    c0, cw = IN_SLABS[i]
                    if n % 2 == 0:
                        M = 128 if t < 4 else TS
                        dst = proj[:, t, c0:c0 + cw] if t < 4 else proj_s[:, c0:c0 + cw]
                        act.wait_ge(in_acc.sem, in_acc.at(at + 1, L))
                        A_(dst, ps[n % 8][0:M, 0:cw], ACT.Copy).then_inc(in_act.sem, 1)
                    if t == 3:
                        act.wait_ge(dp_acc.sem, dp_acc.at(i + 1, L))
                        if i >= 2:
                            act.wait_ge(in_acc.sem, in_acc.at(IN_ORDER.index(5 * i - 6) + 1, L))
                        A_(dpart[:, i % 2, 0:cw], ps[(n + 1) % 8][:, 0:cw], ACT.Copy).then_inc(dp_copy.sem, 1)
                act.drain().then_inc(stage_done, 1)
                act.wait_ge(stage_done, stage_end(4, L))
                stand_alone(act)
                A_(proj[:, :, C_MK:C_MK + 256], proj[:, :, C_MK:C_MK + 256], ACT.Copy, scale=DK ** -0.5)
                A_(proj_s[:, C_MK:C_MK + 256], proj_s[:, C_MK:C_MK + 256], ACT.Copy, scale=DK ** -0.5).then_inc(k_scaled.sem, 1)
                for n in range(3):
                    act.wait_ge(mt_tr.sem, mt_tr.at(n + 1, L))
                    A_(mqk[0:64, n, :], ps[4 + n % 2][0:64, :], ACT.Copy).then_inc(mt_cp.sem, 1)
                A_(gates[:, :, :], proj[:, :, C_G:C_G + 24], ACT.Sigmoid)
                A_(gates_s[:, :], proj_s[:, C_G:C_G + 24], ACT.Sigmoid)
                A_(proj[:, :, C_MO:C_MO + 512], proj[:, :, C_MO:C_MO + 512], ACT.Sigmoid)
                A_(proj_s[:, C_MO:C_MO + 512], proj_s[:, C_MO:C_MO + 512], ACT.Sigmoid)
                for n in range(3, 9):
                    act.wait_ge(mt_tr.sem, mt_tr.at(n + 1, L))
                    if n < 8:
                        A_(mqk[0:64, n, :], ps[4 + n % 2][0:64, :], ACT.Copy).then_inc(mt_cp.sem, 1)
                    else:
                        A_(mqks[:, :, :].rearrange("p n t -> p (n t)"), ps[4][0:64, 0:256], ACT.Copy).then_inc(mt_cp.sem, 1)
                act.wait_ge(ml_abs.sem, ml_abs.at(1, L))
                A_(rr[:, 5, :], rr[:, 4, :], ACT.Exp, scale=-1.0)
                drain()
                A_(rr[:, 5, :], rr[:, 5, :], ACT.Ln, bias=1.0).then_inc(ml_ln.sem, 1)
                act.wait_ge(ml_rows.sem, ml_rows.at(1, L))
                A_(rr[:, 1, :], rr[:, 1, :], ACT.Exp)
                A_(rr[:, 2, :], rr[:, 2, :], ACT.Exp, scale=-1.0)
                A_(rr[:, 3, :], rr[:, 3, :], ACT.Exp).then_inc(ml_exp.sem, 1)
                act.drain().then_inc(stage_done, 1)
                act.wait_ge(stage_done, stage_end(5, L))
                stand_alone(act)
                wo = [0, 512, 896, 1152]
                for h in range(MH):
                    act.wait_ge(ml_diag.sem, ml_diag.at(h + 1, L))
                    for i in range(PT_):
                        g = RT[:, i, 0, h:h + 1]
                        ins = A_(E[:, wo[i]:wo[i] + 128], E[:, wo[i]:wo[i] + 128], ACT.Exp, bias=g)
                        if i < 3:
                            n = 128 * (3 - i)
                            ins = A_(E[:, wo[i] + 128:wo[i] + 128 + n], ps[0][:, 128 * (i + 1):SEQ], ACT.Exp, bias=g)
                        ins.then_inc(ml_E.sem, 1)
                    act.wait_ge(ml_num.sem, ml_num.at(h + 1, L))
                    A_(Cp[0:64, h, :], ps[5][0:64, 0:DV + 1], ACT.Copy).then_inc(ml_Cc.sem, 1)
                act.wait_ge(d_cm.sem, d_cm.at(NB, L))
                A_(KmTd[:, :, :].rearrange("p b n -> p (b n)"), ps[6][:, 0:128], ACT.Copy)
                A_(Vmd[:, :, :].rearrange("p g d -> p (g d)"), ps[7][0:64, 256:512], ACT.Copy)
                act.wait_ge(h_var.sem, h_var.at(1, L))
                A_(hvar, hvar, ACT.Sqrt).then_inc(h_root.sem, 1)
                act.drain().then_inc(stage_done, 1)
                act.wait_ge(stage_done, stage_end(6, L))
                stand_alone(act)
                for n in range(0, 12, 2):
                    act.wait_ge(th_tr.sem, th_tr.at(n + 1, L))
                    A_(TH[0:64, n, :], ps[n % 4][0:64, :], ACT.Copy, scale=HD ** -0.5 if n < 8 else 1.0).then_inc(th_act.sem, 1)
                act.wait_ge(cm_sub.sem, cm_sub.at(1, L))
                A_(cS, cS, ACT.Exp).then_inc(cm_exp.sem, 1)
                act.wait_ge(cm_o.sem, cm_o.at(1, L))
                for t in range(PT_):
                    A_(proj[:, t, 0:512], ps[t][:, :], ACT.Copy)
                act.drain().then_inc(stage_done, 1)
                act.wait_ge(stage_done, stage_end(7, L))
                stand_alone(act)
                with act.Fori(0, 4) as j:
                    def exp(u):
                        nk = 128 * (u % 4) + 128
                        act.wait_ge(a_max.sem, a_max.at(u + 1, L, j))
                        if u >= 2:
                            act.wait_ge(a_t.sem, a_t.at(u - 1, L, j))
                        A_(Pb[:, u % 2, 0:nk], ps[u % 3][:, 0:nk], ACT.Exp, bias=nmax[:, u:u + 1],
                                     accum_out=den[:, u:u + 1]).then_inc(a_exp.sem, 1)

                    def copy(u):
                        nk = 128 * (u % 4) + 128
                        act.wait_ge(a_t.sem, a_t.at(u + 1, L, j))
                        if u >= 2:
                            act.wait_ge(a_pv.sem, a_pv.at(u - 1, L, j))
                        A_(PTb[:, u % 2, 0:nk], ps[3 + u % 2][:, 0:nk], ACT.Copy).then_inc(a_tc.sem, 1)

                    A_(qs[0:64, 0, :], TH[0:64, bass.ds(j, 1), :].squeeze(1), ACT.Copy)
                    A_(qs[0:64, 1, :], TH[0:64, bass.ds(j + 4, 1), :].squeeze(1), ACT.Copy).then_inc(q_stage.sem, 1)
                    exp(0)
                    for u in range(U):
                        if u + 1 < U:
                            exp(u + 1)
                        copy(u)
                act.drain().then_inc(stage_done, 1)
                act.wait_ge(stage_done, stage_end(8, L))
                stand_alone(act)
                for n in range(8):
                    act.wait_ge(mx_t.sem, mx_t.at(n + 1, L))
                    A_(xnT[:, n, 0:SEQ], ps[n % 4][:, :], ACT.Copy).then_inc(mx_c.sem, 1)
                act.drain().then_inc(stage_done, 1)
                act.wait_ge(stage_done, stage_end(9, L))
                stand_alone(act)
                for j in range(2):
                    act.wait_ge(d_csub.sem, d_csub.at(1, L, j))
                    A_(imp[:, 0:16], ps[4][:, 0:16], ACT.Exp, bias=small[:, 0:1], accum_out=small[:, 1:2]).then_inc(d_cexp.sem, 1)
                    for n in range(8):
                        act.wait_ge(d_kt.sem, d_kt.at(n + 1, L, j))
                        A_(KT[:, n // 2 % 2, 512 * (n % 2):512 * (n % 2) + 512], ps[n % 2][:, :], ACT.Copy).then_inc(d_ktc.sem, 1)
                    act.wait_ge(d_ct.sem, d_ct.at(1, L, j))
                    A_(PTc[0:64, :], ps[3][0:64, 0:128], ACT.Copy).then_inc(d_ctc.sem, 1)
                    for br in range(2):
                        nt = (8, 4)[br]
                        if br == 1:
                            for n in range(8, 12):
                                act.wait_ge(d_kt.sem, d_kt.at(n + 1, L, j))
                                A_(KT[:, n % 2, 0:512], ps[n % 2][:, :], ACT.Copy).then_inc(d_ktc.sem, 1)
                        act.wait_ge(d_max.sem, d_max.at(br + 1, L, j))
                        wd = 128 * nt + TS
                        A_(Ssb[:, 0:wd], Ssb[:, 0:wd], ACT.Exp, bias=small[:, 2 + br:3 + br],
                                     accum_out=small[:, 4 + br:5 + br]).then_inc(d_exp.sem, 1)
                        act.wait_ge(d_pt.sem, d_pt.at(br + 1, L, j))
                        for q in range(nt // 4):
                            A_(PTs[:, 4 * q:4 * q + 4, :].rearrange("p a b -> p (a b)"), ps[q][:, :], ACT.Copy)
                        A_(PTs[0:TS, 8, :], ps[3][0:TS, 128:256], ACT.Copy).then_inc(d_ptc.sem, 1)
                act.drain().then_inc(stage_done, 1)
                act.wait_ge(stage_done, stage_end(10, L))
                stand_alone(act)
                for h in range(MH):
                    act.wait_ge(ms_E.sem, ms_E.at(h + 1, L))
                    A_(Es[0:TS, :], Es[0:TS, :], ACT.Exp, bias=RT[0:TS, 4, 0, h:h + 1]).then_inc(ms_W.sem, 1)
                act.wait_ge(hs_var.sem, hs_var.at(1, L))
                A_(h_small[0:TS, 8:12], h_small[0:TS, 8:12], ACT.Sqrt).then_inc(hs_root.sem, 1)
                act.drain().then_inc(stage_done, 1)
                act.wait_ge(stage_done, stage_end(11, L))
                stand_alone(act)
                act.drain().then_inc(stage_done, 1)
                act.wait_ge(stage_done, stage_end(12, L))
                stand_alone(act)
                act.drain().then_inc(stage_done, 1)
                act.wait_ge(stage_done, stage_end(13, L))
                stand_alone(act)
                norm_act(NRM["n2"], L)
                modulate(NRM["n2"], 24, L)
                act.drain().then_inc(stage_done, 1)
                act.wait_ge(stage_done, stage_end(14, L))
                stand_alone(act)

                def u_chunk(c, cd, j=0):
                    s = c % 2
                    act.wait_ge(u_acc.sem, u_acc.at(c + 1 + j * 6, L))
                    act.wait_ge(u_cv.sem, u_cv.at(c - 1 + j * 6, L))
                    A_(up[:, s, 2:2 + HALF], ps[4 * s][:, 0:HALF], ACT.Copy)
                    A_(up[:, s, 2 + HALF:2 + SEQ], ps[4 * s + 1][:, 0:SEQ - HALF], ACT.Copy)
                    A_(up[:, s, 2 + SEQ:UPW].rearrange("p (b t) -> p b t", b=NB)[:, :, 2:],
                                ps[4 * s + 1][:, SEQ - HALF:HALF].rearrange("p (b t) -> p b t", b=NB), ACT.Copy).then_inc(u_cp.sem, 1)
                    act.wait_ge(u_cv.sem, u_cv.at(c + 1 + j * 6, L))
                    A_(cv[:, s, 0:UPW - 2], cv[:, s, 0:UPW - 2], ACT.Silu, bias=cbias[:, s:s + 1]).then_inc(u_si.sem, 1)

                with act.Fori(0, 3) as j:
                    for c in range(6):
                        u_chunk(c, j * 6 + c, j)
                for c in range(18, FC):
                    u_chunk(c, c)
                for c in range(FC):
                    act.wait_ge(ul_t.sem, ul_t.at(c + 1, L))
                    A_(ulrow[0:18, 128 * c:128 * c + 128], ps[6 + c % 2][0:18, 0:128], ACT.Copy).then_inc(ul_c.sem, 1)
                act.drain().then_inc(stage_done, 1)
                act.wait_ge(stage_done, stage_end(15, L))
                stand_alone(act)

            norm_act(dict(sq=final_sq, used=final_used, var=final_var, root=final_sqrt))
            for n in range(10):
                M = 128 if n < 8 else TS
                act.wait_ge(final_tr.sem, final_tr.at(n + 1))
                A_(ybuf[0:M, n, :], ps[4 + n % 4][0:M, :], ACT.Copy).then_inc(final_copy.sem, 1)

        @block.vector
        def _(dve):
            V = nc.vector
            tt, ts_, stt, cp, red = V.tensor_tensor, V.tensor_scalar, V.scalar_tensor_tensor, V.tensor_copy, V.tensor_reduce
            drain = dve.drain
            for s in (u_cv, u_h, y_add):
                dve.sem_inc(s.sem, s.credit)
            V.memset(cT[:, :, :], 0.0)
            drain()
            dve.wait_ge(pro_ct, 1)
            cp(cT[:, :, 0:9], ps[7][:, 0:72].rearrange("p (k r) -> p k r", k=KC))
            for k in range(KC):
                dve.wait_ge(pro_xt, k + 1)
                cp(xT[:, k, SEQ:TT], ps[2 * (k % 3) + 1][:, 0:TS]).then_inc(pro_copy_s, 1)

            def norm_rstd(S, L=0):
                dve.wait_ge(S["used"].sem, S["used"].at(KC, L))
                ts_(rstd[:, 0:HALF], ps[0][:, 0:HALF], 1.0 / D, EPS, ALU.mult, ALU.add)
                ts_(rstd[:, HALF:TT], ps[1][:, 0:HALF], 1.0 / D, EPS, ALU.mult, ALU.add).then_inc(S["var"].sem, 1)
                dve.wait_ge(S["root"].sem, S["root"].at(1, L))
                V.reciprocal(rstd[:, :], rstd[:, :])
                drain()

            def norm_dve(S, norm, scale, shift, L):
                stt(scale_n[:, :, :], modT[:, scale:scale + KC, :], 1.0, bc(colsA[:, norm:norm + KC], 2, 9), ALU.add, ALU.mult)
                norm_rstd(S, L)
                for k in range(KC):
                    tt(xnT[:, k, :], xT[:, k, :], rstd[:, :], ALU.mult).then_inc(S["xr"].sem, 1)
                drain()
                d = xnT[:, :, SEQ:TT].rearrange("p k (b t) -> p k b t", b=NB)
                tt(d, d, bc(scale_n[:, :, 1:9], 3, NT), ALU.mult)
                drain()
                tt(d, d, bc(modT[:, shift:shift + KC, 1:9], 3, NT), ALU.add)

            with dve.Fori(0, DEPTH) as L:
                dve.drain().then_inc(stage_done, 1)
                dve.wait_ge(stage_done, stage_end(1, L))
                stand_alone(dve)
                dve.wait_ge(rows_tr.sem, rows_tr.at(1, L))
                cp(colsA[:, :], ps[6][:, 0:64])
                cp(colsB[:, :], ps[6][:, 64:160])
                dve.drain().then_inc(stage_done, 1)
                dve.wait_ge(stage_done, stage_end(2, L))
                stand_alone(dve)
                tt(modT[:, :, :], ps[7][:, 0:432].rearrange("p (c r) -> p c r", c=48), bc(colsA[:, 16:64], 2, 9), ALU.add)
                drain()
                norm_dve(NRM["n1"], 0, 8, 0, L)
                dve.drain().then_inc(stage_done, 1)
                dve.wait_ge(stage_done, stage_end(3, L))
                stand_alone(dve)
                for at, n in enumerate(IN_ORDER):
                    i, t = divmod(n, 5)
                    c0, cw = IN_SLABS[i]
                    if n % 2 == 1:
                        M = 128 if t < 4 else TS
                        dst = proj[:, t, c0:c0 + cw] if t < 4 else proj_s[:, c0:c0 + cw]
                        dve.wait_ge(in_acc.sem, in_acc.at(at + 1, L))
                        cp(dst, ps[n % 8][0:M, 0:cw]).then_inc(in_dve.sem, 1)
                dve.drain().then_inc(stage_done, 1)
                dve.wait_ge(stage_done, stage_end(4, L))
                stand_alone(dve)
                bif = rows_bc[:, 512:520]
                tt(proj[:, :, C_IF:C_IF + 8], proj[:, :, C_IF:C_IF + 8], bc(bif, 1, PT_), ALU.add)
                tt(proj_s[:, C_IF:C_IF + 8], proj_s[:, C_IF:C_IF + 8], rows_bc[0:TS, 512:520], ALU.add).then_inc(if_ready.sem, 1)
                dve.wait_ge(if_tr.sem, if_tr.at(1, L))
                cp(rr[:, 0, 0:SEQ], ps[0][0:MH, :])
                cp(row8[:, 0:SEQ], ps[1][0:MH, :])
                cp(rr[:, 0, SEQ:TT], ps[2][0:MH, 0:TS])
                cp(row8[:, SEQ:TT], ps[2][0:MH, TS:2 * TS])
                V.memset(rr[:, 6, 0:SEQ], 0.0)
                cp(rr[:, 6, SEQ:TT].rearrange("p (b t) -> p b t", b=NB), bc(m0s[:, :], 2, NT))
                drain()
                stt(rr[:, 4, :], row8[:, :], -1.0, row8[:, :], ALU.mult, ALU.max).then_inc(ml_abs.sem, 1)

                dve.wait_ge(ml_ln.sem, ml_ln.at(1, L))
                stt(rr[:, 4, :], row8[:, :], 0.0, rr[:, 5, :], ALU.min, ALU.subtract)
                drain()
                V.tensor_tensor_scan(rr[:, 5, :], seqc[:, 0, :], rr[:, 4, :], 0.0, ALU.mult, ALU.add)
                drain()
                tt(rr[:, 0, :], rr[:, 0, :], rr[:, 5, :], ALU.subtract)
                drain()
                tt(rr[:, 4, :], rr[:, 0, :], rr[:, 6, :], ALU.max)
                drain()
                V.tensor_tensor_scan(row8[:, :], seqc[:, 1, :], rr[:, 4, :], 0.0, ALU.add, ALU.max)
                drain()
                tt(rr[:, 2, :], rr[:, 5, :], row8[:, :], ALU.add)
                tt(rr[:, 4, :], rr[:, 5, :], row8[:, :], ALU.add)
                ts_(rr[:, 7, :], row8[:, :], -1.0, None, ALU.mult)
                ts_(negG_s[:, :], row8[:, SEQ:TT], -1.0, None, ALU.mult)
                ts_(rr[:, 1, 0:SEQ], rr[:, 0, 0:SEQ], row8[:, SEQ - 1:SEQ], None, ALU.subtract)
                gb = row8[:, SEQ:TT].rearrange("p (b t) -> p b t", b=NB)[:, :, NT - 1]
                tt(rr[:, 1, SEQ:TT].rearrange("p (b t) -> p b t", b=NB), rr[:, 0, SEQ:TT].rearrange("p (b t) -> p b t", b=NB),
                   bc(gb, 2, NT), ALU.subtract)
                tt(rr[:, 3, :], rr[:, 6, :], row8[:, :], ALU.subtract)
                dve.drain().then_inc(ml_rows.sem, 1)
                dve.wait_ge(ml_colt.sem, ml_colt.at(1, L))
                cp(RT[:, 0:4, :, :].rearrange("p t q h -> p (t q h)"), ps[3][:, 0:64])
                cp(RT[0:TS, 4, :, :].rearrange("p q h -> p (q h)"), ps[3][0:TS, 64:80])
                dve.drain().then_inc(stage_done, 1)
                dve.wait_ge(stage_done, stage_end(5, L))
                stand_alone(dve)
                tt(kw[:, :, :].rearrange("p t (h d) -> p t h d", h=MH),
                             proj[:, :, C_MK:C_MK + 256].rearrange("p t (h d) -> p t h d", h=MH),
                             bc(RT[:, 0:4, 1, :], 3, DK), ALU.mult).then_inc(ml_kw.sem, 1)

                def rope(x, P, nh, c, s_, nt):
                    x1, x2 = x[:, :, :, 0:32], x[:, :, :, 32:64]
                    n = nt * nh * 32
                    t = [rope_t[0:P, r, 0:n].rearrange("p (t h d) -> p t h d", t=nt, h=nh) for r in range(4)]
                    cb, sb_ = bc(c, 2, nh), bc(s_, 2, nh)
                    tt(t[0], x1, cb, ALU.mult)
                    tt(t[1], x2, sb_, ALU.mult)
                    tt(t[2], x1, sb_, ALU.mult)
                    tt(t[3], x2, cb, ALU.mult)
                    drain()
                    tt(x1, t[0], t[1], ALU.subtract)
                    tt(x2, t[2], t[3], ALU.add)
                    drain()

                def rope_prompt(c, nh, t0, t1):
                    rope(proj[:, t0:t1, c:c + 64 * nh].rearrange("p t (h d) -> p t h d", h=nh), 128, nh, cos[:, t0:t1, :],
                         sin[:, t0:t1, :], t1 - t0)

                def rope_decode(c, nh):
                    rope(proj_s[:, c:c + 64 * nh].rearrange("p (t h d) -> p t h d", t=1, h=nh), TS, nh, cos[0:TS, 4:5, :],
                         sin[0:TS, 4:5, :], 1)

                def rotations(h):
                    if h == 0:
                        rope_prompt(C_KC, 2, 0, PT_)
                        rope_prompt(C_KS, 2, 0, PT_)
                        rope_decode(C_KC, 2)
                        rope_decode(C_KS, 2)
                    if h == 1:
                        rope_prompt(C_KW, 2, 0, PT_)
                        rope_decode(C_KW, 2)
                        dve.drain().then_inc(roped.sem, 1)
                        rope_prompt(C_Q, 8, 0, 1)
                    if h == 2:
                        rope_prompt(C_Q, 8, 1, 2)
                        rope_prompt(C_Q, 8, 2, 3)
                    if h == 3:
                        rope_prompt(C_Q, 8, 3, 4)
                        rope_decode(C_Q, 8)

                wo = [0, 512, 896, 1152]
                for h in range(MH):
                    dve.wait_ge(ml_g.sem, ml_g.at(h + 1, L))
                    for i in range(PT_):
                        ins = tt(E[:, wo[i]:wo[i] + 128], ps[0][:, 128 * i:128 * i + 128], K["causalT"], ALU.add)
                    ins.then_inc(ml_diag.sem, 1)
                    if h:
                        dve.wait_ge(ml_num.sem, ml_num.at(h, L))
                    for i in range(PT_):
                        n = 128 * (PT_ - i)
                        dve.wait_ge(ml_qk.sem, ml_qk.at(4 * h + i + 1, L))
                        dve.wait_ge(ml_E.sem, ml_E.at(4 * h + i + 1, L))
                        tt(W[:, wo[i]:wo[i] + n], E[:, wo[i]:wo[i] + n], ps[1 + i % 2][:, 0:n], ALU.mult).then_inc(ml_W.sem, 1)
                    rotations(h)
                    dve.wait_ge(ml_num.sem, ml_num.at(h + 1, L))
                    ts_(hden, ps[4][:, 0:4], -1.0, None, ALU.mult)
                    drain()
                    tt(hden, hden, ps[4][:, 0:4], ALU.max)
                    drain()
                    tt(hden, hden, RT[:, 0:4, 2, h], ALU.max)
                    drain()
                    V.reciprocal(hden, hden)
                    drain()
                    tt(proj[:, :, C_MV + DV * h:C_MV + DV * h + DV],
                                   ps[3][:, :].rearrange("p (t d) -> p t d", t=PT_), bc(hden, 2, DV), ALU.mult).then_inc(ml_numc.sem, 1)
                drain()
                Hv = proj[:, :, C_MV:C_MV + 512].rearrange("p t (h d) -> p t h d", h=MH)
                Hsq = work[:, 0:2048].rearrange("p (t h d) -> p t h d", t=PT_, h=MH)
                tt(Hsq, Hv, Hv, ALU.mult)
                drain()
                red(hvar.rearrange("p (t h) -> p t h", t=PT_), Hsq, X, ALU.add)
                drain()
                ts_(hvar, hvar, 1.0 / DV, EPS, ALU.mult, ALU.add).then_inc(h_var.sem, 1)
                dve.wait_ge(h_root.sem, h_root.at(1, L))
                V.reciprocal(hvar, hvar)
                drain()
                tt(Hv, Hv, bc(hvar.rearrange("p (t h) -> p t h", t=PT_), 3, DV), ALU.mult)
                drain()
                hflat = proj[:, :, C_MV:C_MV + 512]
                tt(hflat, hflat, bc(rows_bc[:, 0:512], 1, PT_), ALU.mult)
                drain()
                tt(proj[:, :, C_MO:C_MO + 512], proj[:, :, C_MO:C_MO + 512], hflat, ALU.mult)
                dve.drain().then_inc(stage_done, 1)
                dve.wait_ge(stage_done, stage_end(6, L))
                stand_alone(dve)
                for n in range(1, 12, 2):
                    dve.wait_ge(th_tr.sem, th_tr.at(n + 1, L))
                    ts_(TH[0:64, n, :], ps[n % 4][0:64, :], HD ** -0.5 if n < 8 else 1.0, None, ALU.mult).then_inc(th_dve.sem, 1)
                dve.wait_ge(cm_mean.sem, cm_mean.at(1, L))
                cp(KmT[0:64, :], ps[4][0:64, 0:16])
                vr = bc(ps[5][0:64, 0:128].rearrange("p (k d) -> p k d", k=KV), 2, AG)
                tt(VmBD[0:64, :].rearrange("p (k g d) -> p k g d", k=KV, g=AG), vr,
                                bc(K["hmask"][0:64, :].rearrange("p (k g) -> p k g", k=KV), 3, HD), ALU.mult).then_inc(cm_meanc.sem, 1)
                dve.wait_ge(cm_s.sem, cm_s.at(1, L))
                c4 = cS.rearrange("p (t h n) -> p t h n", t=PT_, h=AH)
                smv = sm[:, 0:32].rearrange("p (t h) -> p t h", t=PT_)
                tt(c4, ps[6][:, 0:256].rearrange("p (t h n) -> p t h n", t=PT_, h=AH),
                   bc(view("cmpadd", "p (t n) -> p t n", t=PT_), 2, AH), ALU.add)
                drain()
                red(smv, c4, X, ALU.max)
                drain()
                tt(c4, c4, bc(smv, 3, 8), ALU.subtract).then_inc(cm_sub.sem, 1)
                dve.wait_ge(cm_exp.sem, cm_exp.at(1, L))
                tt(c4, c4, bc(view("cmp01", "p (t n) -> p t n", t=PT_), 2, AH), ALU.mult)
                drain()
                red(smv, c4, X, ALU.add)
                drain()
                ts_(sm[:, 32:64], sm[:, 0:32], 0.5, None, ALU.max)
                drain()
                V.reciprocal(sm[:, 64:96], sm[:, 32:64])
                drain()
                gv = gates[:, :, :].rearrange("p t (h b) -> p t h b", b=3)
                tt(smv, sm[:, 64:96].rearrange("p (t h) -> p t h", t=PT_), gv[:, :, :, 0], ALU.mult)
                drain()
                tt(c4, c4, bc(smv, 3, 8), ALU.mult).then_inc(cm_p.sem, 1)
                dve.wait_ge(cm_t.sem, cm_t.at(1, L))
                cp(PTb[0:64, 0, :], ps[7][0:64, :]).then_inc(cm_tc.sem, 1)
                dve.drain().then_inc(stage_done, 1)
                dve.wait_ge(stage_done, stage_end(7, L))
                stand_alone(dve)
                with dve.Fori(0, 4) as j:
                    def maxed(u):
                        t = u % 4
                        s = ps[u % 3]
                        dve.wait_ge(a_s.sem, a_s.at(u + 1, L, j))
                        tt(s[:, 128 * t:128 * t + 128], s[:, 128 * t:128 * t + 128], K["causal"], ALU.add)
                        drain()
                        red(nmax[:, u:u + 1], s[:, 0:128 * t + 128], X, ALU.max, negate=True).then_inc(a_max.sem, 1)

                    def added(u):
                        hh, br, t = u // 8, u // 4 % 2, u % 4
                        dve.wait_ge(a_pv.sem, a_pv.at(u + 1, L, j))
                        V.reciprocal(rg[:, 0:1], den[:, u:u + 1])
                        drain()
                        tt(rg[:, 1:2], rg[:, 0:1], gnow[:, t, hh, br:br + 1], ALU.mult)
                        drain()
                        o_ = proj[:, t, bass.ds(j * 64 + 256 * hh, HD)]
                        stt(o_, ps[5 + u % 2][:, 0:HD], rg[:, 1:2], o_, ALU.mult, ALU.add).then_inc(a_acc.sem, 1)

                    ggv = gates[:, :, :].rearrange("p t (k g b) -> p t k g b", k=KV, g=AG)
                    for hh in range(2):
                        ins = cp(gnow[:, :, hh, :], ggv[:, :, hh, bass.ds(j, 1), 1:3].squeeze(2))
                    ins.then_inc(g_stage.sem, 1)
                    drain()
                    maxed(0)
                    maxed(1)
                    for u in range(U):
                        if u + 2 < U:
                            maxed(u + 2)
                        if u >= 1:
                            added(u - 1)
                    added(U - 1)
                    drain()
                dve.drain().then_inc(stage_done, 1)
                dve.wait_ge(stage_done, stage_end(8, L))
                stand_alone(dve)
                cp(Ssb[0:TS, 0:512].rearrange("p (g k d) -> p g k d", g=AG, k=KV),
                              proj_s[:, 0:512].rearrange("p (k g d) -> p g k d", k=KV, g=AG)).then_inc(d_pair.sem, 1)
                dve.wait_ge(d_tr.sem, d_tr.at(1, L))
                ts_(qTs[:, :, :].rearrange("p a b -> p (a b)"), ps[4][:, 0:128], HD ** -0.5, None, ALU.mult)
                cp(KN[:, :, :].rearrange("p a b -> p (a b)"), ps[4][:, 128:192])
                for g in range(2):
                    pr = ps[5][:, 24 * g:24 * g + 24].rearrange("p (h b) -> p b h", b=3)
                    gt_ = small[:, 0:24].rearrange("p (b h) -> p b h", b=3)
                    tt(gt_, pr, bc(K["hsel"], 1, 3), ALU.mult)
                    drain()
                    red(gq[:, g, :], gt_, X, ALU.add)
                    drain()
                V.memset(aTs[:, :, :], 0.0)
                V.memset(Qbd[:, :, :], 0.0)
                V.memset(P4, 0.0)
                dve.drain().then_inc(stage_done, 1)
                dve.wait_ge(stage_done, stage_end(9, L))
                stand_alone(dve)
                for j in range(2):
                    for k in range(KV):
                        src = qTs[64 * k:64 * k + 64, :, bass.ds(j * 16, 16)].rearrange("p g (b t) -> p b g t", b=4)
                        cp(Qbd[64 * k:64 * k + 64, :, 16 * k:16 * k + 16].rearrange("p b (g t) -> p b g t", g=AG), src)
                    cp(rownow.rearrange("p h t -> p (h t)"), K["rowtok"][:, bass.ds(j * 256, 256)])
                    cp(gq_now[:, :], gq[:, bass.ds(j, 1), :].squeeze(1))
                    dve.drain().then_inc(d_q.sem, 1)
                    dve.wait_ge(d_cs.sem, d_cs.at(1, L, j))
                    red(small[:, 0:1], ps[4][:, 0:16], X, ALU.max, negate=True).then_inc(d_csub.sem, 1)
                    dve.wait_ge(d_cexp.sem, d_cexp.at(1, L, j))
                    V.reciprocal(small[:, 6:7], small[:, 1:2])
                    drain()
                    ts_(imp[:, 0:16], imp[:, 0:16], small[:, 6:7], None, ALU.mult)
                    drain()
                    for b in range(4):
                        r = slice(32 * b, 32 * b + 32)
                        ins = ts_(P4[r, 16 * b:16 * b + 16], imp[r, 0:16], gq_now[r, 0:1], None, ALU.mult)
                    ins.then_inc(d_cp.sem, 1)
                    dve.wait_ge(d_imp.sem, d_imp.at(1, L, j))
                    red(small[:, 7:8], ps[2][:, 1:16], X, ALU.min)
                    drain()
                    ts_(small[:, 16:31], ps[2][:, 1:16], small[:, 7:8], None, ALU.is_equal)
                    drain()
                    tt(small[:, 16:31], small[:, 16:31], K["iota"], ALU.mult)
                    drain()
                    red(small[:, 8:9], small[:, 16:31], X, ALU.max)
                    V.memset(small[:, 32:33], 0.0)
                    drain()
                    ts_(small[:, 33:48], K["iota"], small[:, 8:9], NEG, ALU.is_equal, ALU.mult)
                    drain()
                    newa = K["newadd"][:, bass.ds(j * TS, TS)]
                    for br in range(2):
                        nt = (8, 4)[br]
                        wd = 128 * nt + TS
                        dve.wait_ge(d_s.sem, d_s.at(br + 1, L, j))
                        if br == 0:
                            for q in range(2):
                                tt(Ssb[:, 512 * q:512 * q + 512].rearrange("p (n d) -> p n d", n=8),
                                   ps[5 + q][:, :].rearrange("p (n d) -> p n d", n=8),
                                   bc(small[:, 32 + 8 * q:40 + 8 * q], 2, BLK), ALU.add)
                        else:
                            dve.wait_ge(d_pt.sem, d_pt.at(1, L, j))
                            cp(Ssb[:, 0:512], ps[5][:, :])
                            drain()
                            f4 = Ssb[:, 0:512].rearrange("p (n d) -> p n d", n=4)[:, :, 0]
                            tt(f4, f4, K["winadd"], ALU.add)
                        tt(Ssb[:, 128 * nt:wd], ps[7][:, 0:TS], newa, ALU.add)
                        drain()
                        red(small[:, 2 + br:3 + br], Ssb[:, 0:wd], X, ALU.max, negate=True).then_inc(d_max.sem, 1)
                    dve.wait_ge(d_pv.sem, d_pv.at(2, L, j))
                    V.reciprocal(small[:, 9:11], small[:, 4:6])
                    cp(cmb, ps[4][:, 128:256])
                    drain()
                    tt(small[:, 11:13], small[:, 9:11], gq_now[:, 1:3], ALU.mult)
                    drain()
                    stt(cmb, ps[4][:, 256:384], small[:, 11:12], cmb, ALU.mult, ALU.add)
                    drain()
                    stt(cmb, ps[2][:, 128:256], small[:, 12:13], cmb, ALU.mult, ALU.add).then_inc(d_cmb.sem, 1)
                    dve.wait_ge(d_out.sem, d_out.at(1, L, j))
                    tt(aTs[:, :, :].rearrange("p a b -> p (a b)"), aTs[:, :, :].rearrange("p a b -> p (a b)"),
                                 ps[3][:, 256:384], ALU.add).then_inc(d_add.sem, 1)
                    drain()
                dve.drain().then_inc(stage_done, 1)
                dve.wait_ge(stage_done, stage_end(10, L))
                stand_alone(dve)
                tt(kws.rearrange("p (h d) -> p h d", h=MH), proj_s[:, C_MK:C_MK + 256].rearrange("p (h d) -> p h d", h=MH),
                   bc(RT[0:TS, 4, 1, :], 2, DK), ALU.mult)
                drain()
                tt(awl[0:TS, :, :], bc(K["lastT"][0:TS, :], 2, MH), bc(RT[0:TS, 4, 3, :], 1, NB), ALU.mult).then_inc(ms_kq.sem, 1)
                dve.wait_ge(ms_dec.sem, ms_dec.at(1, L))
                cp(decayb[0:64, :], ps[6][0:64, 0:NB * MH])
                dve.wait_ge(st_in, L * 32 + 32)
                Cv = Cst[0:64, :, :].rearrange("p (b h) d -> p b h d", h=MH)
                Cn = Cnew[0:64, :, :].rearrange("p (b h) d -> p b h d", h=MH)
                dv_, nv, nn = [a[0:64, :].rearrange("p (b h) -> p b h", h=MH) for a in (decayb, nst, nnew)]
                for h in range(MH):
                    if h:
                        dve.wait_ge(ms_C.sem, ms_C.at(2 * h, L))
                    tt(Qm[0:64, :, :], bc(mqks[:, h, :], 1, NB), view("inbatch", "p (b t) -> p b t", b=NB)[0:64], ALU.mult)
                    tt(kwb[0:TS, :, :], bc(kws[:, DK * h:DK * h + DK], 1, NB), bc(K["inbatchT"][0:TS, :], 2, DK),
                                ALU.mult).then_inc(ms_q.sem, 1)
                    dve.wait_ge(ms_g.sem, ms_g.at(h + 1, L))
                    tt(Es[0:TS, :], ps[0][0:TS, 0:TS], K["samebatch"][0:TS, :], ALU.add).then_inc(ms_E.sem, 1)
                    dve.wait_ge(ms_W.sem, ms_W.at(h + 1, L))
                    tt(Ws[0:TS, :], Es[0:TS, :], ps[1][0:TS, 0:TS], ALU.mult).then_inc(ms_Wd.sem, 1)
                    dve.wait_ge(ms_num.sem, ms_num.at(h + 1, L))
                    cp(hs2[0:TS, 0:DV + 1], ps[2][0:TS, 0:DV + 1])
                    drain()
                    stt(nd[0:TS, :], ps[3][0:TS, 0:DV + 1], RT[0:TS, 4, 3, h:h + 1], hs2[0:TS, 0:DV + 1], ALU.mult, ALU.add)
                    drain()
                    d1 = h_small[0:TS, 0:1]
                    stt(d1, nd[0:TS, DV:DV + 1], -1.0, nd[0:TS, DV:DV + 1], ALU.mult, ALU.max)
                    drain()
                    tt(d1, d1, RT[0:TS, 4, 2, h:h + 1], ALU.max)
                    drain()
                    V.reciprocal(d1, d1)
                    drain()
                    ts_(hs[0:TS, DV * h:DV * h + DV], nd[0:TS, 0:DV], d1, None, ALU.mult).then_inc(ms_numc.sem, 1)
                    for half in range(2):
                        r = slice(4 * half, 4 * half + 4)
                        tt(Cn[:, r, h, :], Cv[:, r, h, :], bc(dv_[:, r, h], 2, DV), ALU.mult)
                        tt(nn[:, r, h], nv[:, r, h], dv_[:, r, h], ALU.mult)
                        drain()
                        dve.wait_ge(ms_C.sem, ms_C.at(2 * h + half + 1, L))
                        tt(Cn[:, r, h, :], Cn[:, r, h, :], ps[4][0:64, :].rearrange("p (b d) -> p b d", b=4), ALU.add)
                        tt(nn[:, r, h], nn[:, r, h], ps[5][0:64, 0:4], ALU.add).then_inc(ms_Cc.sem, 1)
                drain()
                h3 = hs[0:TS, :].rearrange("p (h d) -> p h d", h=MH)
                tt(hs2[0:TS, :], hs[0:TS, :], hs[0:TS, :], ALU.mult)
                drain()
                red(h_small[0:TS, 4:8], hs2[0:TS, :].rearrange("p (h d) -> p h d", h=MH), X, ALU.add)
                drain()
                ts_(h_small[0:TS, 8:12], h_small[0:TS, 4:8], 1.0 / DV, EPS, ALU.mult, ALU.add).then_inc(hs_var.sem, 1)
                dve.wait_ge(hs_root.sem, hs_root.at(1, L))
                V.reciprocal(h_small[0:TS, 12:16], h_small[0:TS, 8:12])
                drain()
                tt(h3, h3, bc(h_small[0:TS, 12:16], 2, DV), ALU.mult)
                drain()
                tt(hs[0:TS, :], hs[0:TS, :], rows_bc[0:TS, 0:512], ALU.mult)
                drain()
                tt(hs[0:TS, :], hs[0:TS, :], proj_s[:, C_MO:C_MO + 512], ALU.mult)
                dve.drain().then_inc(stage_done, 1)
                dve.wait_ge(stage_done, stage_end(11, L))
                stand_alone(dve)
                dve.wait_ge(ms_t.sem, ms_t.at(1, L))
                cp(xnT[:, 4:8, SEQ:TT], ps[0][:, 0:128].rearrange("p (c t) -> p c t", c=4))
                cp(xnT[:, 0:4, SEQ:TT], aTs[:, :, :])
                dve.drain().then_inc(stage_done, 1)
                dve.wait_ge(stage_done, stage_end(12, L))
                stand_alone(dve)

                def residual(cx, lo, hi, mod):
                    x_ = xT[:, cx, :].squeeze(1) if not isinstance(cx, int) else xT[:, cx, :]
                    gp = modT[:, mod, 0:1] if isinstance(cx, int) else modT[:, mod, 0:1].squeeze(1)
                    gs = modT[:, mod, 1:9] if isinstance(cx, int) else modT[:, mod, 1:9].squeeze(1)
                    tmp = up[:, 0, 0:TS]
                    tt(tmp.rearrange("p (b t) -> p b t", b=NB), hi[:, SEQ - HALF:HALF].rearrange("p (b t) -> p b t", b=NB),
                       bc(gs, 2, NT), ALU.mult)
                    stt(x_[:, 0:HALF], lo[:, 0:HALF], gp, x_[:, 0:HALF], ALU.mult, ALU.add)
                    stt(x_[:, HALF:SEQ], hi[:, 0:SEQ - HALF], gp, x_[:, HALF:SEQ], ALU.mult, ALU.add)
                    drain()
                    return tt(x_[:, SEQ:TT], x_[:, SEQ:TT], tmp, ALU.add)

                for c in range(8):
                    dve.wait_ge(o_acc.sem, o_acc.at(c + 1, L))
                    residual(c, ps[2 * (c % 4)], ps[2 * (c % 4) + 1], 16 + c).then_inc(o_add.sem, 1)
                    drain()
                dve.drain().then_inc(stage_done, 1)
                dve.wait_ge(stage_done, stage_end(13, L))
                stand_alone(dve)
                norm_dve(NRM["n2"], 8, 32, 24, L)
                dve.wait_ge(cv_t.sem, cv_t.at(1, L))
                cp(convS[:, :, :].rearrange("p c n -> p (c n)"), ps[2][:, 0:16 * FC])
                V.memset(up[:, :, 0:2], 0.0)
                dve.drain().then_inc(stage_done, 1)
                dve.wait_ge(stage_done, stage_end(14, L))
                stand_alone(dve)

                def hidden(c, cd, j=0):
                    s = c % 2
                    one = isinstance(cd, int)
                    cix = cd if one else bass.ds(cd, 1)
                    hist = convS[:, cix, :] if one else convS[:, cix, :].squeeze(1)
                    cp(up[:, s, 2 + SEQ:UPW].rearrange("p (b t) -> p b t", b=NB)[:, :, 0:2],
                       hist.rearrange("p (b t) -> p b t", b=NB))
                    for w_ in range(3):
                        cp(cwt[:, 3 * s + w_:3 * s + w_ + 1], colsB[:, bass.ds(cd + FC * w_, 1)])
                    cp(cbias[:, s:s + 1], colsB[:, bass.ds(cd + 66, 1)])
                    drain()
                    dve.wait_ge(u_cp.sem, u_cp.at(c + 1 + j * 6, L))
                    n = UPW - 2
                    ts_(cv[:, s, 0:n], up[:, s, 0:n], cwt[:, 3 * s:3 * s + 1], None, ALU.mult)
                    drain()
                    stt(cv[:, s, 0:n], up[:, s, 1:1 + n], cwt[:, 3 * s + 1:3 * s + 2], cv[:, s, 0:n], ALU.mult, ALU.add)
                    ul = uLast[:, cix, :] if one else uLast[:, cix, :].squeeze(1)
                    cp(ul[:, 0:2], up[:, s, SEQ:SEQ + 2])
                    cp(ul[:, 2:18].rearrange("p (b t) -> p b t", b=NB),
                       up[:, s, 2 + SEQ:UPW].rearrange("p (b t) -> p b t", b=NB)[:, :, 4:6])
                    drain()
                    stt(cv[:, s, 0:n], up[:, s, 2:2 + n], cwt[:, 3 * s + 2:3 * s + 3], cv[:, s, 0:n], ALU.mult, ALU.add).then_inc(u_cv.sem, 1)
                    dve.wait_ge(u_si.sem, u_si.at(c + 1 + j * 6, L))
                    g0, g1 = ps[4 * s + 2], ps[4 * s + 3]
                    h_ = hT[:, cix, :] if one else hT[:, cix, :].squeeze(1)
                    tt(h_[:, 0:HALF], g0[:, 0:HALF], cv[:, s, 0:HALF], ALU.mult)
                    tt(h_[:, HALF:SEQ], g1[:, 0:SEQ - HALF], cv[:, s, HALF:SEQ], ALU.mult)
                    tt(h_[:, SEQ:TT].rearrange("p (b t) -> p b t", b=NB),
                               g1[:, SEQ - HALF:HALF].rearrange("p (b t) -> p b t", b=NB),
                               cv[:, s, 2 + SEQ:UPW].rearrange("p (b t) -> p b t", b=NB)[:, :, 0:4], ALU.mult).then_inc(u_h.sem, 1)

                with dve.Fori(0, 3) as j:
                    for c in range(6):
                        hidden(c, j * 6 + c, j)
                    drain()
                for c in range(18, FC):
                    hidden(c, c)
                drain()

                def down(c, cd, j=0):
                    dve.wait_ge(y_acc.sem, y_acc.at(c + 1 + j * 3, L))
                    one = isinstance(cd, int)
                    r = residual(cd if one else bass.ds(cd, 1), ps[2 * (c % 3)], ps[2 * (c % 3) + 1],
                                 40 + cd if one else bass.ds(cd + 40, 1))
                    r.then_inc(y_add.sem, 1)
                    drain()

                with dve.Fori(0, 2) as j:
                    for c in range(3):
                        down(c, j * 3 + c, j)
                for c in (6, 7):
                    down(c, c)
                dve.drain().then_inc(stage_done, 1)
                dve.wait_ge(stage_done, stage_end(15, L))
                stand_alone(dve)

            norm_rstd(dict(used=final_used, var=final_var, root=final_sqrt))
            for k in range(KC):
                stt(xnT[:, k, :], xT[:, k, :], colsB[:, 88 + k:89 + k], rstd[:, :], ALU.mult, ALU.mult).then_inc(final_xn.sem, 1)

        @block.gpsimd
        def _(pool):
            ld = pool.dma_start
            pool.dma_start(cst[:, :], A["shape_constants"][:, 0:sum(_WIDTHS)]).then_inc(load_in, 16)
            ld(xrow[:, :, :], A["x_prompt"][0].rearrange("(t p) d -> p t d", p=128)).then_inc(load_in, 16)
            ld(crow2[0:TS, :], A["x_sample"].rearrange("b t d -> (b t) d")).then_inc(load_in, 16)
            ld(crow[0:1, :], A["c_prompt"]).then_inc(load_in, 16)
            ld(crow[1:9, :], A["c_sample"]).then_inc(load_in, 16)
            ld(pages_sb[:, :], A["page_table"].rearrange("b n -> (b n)").unsqueeze(0)).then_inc(load_in, 16)
            pool.wait_ge(load_in, PRO_LOADS)
            n_st = [0]
            ST_ALL = 16 * (3 + 2 + NB + 1 + NB + 2 + 16 + 2 + 2)

            with pool.Fori(0, DEPTH) as L:
                def put(dst, src):
                    n_st[0] += 16
                    return pool.dma_start(dst, src).then_inc(stored, 16)

                def all_stored():
                    pool.wait_ge(stored, L * ST_ALL + n_st[0])
                    stand_alone(pool)

                pool.drain().then_inc(stage_done, 1)

                pool.wait_ge(stage_done, stage_end(1, L))

                stand_alone(pool)
                r8 = lambda a: a.rearrange("(k n) -> k n", n=128)
                row = lambda name: A[name][L, :]
                for dst, src in ((rowsA[0:8, :], r8(row("norm1_g"))), (rowsA[8:16, :], r8(row("norm2_g"))),
                                 (rowsA[16:64, :], r8(row("b_mod"))),
                                 (rowsB[0:66, :], A["w_conv"][L, :, :].rearrange("w (k n) -> (w k) n", n=128)),
                                 (rowsB[66:88, :], r8(row("b_conv"))), (rowsB[88:96, :], r8(A["final_g"])),
                                 (rows_bc[:, 0:512], row("mlstm_norm_g").partition_broadcast(128)),
                                 (rows_bc[:, 512:520], row("b_if").partition_broadcast(128)),
                                 (seqc, A["shape_constants"][0:MH, sum(_WIDTHS):].rearrange("p (a n) -> p a n", a=2)),
                                 (m0s[:, :], A["state_mlstm_m"][L, :, :].rearrange("b h -> h b"))):
                    pool.dma_start(dst, src, allow_slow_non_contiguous=True).then_inc(rows_in, 16)
                pool.wait_ge(rows_in, L * ROWS_PER_LAYER + ROWS_PER_LAYER)
                stand_alone(pool)
                for n in (2, 3, 4):
                    pool.drain().then_inc(stage_done, 1)
                    pool.wait_ge(stage_done, stage_end(n, L))
                    stand_alone(pool)
                pool.wait_ge(ml_rows.sem, ml_rows.at(1, L))
                stand_alone(pool)
                put(p_m[L].rearrange("o h -> h o"), rr[:, 4, SEQ - 1:SEQ])
                for b in range(NB):
                    put(s_m[L][b].unsqueeze(1), rr[:, 4, SEQ + NT * b + NT - 1:SEQ + NT * b + NT])
                pool.drain().then_inc(stage_done, 1)
                pool.wait_ge(stage_done, stage_end(5, L))
                stand_alone(pool)
                pool.wait_ge(roped.sem, roped.at(1, L))
                stand_alone(pool)
                for o_p, o_s, c in ((p_cmp, s_cmp, C_KC), (p_sel, s_sel, C_KS), (p_win, s_win, C_KW)):
                    put(o_p[L].rearrange("o (t p) a k d -> p (o t) (a k d)", p=128), proj[:, :, c:c + 256])
                    if c == C_KW:
                        for b in range(NB):
                            put(o_s[L][b, WINDOW - NT:WINDOW].rearrange("t a k d -> t (a k d)"), proj_s[NT * b:NT * b + NT, c:c + 256])
                    else:
                        put(o_s[L].rearrange("b t a k d -> (b t) (a k d)"), proj_s[:, c:c + 256])
                pool.wait_ge(ml_Cc.sem, ml_Cc.at(MH, L))
                stand_alone(pool)
                put(p_C[L].rearrange("o h k v -> k (o h) v"), Cp[0:64, :, 0:DV])
                pool.dma_start(p_n[L].rearrange("o h k -> k (o h)"), Cp[0:64, :, DV], allow_slow_non_contiguous=True).then_inc(stored, 16)
                n_st[0] += 16
                all_stored()
                for n in (6, 7, 8):
                    pool.drain().then_inc(stage_done, 1)
                    pool.wait_ge(stage_done, stage_end(n, L))
                    stand_alone(pool)
                pool.wait_ge(mx_t.sem, mx_t.at(8, L))
                stand_alone(pool)
                by_part = lambda a: a.rearrange("(p i) a k d -> p (i a k d)", i=4)
                for b in range(NB):
                    pool.dma_start(wpg[b].rearrange("p i c -> p (i c)"), by_part(A["cache_win_kv"][L][b])).then_inc(wpg_in[b // 4], 16)
                pool.drain().then_inc(stage_done, 1)
                pool.wait_ge(stage_done, stage_end(9, L))
                stand_alone(pool)
                for b in range(NB):
                    if b % 4 == 0:
                        pool.wait_ge(wpg_in[b // 4], L * 64 + 64)
                        stand_alone(pool)
                    ob = by_part(s_win[L][b][0:WINDOW - NT])
                    for lo, hi in ((1, 113), (113, 128)):
                        put(ob[lo - 1:hi - 1], wpg[b][lo:hi].rearrange("p i c -> p (i c)"))
                all_stored()
                pool.wait_ge(d_pv.sem, d_pv.at(1, L, 1))
                stand_alone(pool)
                pool.dma_start(Cst[0:64, :, :], A["state_mlstm_C"][L].rearrange("b h k v -> k (b h) v")).then_inc(st_in, 16)
                pool.dma_start(nst[0:64, :], A["state_mlstm_n"][L].rearrange("b h k -> k (b h)"), allow_slow_non_contiguous=True).then_inc(st_in, 16)
                pool.wait_ge(st_in, L * 32 + 32)
                stand_alone(pool)
                pool.drain().then_inc(stage_done, 1)
                pool.wait_ge(stage_done, stage_end(10, L))
                stand_alone(pool)
                pool.drain().then_inc(stage_done, 1)
                pool.wait_ge(stage_done, stage_end(11, L))
                stand_alone(pool)
                put(s_C[L].rearrange("b h k v -> k (b h) v"), Cnew[0:64, :, :])
                pool.dma_start(s_n[L].rearrange("b h k -> k (b h)"), nnew[0:64, :], allow_slow_non_contiguous=True).then_inc(stored, 16)
                n_st[0] += 16
                pool.drain().then_inc(stage_done, 1)
                pool.wait_ge(stage_done, stage_end(12, L))
                stand_alone(pool)
                pool.dma_start(csrow[0:16, :], A["state_ffn_conv"][L].rearrange("b j f -> (b j) f")).then_inc(cv_in, 16)
                all_stored()
                pool.drain().then_inc(stage_done, 1)
                pool.wait_ge(stage_done, stage_end(13, L))
                stand_alone(pool)
                pool.drain().then_inc(stage_done, 1)
                pool.wait_ge(stage_done, stage_end(14, L))
                stand_alone(pool)
                pool.drain().then_inc(stage_done, 1)
                pool.wait_ge(stage_done, stage_end(15, L))
                stand_alone(pool)
                put(p_conv[L].rearrange("o j f -> (o j) f"), ulrow[0:2, :])
                put(s_conv[L].rearrange("b j f -> (b j) f"), ulrow[2:18, :])
                all_stored()
                assert n_st[0] == ST_ALL, (n_st[0], ST_ALL)
            for n in range(10):
                t, hf = n // 2, n % 2
                pool.wait_ge(final_copy.sem, final_copy.at(n + 1))
                dst = y_p[0, 128 * t:128 * t + 128, 512 * hf:512 * hf + 512] if t < 4 else \
                    y_s.rearrange("b t d -> (b t) d")[:, 512 * hf:512 * hf + 512]
                pool.dma_start(dst, ybuf[0:128 if t < 4 else TS, n, :]).then_inc(stored, 16)
            pool.wait_ge(stored, DEPTH * ST_ALL + 160)


_INS = ["x_prompt", "x_sample", "cache_cmp_kv", "cache_sel_kv", "cache_win_kv", "state_mlstm_C", "state_mlstm_n",
        "state_mlstm_m", "state_ffn_conv", "page_table", "c_prompt", "c_sample", "norm1_g", "norm2_g", "w_mod", "b_mod",
        "w_in", "b_if", "mlstm_norm_g", "w_out", "w_up", "w_conv", "b_conv", "w_down", "final_g"]
_KVS = (2, KV, HD)
_OUTS = [(1, SEQ, D), (NB, NT, D), (DEPTH, 1, SEQ) + _KVS, (DEPTH, 1, SEQ) + _KVS, (DEPTH, 1, SEQ) + _KVS,
         (DEPTH, 1, MH, DK, DV), (DEPTH, 1, MH, DK), (DEPTH, 1, MH), (DEPTH, 1, 2, FF),
         (DEPTH, NB, NT) + _KVS, (DEPTH, NB, NT) + _KVS, (DEPTH, NB, WINDOW) + _KVS,
         (DEPTH, NB, MH, DK, DV), (DEPTH, NB, MH, DK), (DEPTH, NB, MH), (DEPTH, NB, 2, FF)]


def kernel(**inputs):
    import numpy as _np
    import concourse.bacc as _bacc
    from concourse import mybir as _mybir
    from concourse.bass_utils import run_bass_kernel_spmd as _run

    nc = _bacc.Bacc("TRN2", target_bir_lowering=False, num_devices=1)
    arrays, args = {}, {}
    for name in _INS:
        a = _np.ascontiguousarray(inputs[name])
        arrays[f"in_{name}"] = a
        args[name] = nc.dram_tensor(f"in_{name}", a.shape, _mybir.dt.from_np(a.dtype), kind="ExternalInput").ap()
    c = _np.ascontiguousarray(_np.concatenate(shape_constants(), axis=1))
    arrays["in_shape_constants"] = c
    args["shape_constants"] = nc.dram_tensor("in_shape_constants", c.shape, _mybir.dt.float32, kind="ExternalInput").ap()
    outs = [nc.dram_tensor(f"out_{i}", s, _mybir.dt.float32, kind="ExternalOutput").ap() for i, s in enumerate(_OUTS)]
    trunk_program(nc, args, outs)
    r = _run(nc, [arrays], core_ids=[0])
    return tuple(r.results[0][f"out_{i}"] for i in range(len(_OUTS)))
```

```python
import numpy as np
import concourse.bass as bass
from concourse import mybir
from contextlib import ExitStack

D = 1024
SEQ = 512
DEPTH = 2
NB = 8
NT = 4
PAST = 1024
PAGE = 128
N_PHYS = 80
HD = 64
AH = 8
KV = 2
AG = AH // KV
BLK = 64
WINDOW = 512
MH = 4
DK = 64
DV = 128
FF = 2816
EPS = 1e-6
KC = D // 128
TS = NB * NT
TT = SEQ + TS
HALF = TT // 2
PT_ = SEQ // 128
NPG = PAST // PAGE
NEG = -1e30
C_Q, C_KC, C_KS, C_KW, C_G = 0, 512, 768, 1024, 1280
C_MQ, C_MK, C_MV, C_MO, C_IF = 1304, 1560, 1816, 2328, 2840
IN_W = 2848
IN_SLABS = [(512 * i, min(512, IN_W - 512 * i)) for i in range(6)]
FC = FF // 128
U = 16
UPW = 2 + SEQ + NB * (NT + 2)

_NAMES = ["ident", "ones", "causal", "causalT", "cos", "sin", "cmpadd", "cmp01", "ind8", "ind64", "hmask",
          "ind2", "slide", "sum32", "samegroup", "iota", "newadd", "winadd", "tokrow", "hsel", "rowtok",
          "onehot", "samebatch", "inbatch", "inbatchT", "lastT"]
_SEQ_NAMES = ["seg", "pen"]


def shape_constants():
    f = np.float32
    p = np.arange(128)
    c = {}
    c["ident"] = np.eye(128, dtype=f)
    c["ones"] = np.ones((128, 128), f)
    c["causal"] = np.where(p[None, :] <= p[:, None], 0, NEG).astype(f)
    c["causalT"] = np.where(p[None, :] >= p[:, None], 0, NEG).astype(f)
    half = HD // 2
    freq = np.power(f(10000.0), (f(-2.0) * np.arange(half, dtype=f) / f(HD))).astype(f)
    pos = np.concatenate([np.arange(SEQ).reshape(PT_, 128), (PAST + p % NT)[None]]).astype(f)
    ang = (pos.T[:, :, None] * freq[None, None, :]).astype(f)
    c["cos"] = np.cos(ang).astype(f)
    c["sin"] = np.sin(ang).astype(f)
    tok = np.arange(SEQ).reshape(PT_, 128).T
    ok = (np.arange(8)[None, None, :] + 1) * BLK <= tok[:, :, None] + 1
    c["cmpadd"] = np.where(ok, 0, NEG).astype(f)
    c["cmp01"] = ok.astype(f)
    ind8 = (tok[:, :, None] // BLK == np.arange(8)[None, None, :]) / f(BLK)
    c["ind8"] = ind8.astype(f)
    c["ind64"] = np.tile(ind8[:, :, None, :], (1, 1, 8, 1)).astype(f)
    c["hmask"] = (p[:, None] // 8 == np.arange(8)[None, :]).astype(f)
    c["ind2"] = ((p[:, None] // BLK == np.arange(2)[None, :]) / f(BLK)).astype(f)
    slide = np.zeros((128, 126), f)
    slide[:, 62:64] = c["ind2"]
    c["slide"] = slide
    c["sum32"] = (p[:, None] % 32 == np.arange(32)[None, :]).astype(f)
    rb, rk, rg, rt = p // 32, p // 16 % 2, p // 4 % 4, p % 4
    key = rb * 8 + rk * 4 + rt
    c["samegroup"] = (key[:, None] == key[None, :]).astype(f)
    c["iota"] = np.tile(np.arange(1, 16, dtype=f), (128, 1))
    tb, tt = np.arange(TS) // NT, np.arange(TS) % NT
    grp = np.arange(2)
    same = (grp[None, :, None] * 4 + rb[:, None, None]) == tb[None, None, :]
    c["newadd"] = np.where(same & (tt[None, None, :] <= rt[:, None, None]), 0, NEG).astype(f)
    c["winadd"] = np.where(np.arange(4)[None, :] > rt[:, None], 0, NEG).astype(f)
    match = same & (tt[None, None, :] == rt[:, None, None])
    t32 = np.zeros((128, 2, 128), f)
    t32[:TS] = match.transpose(2, 1, 0)
    c["tokrow"] = t32
    head = rk * 4 + rg
    c["hsel"] = (head[:, None] == np.arange(8)[None, :]).astype(f)
    c["rowtok"] = (match[:, :, None, :] * c["hsel"][:, None, :, None]).astype(f)
    oh = np.zeros((128, MH, 128), f)
    for h in range(MH):
        oh[h, h] = 1
    c["onehot"] = oh
    seg = np.ones(TT, f)
    seg[SEQ::NT] = 0
    c["seg"] = np.tile(seg, (128, 1))
    c["pen"] = np.tile(np.where(seg == 0, NEG, 0).astype(f), (128, 1))
    sb = np.full((128, TS), NEG, f)
    sb[:TS] = np.where((tb[:, None] == tb[None, :]) & (tt[None, :] >= tt[:, None]), 0, NEG)
    c["samebatch"] = sb
    c["inbatch"] = np.tile((np.arange(NB)[:, None] == tb[None, :]).astype(f)[None], (128, 1, 1))
    it = np.zeros((128, NB), f)
    it[:TS] = tb[:, None] == np.arange(NB)[None, :]
    c["inbatchT"] = it
    lt = np.zeros((128, NB), f)
    lt[:TS] = (tb[:, None] == np.arange(NB)[None, :]) & (tt[:, None] == NT - 1)
    c["lastT"] = lt
    return [np.ascontiguousarray(c[n].reshape(128, -1), dtype=f) for n in _NAMES + _SEQ_NAMES]


_WIDTHS = [a.shape[1] for a in shape_constants()][:len(_NAMES)]


def trunk_program(nc, A, O):
    F = mybir.dt.float32
    FR = mybir.dt.float32r
    I32 = mybir.dt.int32
    ACT = mybir.ActivationFunctionType
    ALU = mybir.AluOpType
    X = mybir.AxisListType.X
    (y_p, y_s, p_cmp, p_sel, p_win, p_C, p_n, p_m, p_conv,
     s_cmp, s_sel, s_win, s_C, s_n, s_m, s_conv) = O
    ctx = ExitStack()
    with ctx:
        def sb(name, shape, dt=F):
            return ctx.enter_context(nc.sbuf_tensor(name, shape, dt))

        rounded = {}

        def sb_both(name, shape):
            t = sb(name, shape)
            n = 4 * int(np.prod(shape[1:]))
            rounded[name] = nc.alloc_sbuf_tensor_at(name + "_r", shape, FR, offset=nc.sbuf_base - n)
            return t

        def fr(a):
            return bass.AP(tensor=rounded[a.tensor.name], offset=a.offset, ap=a.ap)

        cst = sb("shape_constants", [128, sum(_WIDTHS)])
        at, K = 0, {}
        for n, w in zip(_NAMES, _WIDTHS):
            K[n] = cst[:, at:at + w]
            at += w
        ident, ones = K["ident"], K["ones"]

        def view(name, pattern, **kw):
            return K[name].rearrange(pattern, **kw)

        cos, sin = view("cos", "p (t d) -> p t d", t=5), view("sin", "p (t d) -> p t d", t=5)
        xT = sb("xT", [128, KC, TT])
        xnT = sb_both("xnT", [128, KC, TT])
        NSLAB = 3
        slab = [sb_both(f"slab{i}", [128, 4096]) for i in range(NSLAB)]
        big = sb_both("big", [128, 12288])
        proj = big[:, 0:PT_ * IN_W].rearrange("p (t n) -> p t n", t=PT_)
        side = sb_both("side", [128, IN_W])
        proj_s = side[0:TS, :]
        work = sb_both("work", [128, 10496])
        cT = sb("cT", [128, KC, 32])
        modT = sb("modT", [128, 48, 9])
        scale_n = sb("scale_n", [128, KC, 9])
        colsA = sb("colsA", [128, 64])
        colsB = sb("colsB", [128, 96])
        rows_bc = sb("rows_bc", [128, 512 + 8])
        rstd = sb("rstd", [128, TT])
        gates = sb("gates", [128, PT_, 24])
        gates_s = sb("gates_s", [TS, 24])
        aTs = sb("aTs", [128, 4, TS])
        RT = sb("RT", [128, 5, 4, MH])
        ybuf = big[:, 0:5120].rearrange("p (n d) -> p n d", n=10)
        pages_sb = sb("pages_sb", [1, NB * NPG], I32)
        seqc = work[0:MH, 9216:9216 + 2 * TT].rearrange("p (a n) -> p a n", a=2)
        ps = [ctx.enter_context(nc.psum_tensor(f"ps{i}", [128, 512], F)) for i in range(8)]

        class carve:
            def __init__(self, region):
                self.r, self.at = region, 0

            def __call__(self, *shape):
                n = int(np.prod(shape))
                a = self.r[:, self.at:self.at + n]
                self.at += n
                assert self.at <= self.r.shape[1], (self.at, self.r.shape)
                if len(shape) == 1:
                    return a
                names = "abcd"[:len(shape)]
                return a.rearrange(f"p ({' '.join(names)}) -> p {' '.join(names)}",
                                   **{names[i]: shape[i] for i in range(1, len(shape))})

        w = carve(work)
        modp, rowsA, rowsB = w(NSLAB, 512), w(128), w(128)
        crow, crow2 = w(D), w(D)
        xrow = w(4, D)
        w = carve(work)
        sq = w(2, TT)
        w = carve(work)
        hiXi = w(KC, TT)
        hiW = (w(4096), slab[2][:, :])
        w = carve(work)
        mqk = w(8, SEQ)
        kw = w(PT_, MH * DK)
        E, W = w(1280), w(1280)
        Cp = w(MH, DV + 1)
        hden, hvar = w(4), w(16)
        rope_t = w(4, 256)
        rr = xnT[0:MH, :, :]
        row8 = big[0:MH, PT_ * IN_W:PT_ * IN_W + TT]
        negG_s = sb("neg_g_decode", [MH, TS])
        m0s = sb("m0s", [MH, NB])
        mqks = sb("mqks", [64, 8, TS])
        w = carve(work)
        TH = w(12, SEQ)
        qs, Pb, PTb = w(2, SEQ), w(2, SEQ), w(2, SEQ)
        cS = w(256)
        KmT, VmBD = w(16), w(512)
        sm = w(96)
        gnow = w(PT_, 2, 2)
        nmax, den = w(U), w(U)
        rg = w(2)
        w = carve(work)
        KT = w(2, 1024)
        Ssb, PTs = w(1024 + TS), w(9, 128)
        qTs, Qbd, KN = w(4, TS), w(4, 32), w(2, TS)
        cmb, imp, rownow = w(128), w(96), w(8, TS)
        P4 = imp[:, 32:96]
        small = w(64)
        PTc = w(128)
        KmTd, Vmd = sb("decode_k_means", [128, NB, 16]), sb("decode_v_means", [64, 2, 128])
        paged = lambda a: a.rearrange("p (n c) -> p n c", c=256)
        cpg = [paged(slab[0][:, 2048 * i:2048 * i + 2048]) for i in range(2)]
        spg = [paged((slab[1], slab[2], slab[0], big)[b // 2][:, 2048 * (b % 2):2048 * (b % 2) + 2048]) for b in range(NB)]
        wpg = [paged(big[:, 4096 + 1024 * b:4096 + 1024 * b + 1024]) for b in range(NB)]
        w = carve(big)
        Cst, Cnew = w(NB * MH, DV), w(NB * MH, DV)
        w = carve(work)
        w.at = 10000
        nst, nnew, decayb = w(NB * MH), w(NB * MH), w(NB * MH)
        w = carve(work)
        Qm, kwb, Es, Ws = w(NB, TS), w(NB, DK), w(TS), w(TS)
        hs, hs2, h_small = w(512), w(512), w(32)
        nd = w(DV + 1)
        kws = w(MH * DK)[0:TS, :]
        awl = w(NB, MH)
        gq = sb("gq", [128, 2, 3])
        gq_now = sb("gq_now", [128, 3])
        w = carve(big)
        hiU = w(2, 8, 2, 128)
        hiD = w(4, D)
        hid = w(4, TT)
        convS = w(FC, 16)
        uLast = w(FC, 18)
        cv = w(2, UPW)
        w = carve(side)
        hiH = w(4, TT)
        w = carve(work)
        w.at = 2 * TT
        up = w(2, UPW)
        cwt, cbias, tail_g = w(6), w(2), w(TS)
        hiX = w(KC, TT)
        hiO = [big[:, a:a + 4096].rearrange("p (k n) -> p k n", k=8) for a in (8192, 0)]
        ulrow = w(FF)
        csrow = ulrow

        passed = ctx.enter_context(nc.semaphore("register_waits_passed"))

        def stand_alone(eng):
            eng.sem_inc(passed, 1)

        class Signal:
            def __init__(self, name, per_iter, trips=1, credit=0):
                self.sem = ctx.enter_context(nc.semaphore(name))
                self.name, self.per_iter, self.trips, self.credit = name, per_iter, trips, credit

            def at(self, k, L=0, j=0):
                k = k + self.credit
                assert not isinstance(k, int) or k >= 1, self.name
                return L * (self.per_iter * self.trips) + j * self.per_iter + k

        sig = Signal

        N_FENCE = 15

        stage_done = ctx.enter_context(nc.semaphore("stage_done"))

        def stage_end(n, L):
            return L * (4 * N_FENCE) + 4 * n

        PRO_LOADS = 16 * 6
        pro_silu, pro_ct = ctx.enter_context(nc.semaphore("c_silu")), ctx.enter_context(nc.semaphore("c_transposed"))
        pro_xt = ctx.enter_context(nc.semaphore("x_transposed"))
        pro_copy_p, pro_copy_s = ctx.enter_context(nc.semaphore("x_copied_prompt")), ctx.enter_context(nc.semaphore("x_copied_decode"))
        load_in = ctx.enter_context(nc.semaphore("prologue_loaded"))
        final_sq, final_used = sig("final_squared", KC), sig("final_square_summed", KC)
        final_var, final_sqrt = sig("final_var", 1), sig("final_sqrt", 1)
        final_tr, final_copy, final_xn = sig("final_transposed", 10), sig("final_copied", 10), sig("final_scaled", KC)
        stored = ctx.enter_context(nc.semaphore("outputs_stored"))

        STAGES = [("mod", (4, 4, 4)), ("in", (3, 3, 1)), ("pages", (1, 1, 1)), ("out", (1, 1, 0)), ("ffn", (5, 6, 6))]
        PARTS = {"mod": 1, "in": 1, "pages": 0, "out": 1, "ffn": 2}
        uses, dmas = [0] * NSLAB, [0] * NSLAB
        first_use, first_dma = {}, {}
        for name, n in STAGES:
            for s in range(NSLAB):
                first_use[name, s], first_dma[name, s] = uses[s], dmas[s]
                uses[s] += n[s]
                dmas[s] += PARTS[name] * n[s] if (name, s) != ("in", 2) else 0
        slab_in = [ctx.enter_context(nc.semaphore(f"slab{s}_loaded")) for s in range(NSLAB)]
        slab_out = [ctx.enter_context(nc.semaphore(f"slab{s}_used")) for s in range(NSLAB)]

        def slab_loads(stage, i, L, j=0):
            s, m = i % NSLAB, PARTS[stage]
            return L * (16 * dmas[s]) + j * (16 * m) + 16 * (first_dma[stage, s] + m * (i // NSLAB + 1))


        mod_acc, mod_copy = sig("mod_accumulated", 3, 4), sig("mod_part_copied", 3, 4)
        rows_in = ctx.enter_context(nc.semaphore("layer_rows_loaded"))
        ROWS_PER_LAYER = 16 * 10
        rows_tr = sig("rows_transposed", 1)
        NRM = {}
        for nm in ("n1", "n2"):
            NRM[nm] = dict(sq=sig(nm + "_squared", KC), used=sig(nm + "_square_summed", KC),
                           var=sig(nm + "_var", 1), root=sig(nm + "_sqrt", 1), xr=sig(nm + "_scaled", KC))
        N_IN = 6 * 5
        IN_AT = [i % 2 + NSLAB * (i // 2) for i in range(6)]
        SBANK = (0, 1, 2, 7)
        in_acc = sig("in_accumulated", N_IN)
        in_act, in_dve = sig("in_copied_act", N_IN // 2), sig("in_copied_dve", N_IN // 2)
        if_ready, if_tr = sig("if_gates_ready", 1), sig("if_gates_transposed", 1)
        ml_abs, ml_ln = sig("forget_abs", 1), sig("forget_ln", 1)
        ml_rows, ml_exp, ml_colt = sig("mlstm_rows_ready", 1), sig("mlstm_rows_exp", 1), sig("mlstm_cols_transposed", 1)
        mt_tr, mt_cp = sig("mlstm_heads_transposed", 9), sig("mlstm_heads_copied", 9)
        ml_g, ml_qk = sig("neg_g_spread", MH), sig("mlstm_qk", MH * 4)
        ml_diag, ml_E, ml_W = sig("mlstm_diag_masked", MH), sig("mlstm_decay_ready", MH * 4), sig("mlstm_w_ready", MH * 4)
        ml_num, ml_numc = sig("mlstm_num", MH), sig("mlstm_num_copied", MH)
        ml_kw, k_scaled, roped = sig("mlstm_kw_ready", 1), sig("mlstm_k_scaled", 1), sig("roped", 1)
        h_var, h_root = sig("head_var", 1), sig("head_sqrt", 1)
        hs_var, hs_root = sig("dec_head_var", 1), sig("dec_head_sqrt", 1)
        ms_kq, ms_q = sig("dec_keys_weighted", 1), sig("dec_q_spread", MH)
        ml_Cc = sig("mlstm_state_copied", MH)
        th_tr, th_act, th_dve = sig("heads_transposed", 12), sig("heads_copied_act", 6), sig("heads_copied_dve", 6)
        cm_mean, cm_meanc = sig("block_means", 1), sig("block_means_copied", 1)
        cm_s, cm_sub, cm_exp, cm_p = sig("cmp_scores", 1), sig("cmp_shifted", 1), sig("cmp_exp", 1), sig("cmp_probs", 1)
        cm_t, cm_tc, cm_o = sig("cmp_probs_transposed", 1), sig("cmp_probsT_copied", 1), sig("cmp_out", 1)
        q_stage, g_stage = sig("q_staged", 1, 4), sig("gates_staged", 1, 4)
        a_s, a_max, a_exp = sig("attn_scores", U, 4), sig("attn_max", U, 4), sig("attn_exp", U, 4)
        a_t, a_tc, a_pv, a_acc = (sig("attn_probs_transposed", U, 4), sig("attn_probsT_copied", U, 4),
                                  sig("attn_pv", U, 4), sig("attn_added", U, 4))
        mx_t, mx_c = sig("mix_transposed", 8), sig("mix_copied", 8)
        d_pair = sig("dec_q_paired", 1)
        d_tr = sig("dec_heads_transposed", 1)
        cpg_in = [ctx.enter_context(nc.semaphore(f"cmp_pages{s}_loaded")) for s in range(2)]
        spg_in = [ctx.enter_context(nc.semaphore(f"sel_pages{g}_loaded")) for g in range(NB // 2)]
        wpg_in = [ctx.enter_context(nc.semaphore(f"win_rows{j}_loaded")) for j in range(2)]
        d_cm = sig("dec_means", NB)
        d_q = sig("dec_q_ready", 1, 2)
        d_cs = sig("dec_cmp_scores", 1, 2)
        d_csub, d_cexp, d_cp = sig("dec_cmp_shifted", 1, 2), sig("dec_cmp_exp", 1, 2), sig("dec_cmp_probs", 1, 2)
        d_imp = sig("dec_importance", 1, 2)
        d_ct, d_ctc, d_co = sig("dec_cmp_probs_transposed", 1, 2), sig("dec_cmp_probsT_copied", 1, 2), sig("dec_cmp_out", 1, 2)
        d_kt, d_ktc = sig("dec_k_transposed", 12, 2), sig("dec_k_copied", 12, 2)
        d_s, d_max, d_exp = sig("dec_scores", 2, 2), sig("dec_max", 2, 2), sig("dec_exp", 2, 2)
        d_pt, d_ptc, d_pv = sig("dec_probs_transposed", 2, 2), sig("dec_probsT_copied", 2, 2), sig("dec_pv", 2, 2)
        d_cmb, d_out, d_add = sig("dec_combined", 1, 2), sig("dec_out", 1, 2), sig("dec_added", 1, 2)
        st_in = ctx.enter_context(nc.semaphore("decode_state_loaded"))
        ms_g, ms_E, ms_W = sig("dec_neg_g_spread", MH), sig("dec_decay_masked", MH), sig("dec_decay_exp", MH)
        ms_Wd, ms_num, ms_numc = sig("dec_w_ready", MH), sig("dec_num", MH), sig("dec_num_copied", MH)
        ms_C, ms_Cc = sig("dec_state", MH * 2), sig("dec_state_copied", MH * 2)
        ms_dec = sig("dec_decay_spread", 1)
        ms_t = sig("dec_mix_transposed", 1)
        o_acc, o_add = sig("out_accumulated", 8), sig("out_added", 8)
        cv_in, cv_t = ctx.enter_context(nc.semaphore("conv_history_loaded")), sig("history_transposed", 1)
        NG = 5
        u_acc, g_acc, u_cp = sig("u_accumulated", FC), sig("gate_accumulated", FC), sig("u_copied", FC)
        u_cv, u_si, u_h = sig("conv_done", FC, credit=2), sig("silu_done", FC), sig("hidden_done", FC, credit=1)
        w_hi, w_lo, h_hi, h_lo = sig("up_w_high", FC), sig("up_w_low", FC), sig("hidden_high", FC), sig("hidden_low", FC)
        x_hi, x_lo = sig("inputs_high", 3 * KC), sig("inputs_low", 3 * KC)
        d_hi, d_lo = sig("weights_high", 6 + 2 + 2 * (NG + 1)), sig("weights_low", 6 + 2 + 2 * (NG + 1))
        y_acc, y_add = sig("down_accumulated", 8 * (NG + 1)), sig("down_added", 8 * (NG + 1), credit=2)
        ul_t, ul_c = sig("tail_transposed", FC), sig("tail_copied", FC)

        block = ctx.enter_context(nc.Block())

        @block.sync
        def _(sp):
            wmod = A["w_mod"].rearrange("l (k p) n -> l p k n", p=128)
            win = A["w_in"].rearrange("l (k p) n -> l p k n", p=128)
            wout = A["w_out"].rearrange("l (k p) n -> l p k n", p=128)
            wup = A["w_up"].rearrange("l (k p) (h n) -> l p k h n", p=128, h=2)
            wdn = A["w_down"].rearrange("l (k p) n -> l p k n", p=128)

            sp.wait_ge(load_in, PRO_LOADS)
            flat = lambda a: a.rearrange("l n p a k d -> (l n) p (a k d)")
            cmp_pool, sel_pool = flat(A["cache_cmp_kv"]), flat(A["cache_sel_kv"])

            with sp.Fori(0, DEPTH) as L:
                def pages(dst, src, b, sem):
                    for p in range(NPG):
                        pg = sp.value_load(pages_sb[0:1, NPG * b + p:NPG * b + p + 1], min_val=0, max_val=N_PHYS - 1)
                        sp.dma_start(dst[:, p, :], src[bass.ds(pg + L * N_PHYS, 1)].squeeze(0)).then_inc(sem, 16)

                def load(stage, i, copies, j=0):
                    s = i % NSLAB
                    sp.wait_ge(slab_out[s], L * uses[s] + j + (first_use[stage, s] + i // NSLAB) + 1)
                    for dst, src in copies:
                        sp.dma_start(dst, src).then_inc(slab_in[s], 16)

                def sl(i, n, wd):
                    return slab[i % NSLAB][:, 0:n * wd].rearrange("p (k n) -> p k n", k=n)

                with sp.Fori(0, 4) as j:
                    for i in range(3):
                        load("mod", i, [(sl(i, 8, 512), wmod[L, :, :, bass.ds(j * 1536 + 512 * i, 512)])], j)
                for i, (c0, cw) in enumerate(IN_SLABS):
                    load("in", IN_AT[i], [(sl(IN_AT[i], 8, cw), win[L, :, :, c0:c0 + cw])])
                for b in range(NB):
                    if b in (0, 2, 4):
                        load("pages", b // 2, [])
                        stand_alone(sp)
                    if b in (2, 4):
                        for bb in (b - 2, b - 1):
                            pages(spg[bb], sel_pool, bb, spg_in[bb // 2])
                    if b >= 2:
                        sp.wait_ge(d_cm.sem, d_cm.at(b - 1, L))
                        stand_alone(sp)
                    pages(cpg[b % 2], cmp_pool, b, cpg_in[b % 2])
                for b in (4, 5):
                    sp.wait_ge(d_cm.sem, d_cm.at(b + 3, L))
                    stand_alone(sp)
                    pages(spg[b], sel_pool, b, spg_in[b // 2])
                sp.wait_ge(mx_t.sem, mx_t.at(8, L))
                stand_alone(sp)
                for b in (6, 7):
                    pages(spg[b], sel_pool, b, spg_in[b // 2])
                for i in range(2):
                    load("out", i, [(sl(i, 8, 512), wout[L, :, :, 512 * i:512 * i + 512])])
                def up_copies(c, q):
                    dst = slab[(2, 0)[c]][:, :]
                    dst = dst.rearrange("p (k h n) -> p k h n", k=8, h=2)
                    return [(dst[:, :, h, :], wup[L, :, :, h, q]) for h in range(2)]

                def down_copies(row, n):
                    dst = slab[1][:, 0:2 * n * D].rearrange("p (k n) -> p k n", n=D)
                    return [(dst[:, n * i:n * i + n, :], wdn[L, :, row(n * i), :]) for i in range(2)]

                load("ffn", 2, up_copies(0, slice(0, 256)))
                with sp.Fori(0, NG) as j:
                    load("ffn", 0, up_copies(1, bass.ds(j * 512 + 256, 256)), j)
                    load("ffn", 1, down_copies(lambda k: bass.ds(j * 4 + k, 2), 2), j)
                    load("ffn", 5, up_copies(0, bass.ds(j * 512 + 512, 256)), j)
                load("ffn", 16, down_copies(lambda k: slice(4 * NG + k, 4 * NG + k + 1), 1))

        @block.tensor
        def _(pe):
            mm, tr = nc.tensor.matmul, nc.tensor.transpose

            def idn(n):
                return ident[0:n, 0:n]

            for s in range(NSLAB):
                pe.sem_inc(slab_out[s], 1)
            pe.wait_ge(load_in, PRO_LOADS)
            pe.wait_ge(pro_silu, 1)
            for k in range(KC):
                ins = tr(ps[7][:, 9 * k:9 * k + 9], crow[0:9, 128 * k:128 * k + 128], idn(9))
            ins.then_inc(pro_ct, 1)
            for k in range(KC):
                if k >= 3:
                    pe.wait_ge(pro_copy_p, k - 2)
                    pe.wait_ge(pro_copy_s, k - 2)
                for t in range(PT_):
                    tr(ps[2 * (k % 3)][:, 128 * t:128 * t + 128], xrow[:, t, 128 * k:128 * k + 128], ident)
                tr(ps[2 * (k % 3) + 1][:, 0:TS], crow2[0:TS, 128 * k:128 * k + 128], idn(TS)).then_inc(pro_xt, 1)

            def norm_sums(S, L=0, frees=None):
                for k in range(KC):
                    pe.wait_ge(S["sq"].sem, S["sq"].at(k + 1, L))
                    for b in range(2):
                        ins = mm(ps[b][:, 0:HALF], ones, sq[:, k % 2, HALF * b:HALF * b + HALF],
                                 start=k == 0, stop=k == KC - 1)
                        if frees is not None and k == 0 and b == 0:
                            ins.then_inc(slab_out[frees], 1)
                    ins.then_inc(S["used"].sem, 1)

            with pe.Fori(0, DEPTH) as L:
                pe.drain().then_inc(stage_done, 1)
                pe.wait_ge(stage_done, stage_end(1, L))
                stand_alone(pe)
                pe.wait_ge(rows_in, L * ROWS_PER_LAYER + ROWS_PER_LAYER)
                stand_alone(pe)
                tr(ps[6][:, 0:64], rowsA[0:64, :], idn(64))
                tr(ps[6][:, 64:160], rowsB[0:96, :], idn(96)).then_inc(rows_tr.sem, 1)
                sel9 = K["sum32"][:, 0:9]
                with pe.Fori(0, 4) as j:
                    def part(i):
                        pe.wait_ge(slab_in[i % NSLAB], slab_loads("mod", i, L, j))
                        wv = slab[i][:, :].rearrange("p (k n) -> p k n", k=8)
                        for r in range(2):
                            for q in range(4):
                                k = 4 * r + q
                                ins = mm(ps[i][32 * q:32 * q + 32, :], cT[:, k, :], wv[:, k, :], start=r == 0,
                                         stop=r == 1, tile_position=(0, 32 * q), skip_group_check=True)
                                if k == 0 and i == 1:
                                    ins.then_inc(slab_out[0], 1)
                        ins.then_inc(mod_acc.sem, 1)

                    def gather(i):
                        pe.wait_ge(mod_copy.sem, mod_copy.at(i + 1, L, j))
                        for c in range(4):
                            ins = mm(ps[7][:, bass.ds(j * 108 + 36 * i + 9 * c, 9)], modp[:, i, 128 * c:128 * c + 128],
                                     sel9, start=True, stop=True)
                        if i < 2:
                            ins.then_inc(slab_out[i + 1], 1)
                    part(0)
                    part(1)
                    gather(0)
                    part(2)
                    gather(1)
                    gather(2)
                pe.drain().then_inc(stage_done, 1)
                pe.wait_ge(stage_done, stage_end(2, L))
                stand_alone(pe)
                norm_sums(NRM["n1"], L)
                pe.drain().then_inc(stage_done, 1)
                pe.wait_ge(stage_done, stage_end(3, L))
                stand_alone(pe)
                def bank_free(n):
                    if n >= 8:
                        m = n - 8
                        copied = in_act if m % 2 == 0 else in_dve
                        pe.wait_ge(copied.sem, copied.at(m // 2 + 1, L))

                for i, (c0, cw) in enumerate(IN_SLABS):
                    pe.wait_ge(d_lo.sem, d_lo.at(i + 1, L))
                    wl = slab[i % 2][:, 0:8 * cw].rearrange("p (k n) -> p k n", k=8)
                    wh = hiW[i % 2][:, 0:8 * cw].rearrange("p (k n) -> p k n", k=8)
                    for t in range(5):
                        n = 5 * i + t
                        bank_free(n)
                        M = 128 if t < 4 else TS
                        for k in range(KC):
                            if n == 0:
                                pe.wait_ge(x_lo.sem, x_lo.at(k + 1, L))
                            xh, xl = [fr(x[:, k, 128 * t:128 * t + M]) for x in (hiXi, xnT)]
                            for m, (x, wt) in enumerate(((xh, wh), (xh, wl), (xl, wh))):
                                ins = mm(ps[n % 8][0:M, 0:cw], x, fr(wt[:, k, :]), start=k == 0 and m == 0,
                                         stop=k == KC - 1 and m == 2)
                                if i and t == 0 and k == 0 and m == 0:
                                    ins.then_inc(slab_out[(i - 1) % 2], 1)
                        ins.then_inc(in_acc.sem, 1)
                pe.drain().then_inc(stage_done, 1)
                pe.wait_ge(stage_done, stage_end(4, L))
                stand_alone(pe)
                def block_means(b):
                    pe.wait_ge(cpg_in[b % 2], L * (4 * 16 * NPG) + 16 * NPG * (b // 2 + 1))
                    for p in range(NPG):
                        mm(ps[6][:, 16 * b + 2 * p:16 * b + 2 * p + 2], cpg[b % 2][:, p, 0:128], K["ind2"], start=True, stop=True)
                    for p in range(NPG):
                        r = 16 * (b % 4) + 2 * p
                        ins = mm(ps[7][0:64, 256 + 128 * (b // 4):384 + 128 * (b // 4)], K["slide"][:, 62 - r:126 - r],
                                 cpg[b % 2][:, p, 128:256], start=b % 4 == 0 and p == 0, stop=b % 4 == 3 and p == NPG - 1)
                    ins.then_inc(d_cm.sem, 1)

                pe.wait_ge(if_ready.sem, if_ready.at(1, L))
                for half in range(2):
                    c = C_IF + MH * half
                    for t in range(PT_):
                        ins = tr(ps[half][0:MH, 128 * t:128 * t + 128], proj[:, t, c:c + MH], ident)
                        if half == 0 and t < 2:
                            ins.then_inc(slab_out[1 + t], 1)
                    ins = tr(ps[2][0:MH, 32 * half:32 * half + TS], proj_s[:, c:c + MH], idn(TS))
                ins.then_inc(if_tr.sem, 1)
                pe.wait_ge(k_scaled.sem, k_scaled.at(1, L))
                stand_alone(pe)
                for n in range(8):
                    c = (C_MQ if n < 4 else C_MK) + DK * (n % 4)
                    b = 4 + n % 2
                    if n >= 2:
                        pe.wait_ge(mt_cp.sem, mt_cp.at(n - 1, L))
                        stand_alone(pe)
                    for t in range(PT_):
                        ins = tr(ps[b][0:64, 128 * t:128 * t + 128], proj[:, t, c:c + DK], ident)
                    ins.then_inc(mt_tr.sem, 1)
                pe.wait_ge(mt_cp.sem, mt_cp.at(7, L))
                stand_alone(pe)
                for n in range(8):
                    c = (C_MQ if n < 4 else C_MK) + DK * (n % 4)
                    ins = tr(ps[4][0:64, TS * n:TS * n + TS], proj_s[:, c:c + DK], idn(TS))
                ins.then_inc(mt_tr.sem, 1)
                block_means(0)
                block_means(1)
                pe.wait_ge(ml_exp.sem, ml_exp.at(1, L))
                stand_alone(pe)
                for t in range(5):
                    M = 128 if t < 4 else TS
                    for q in range(4):
                        ins = tr(ps[3][0:M, 16 * t + 4 * q:16 * t + 4 * q + 4], rr[:, q, 128 * t:128 * t + M], idn(MH))
                ins.then_inc(ml_colt.sem, 1)
                pe.drain().then_inc(stage_done, 1)
                pe.wait_ge(stage_done, stage_end(5, L))
                stand_alone(pe)
                pe.wait_ge(ml_kw.sem, ml_kw.at(1, L))
                for h in range(MH):
                    if h:
                        pe.wait_ge(ml_E.sem, ml_E.at(4 * h, L))
                    mm(ps[0][:, :], view("onehot", "p (h n) -> p h n", h=MH)[0:MH, h, :], rr[:, 7, 0:SEQ],
                                start=True, stop=True).then_inc(ml_g.sem, 1)
                    for i in range(PT_):
                        n = 128 * (PT_ - i)
                        if h * 4 + i >= 2:
                            pe.wait_ge(ml_W.sem, ml_W.at(h * 4 + i - 1, L))
                        mm(ps[1 + i % 2][:, 0:n], mqk[0:64, 4 + h, 128 * i:128 * i + 128],
                                     mqk[0:64, h, 128 * i:SEQ], start=True, stop=True).then_inc(ml_qk.sem, 1)
                    if h:
                        block_means(2 * h)
                    pe.wait_ge(ml_W.sem, ml_W.at(4 * h + 4, L))
                    if h:
                        pe.wait_ge(ml_numc.sem, ml_numc.at(h, L))
                        pe.wait_ge(ml_Cc.sem, ml_Cc.at(h, L))
                    wo = [0, 512, 896, 1152]
                    for t in range(PT_):
                        for i in range(t + 1):
                            mm(ps[3][:, 128 * t:128 * t + 128], W[:, wo[i] + 128 * (t - i):wo[i] + 128 * (t - i) + 128],
                               proj[:, i, C_MV + DV * h:C_MV + DV * h + DV], start=i == 0, stop=i == t)
                        for i in range(t + 1):
                            ins = mm(ps[4][:, t:t + 1], W[:, wo[i] + 128 * (t - i):wo[i] + 128 * (t - i) + 128],
                                     ones[:, 0:1], start=i == 0, stop=i == t)
                    for i in range(PT_):
                        kh = kw[:, i, DK * h:DK * h + DK]
                        mm(ps[5][0:64, 0:DV], kh, proj[:, i, C_MV + DV * h:C_MV + DV * h + DV],
                           start=i == 0, stop=i == PT_ - 1)
                    for i in range(PT_):
                        ins = mm(ps[5][0:64, DV:DV + 1], kw[:, i, DK * h:DK * h + DK], ones[:, 0:1],
                                 start=i == 0, stop=i == PT_ - 1)
                    ins.then_inc(ml_num.sem, 1)
                    if h:
                        block_means(2 * h + 1)
                pe.drain().then_inc(stage_done, 1)
                pe.wait_ge(stage_done, stage_end(6, L))
                stand_alone(pe)
                for n in range(12):
                    c = C_Q + HD * n if n < 8 else (C_KS if n < 10 else C_KW) + HD * (n % 2)
                    b = n % 4
                    if n >= 4:
                        m = n - 4
                        copied = th_act if m % 2 == 0 else th_dve
                        pe.wait_ge(copied.sem, copied.at(m // 2 + 1, L))
                        stand_alone(pe)
                    for t in range(PT_):
                        ins = tr(ps[b][0:64, 128 * t:128 * t + 128], proj[:, t, c:c + HD], ident)
                    ins.then_inc(th_tr.sem, 1)
                ind8, ind64 = view("ind8", "p (t n) -> p t n", t=4), view("ind64", "p (t n) -> p t n", t=4)
                for kv in range(KV):
                    for t in range(PT_):
                        mm(ps[4][0:64, 8 * kv:8 * kv + 8], proj[:, t, C_KC + HD * kv:C_KC + HD * kv + HD], ind8[:, t, :],
                           start=t == 0, stop=t == PT_ - 1)
                for t in range(PT_):
                    ins = mm(ps[5][0:64, 0:128], ind64[:, t, :], proj[:, t, C_KC + 128:C_KC + 256],
                             start=t == 0, stop=t == PT_ - 1)
                ins.then_inc(cm_mean.sem, 1)
                pe.wait_ge(cm_meanc.sem, cm_meanc.at(1, L))
                pe.wait_ge(th_act.sem, th_act.at(6, L))
                pe.wait_ge(th_dve.sem, th_dve.at(6, L))
                for t in range(PT_):
                    for h in range(AH):
                        ins = mm(ps[6][:, 64 * t + 8 * h:64 * t + 8 * h + 8], TH[0:64, h, 128 * t:128 * t + 128],
                                 KmT[0:64, 8 * (h // AG):8 * (h // AG) + 8], start=True, stop=True)
                ins.then_inc(cm_s.sem, 1)
                pe.wait_ge(cm_p.sem, cm_p.at(1, L))
                stand_alone(pe)
                for t in range(PT_):
                    ins = tr(ps[7][0:64, 128 * t:128 * t + 128], cS[:, 64 * t:64 * t + 64], ident)
                ins.then_inc(cm_t.sem, 1)
                pe.wait_ge(cm_tc.sem, cm_tc.at(1, L))
                for t in range(PT_):
                    ins = mm(ps[t][:, :], PTb[0:64, 0, 128 * t:128 * t + 128], VmBD[0:64, :], start=True, stop=True)
                ins.then_inc(cm_o.sem, 1)
                pe.drain().then_inc(stage_done, 1)
                pe.wait_ge(stage_done, stage_end(7, L))
                stand_alone(pe)
                with pe.Fori(0, 4) as j:
                    units = [(hh, br, t) for hh in range(2) for br in range(2) for t in range(PT_)]

                    def scores(u):
                        hh, br, t = units[u]
                        mm(ps[SBANK[u % 4]][:, 0:128 * t + 128], qs[0:64, hh, 128 * t:128 * t + 128],
                                   TH[0:64, 8 + 2 * br + hh, 0:128 * t + 128], start=True, stop=True).then_inc(a_s.sem, 1)

                    def turn(u):
                        t = units[u][2]
                        pe.wait_ge(a_exp.sem, a_exp.at(u + 1, L, j))
                        for i in range(t + 1):
                            ins = tr(ps[3 + u % 2][:, 128 * i:128 * i + 128], Pb[:, u % 2, 128 * i:128 * i + 128], ident)
                        ins.then_inc(a_t.sem, 1)

                    def values(u):
                        hh, br, t = units[u]
                        pe.wait_ge(a_tc.sem, a_tc.at(u + 1, L, j))
                        if u >= 2:
                            pe.wait_ge(a_acc.sem, a_acc.at(u - 1, L, j))
                        c = (C_KS, C_KW)[br] + 128 + HD * hh
                        for i in range(t + 1):
                            ins = mm(ps[5 + u % 2][:, 0:HD], PTb[:, u % 2, 128 * i:128 * i + 128], proj[:, i, c:c + HD],
                                     start=i == 0, stop=i == t)
                        ins.then_inc(a_pv.sem, 1)

                    pe.wait_ge(q_stage.sem, q_stage.at(1, L, j))
                    pe.wait_ge(g_stage.sem, g_stage.at(1, L, j))
                    scores(0)
                    scores(1)
                    scores(2)
                    for u in range(U):
                        turn(u)
                        if u + 3 < U:
                            scores(u + 3)
                        if u >= 1:
                            values(u - 1)
                    values(U - 1)
                pe.drain().then_inc(stage_done, 1)
                pe.wait_ge(stage_done, stage_end(8, L))
                stand_alone(pe)
                for n in range(8):
                    c = C_Q + 128 * n if n < 4 else C_MO + 128 * (n - 4)
                    if n >= 4:
                        pe.wait_ge(mx_c.sem, mx_c.at(n - 3, L))
                    for t in range(PT_):
                        ins = tr(ps[n % 4][:, 128 * t:128 * t + 128], proj[:, t, c:c + 128], ident)
                    ins.then_inc(mx_t.sem, 1)
                pe.wait_ge(d_pair.sem, d_pair.at(1, L))
                stand_alone(pe)
                for g in range(AG):
                    tr(ps[4][:, TS * g:TS * g + TS],
                       Ssb[0:TS, 128 * g:128 * g + 128], idn(TS))
                for b_, c in enumerate((C_KS, C_KW)):
                    tr(ps[4][:, 128 + TS * b_:128 + TS * b_ + TS], proj_s[:, c:c + 128], idn(TS))
                for g in range(2):
                    ins = mm(ps[5][:, 24 * g:24 * g + 24], view("tokrow", "p (g n) -> p g n", g=2)[0:TS, g, :], gates_s[:, :],
                             start=True, stop=True)
                ins.then_inc(d_tr.sem, 1)
                pe.drain().then_inc(stage_done, 1)
                pe.wait_ge(stage_done, stage_end(9, L))
                stand_alone(pe)
                for j in range(2):
                    pe.wait_ge(d_q.sem, d_q.at(1, L, j))
                    for b in range(4):
                        ins = mm(ps[4][32 * b:32 * b + 32, 0:16], Qbd[:, b, :], KmTd[:, 4 * j + b, :], start=True, stop=True,
                                 tile_position=(0, 32 * b), skip_group_check=True)
                    ins.then_inc(d_cs.sem, 1)
                    nkt = 0
                    for br in range(2):
                        for b in range(4):
                            kv_ = (spg, wpg)[br][4 * j + b]
                            if br == 0 and b % 2 == 0:
                                pe.wait_ge(spg_in[2 * j + b // 2], L * (32 * NPG) + 32 * NPG)
                            if br == 1 and b == 0:
                                pe.wait_ge(wpg_in[j], L * 64 + 64)
                            for half in range(2 - br):
                                if nkt >= 2:
                                    pe.wait_ge(d_ktc.sem, d_ktc.at(nkt - 1, L, j))
                                for i in range(4):
                                    src = kv_[:, 4 * half + i, 0:128]
                                    ins = tr(ps[nkt % 2][:, 128 * i:128 * i + 128], src, ident)
                                    if br == 1 and b == 0 and i < 2 - j:
                                        ins.then_inc(slab_out[0 if j else 1 + i], 1)
                                ins.then_inc(d_kt.sem, 1)
                                nkt += 1
                            for half in range(2 - br):
                                pe.wait_ge(d_ktc.sem, d_ktc.at(nkt - (1 - br) + half, L, j))
                                if br == 1 and b == 0:
                                    pe.wait_ge(d_max.sem, d_max.at(1, L, j))
                                mm(ps[5 + half][32 * b:32 * b + 32, :], Qbd[:, b, :], KT[:, b % 2, 512 * half:512 * half + 512],
                                   start=True, stop=True, tile_position=(0, 32 * b), skip_group_check=True)
                            ins = mm(ps[7][32 * b:32 * b + 32, 0:TS], Qbd[:, b, :], KN[:, br, :], start=True, stop=True,
                                     tile_position=(0, 32 * b), skip_group_check=True)
                        ins.then_inc(d_s.sem, 1)
                        if br == 0:
                            pe.wait_ge(d_cp.sem, d_cp.at(1, L, j))
                            mm(ps[2][:, 0:16], K["samegroup"], imp[:, 0:16], start=True, stop=True).then_inc(d_imp.sem, 1)
                            tr(ps[3][0:64, 0:128], P4, ident).then_inc(d_ct.sem, 1)
                            pe.wait_ge(d_ctc.sem, d_ctc.at(1, L, j))
                            stand_alone(pe)
                            ins = mm(ps[4][:, 128:256], PTc[0:64, :], Vmd[:, j, :], start=True, stop=True)
                            ins.then_inc(d_co.sem, 1)
                        pe.wait_ge(d_exp.sem, d_exp.at(br + 1, L, j))
                        nt = (8, 4)[br]
                        for i in range(nt):
                            tr(ps[i // 4][:, 128 * (i % 4):128 * (i % 4) + 128], Ssb[:, 128 * i:128 * i + 128], ident)
                        tr(ps[3][0:TS, 128:256], Ssb[:, 128 * nt:128 * nt + TS], ident).then_inc(d_pt.sem, 1)
                        pe.wait_ge(d_ptc.sem, d_ptc.at(br + 1, L, j))
                        cn = (C_KS, C_KW)[br] + 128
                        for i in range(nt + 1):
                            for b in range(4):
                                o_ = ps[4][32 * b:32 * b + 32, 256:384] if br == 0 else ps[2][32 * b:32 * b + 32, 128:256]
                                if i < nt:
                                    lt, rh = PTs[:, i, 32 * b:32 * b + 32], (spg, wpg)[br][4 * j + b][:, i, 128:256]
                                else:
                                    lt, rh = PTs[0:TS, 8, 32 * b:32 * b + 32], proj_s[:, cn:cn + 128]
                                ins = mm(o_, lt, rh, start=i == 0, stop=i == nt, tile_position=(0, 32 * b),
                                         skip_group_check=True)
                        ins.then_inc(d_pv.sem, 1)
                    pe.wait_ge(d_cmb.sem, d_cmb.at(1, L, j))
                    for h in range(AH):
                        kv = h // AG
                        q = 64 * (h % 2)
                        ins = mm(ps[3][q:q + 64, 256 + TS * (h // 2):256 + TS * (h // 2) + TS], cmb[:, 64 * kv:64 * kv + 64],
                                 rownow[:, h, :], start=True, stop=True, tile_position=(0, q), skip_group_check=True)
                    ins.then_inc(d_out.sem, 1)
                    pe.wait_ge(d_add.sem, d_add.at(1, L, j))
                    stand_alone(pe)
                pe.drain().then_inc(stage_done, 1)
                pe.wait_ge(stage_done, stage_end(10, L))
                stand_alone(pe)
                oh = view("onehot", "p (h n) -> p h n", h=MH)
                pe.wait_ge(st_in, L * (16 * 2) + 32)
                pe.wait_ge(ms_kq.sem, ms_kq.at(1, L))
                stand_alone(pe)
                mm(ps[6][0:64, 0:NB * MH], ones[0:TS, 0:64], awl[0:TS, :, :].rearrange("p b h -> p (b h)"),
                              start=True, stop=True).then_inc(ms_dec.sem, 1)
                for h in range(MH):
                    if h:
                        pe.wait_ge(ms_numc.sem, ms_numc.at(h, L))
                        pe.wait_ge(ms_W.sem, ms_W.at(h, L))
                        stand_alone(pe)
                    mm(ps[1][0:TS, 0:TS], mqks[:, 4 + h, :], mqks[:, h, :], start=True, stop=True)
                    mm(ps[0][0:TS, 0:TS], oh[0:MH, h, 0:TS], negG_s[:, :], start=True, stop=True).then_inc(ms_g.sem, 1)
                    pe.wait_ge(ms_Wd.sem, ms_Wd.at(h + 1, L))
                    stand_alone(pe)
                    v = proj_s[:, C_MV + DV * h:C_MV + DV * h + DV]
                    mm(ps[2][0:TS, 0:DV], Ws[0:TS, :], v, start=True, stop=True)
                    mm(ps[2][0:TS, DV:DV + 1], Ws[0:TS, :], ones[0:TS, 0:1], start=True, stop=True)
                    pe.wait_ge(ms_q.sem, ms_q.at(h + 1, L))
                    stand_alone(pe)
                    for b in range(NB):
                        mm(ps[3][0:TS, 0:DV], Qm[0:64, b, :], Cst[0:64, b * MH + h, :], start=b == 0, stop=b == NB - 1)
                    for b in range(NB):
                        ins = mm(ps[3][0:TS, DV:DV + 1], Qm[0:64, b, :], nst[0:64, b * MH + h:b * MH + h + 1],
                                 start=b == 0, stop=b == NB - 1)
                    ins.then_inc(ms_num.sem, 1)
                    for half in range(2):
                        if h:
                            pe.wait_ge(ms_Cc.sem, ms_Cc.at(2 * h + half - 1, L))
                            stand_alone(pe)
                        for bb in range(4):
                            b = 4 * half + bb
                            mm(ps[4 + half][0:64, DV * bb:DV * bb + DV], kwb[0:TS, b, :], v, start=True, stop=True)
                            ins = mm(ps[6 + half][0:64, bb:bb + 1], kwb[0:TS, b, :], ones[0:TS, 0:1], start=True, stop=True)
                        ins.then_inc(ms_C.sem, 1)
                pe.drain().then_inc(stage_done, 1)
                pe.wait_ge(stage_done, stage_end(11, L))
                stand_alone(pe)
                for c in range(4):
                    ins = tr(ps[0][:, TS * c:TS * c + TS], hs[0:TS, 128 * c:128 * c + 128], idn(TS))
                ins.then_inc(ms_t.sem, 1)
                pe.drain().then_inc(stage_done, 1)
                pe.wait_ge(stage_done, stage_end(12, L))
                stand_alone(pe)
                for c in range(8):
                    i = c // 4
                    if c % 4 == 0:
                        pe.wait_ge(d_lo.sem, d_lo.at(6 + i + 1, L))
                    if c >= 4:
                        pe.wait_ge(o_add.sem, o_add.at(c - 3, L))
                    cc = 128 * (c % 4)
                    lo = slab[i][:, :].rearrange("p (k n) -> p k n", k=8)
                    for k in range(KC):
                        if c == 0:
                            pe.wait_ge(x_lo.sem, x_lo.at(KC + k + 1, L))
                        wh, wl = fr(hiO[i][:, k, cc:cc + 128]), fr(lo[:, k, cc:cc + 128])
                        for n, (wt, x) in enumerate(((wh, hiX), (wh, xnT), (wl, hiX))):
                            for b in range(2):
                                ins = mm(ps[2 * (c % 4) + b][:, 0:HALF], wt, fr(x[:, k, HALF * b:HALF * b + HALF]),
                                         start=k == 0 and n == 0, stop=k == KC - 1 and n == 2)
                                if c == 4 and k == 0 and n == 0 and b == 0:
                                    ins.then_inc(slab_out[0], 1)
                    ins.then_inc(o_acc.sem, 1)
                pe.drain().then_inc(stage_done, 1)
                pe.wait_ge(stage_done, stage_end(13, L))
                stand_alone(pe)
                norm_sums(NRM["n2"], L, frees=1)
                pe.wait_ge(cv_in, L * 16 + 16)
                stand_alone(pe)
                for c in range(FC):
                    ins = tr(ps[2][:, 16 * c:16 * c + 16], csrow[0:16, 128 * c:128 * c + 128], idn(16))
                ins.then_inc(cv_t.sem, 1)
                pe.drain().then_inc(stage_done, 1)
                pe.wait_ge(stage_done, stage_end(14, L))
                stand_alone(pe)
                def up(q, half, first=False, frees=None):
                    lo = slab[(2, 0)[q // 2]][:, :].rearrange("p (k h n) -> p k h n", k=8, h=2)
                    cc = 128 * (q % 2)
                    for k in range(KC):
                        if first:
                            pe.wait_ge(x_lo.sem, x_lo.at(2 * KC + k + 1, L))
                        wh, wl = fr(hiU[:, q % 2, k, half, :]), fr(lo[:, k, half, cc:cc + 128])
                        for n, (wt, x) in enumerate(((wh, hiX), (wh, xnT), (wl, hiX))):
                            for b in range(2):
                                ins = mm(ps[2 * half + b][:, 0:HALF], wt, fr(x[:, k, HALF * b:HALF * b + HALF]),
                                         start=k == 0 and n == 0, stop=k == KC - 1 and n == 2)
                                if frees is not None and k == 0 and n == 0 and b == 0:
                                    ins.then_inc(slab_out[frees], 1)
                    ins.then_inc((u_acc, g_acc)[half].sem, 1)

                def down(n_k, g=0, frees=None):
                    pe.wait_ge(h_lo.sem, h_lo.at(n_k + 4 * g, L))
                    pe.wait_ge(d_lo.sem, d_lo.at(10 + 2 * g, L))
                    lo = slab[1][:, :].rearrange("p (k n) -> p k n", n=D)
                    for c in range(8):
                        pe.wait_ge(y_add.sem, y_add.at(c - 1 + 8 * g, L))
                        for k in range(n_k):
                            wh, wl = fr(hiD[:, k, 128 * c:128 * c + 128]), fr(lo[:, k, 128 * c:128 * c + 128])
                            for n, (wt, x) in enumerate(((wh, hiH), (wh, hid), (wl, hiH))):
                                for b in range(2):
                                    ins = mm(ps[4 + 2 * (c % 2) + b][:, 0:HALF], wt, fr(x[:, k, HALF * b:HALF * b + HALF]),
                                             start=k == 0 and n == 0, stop=k == n_k - 1 and n == 2)
                                    if frees is not None and c == 0 and k == 0 and n == 0 and b == 0:
                                        ins.then_inc(slab_out[frees], 1)
                        ins.then_inc(y_acc.sem, 1)
                    pe.drain().then_inc(slab_out[1], 1)

                pe.wait_ge(w_lo.sem, w_lo.at(1, L))
                up(0, 0, first=True)
                with pe.Fori(0, NG) as j:
                    for q in range(4):
                        if q:
                            pe.wait_ge(w_lo.sem, w_lo.at(q + 1 + 4 * j, L))
                            pe.wait_ge(u_cp.sem, u_cp.at(q + 4 * j, L))
                            up(q, 0, frees=2 if q == 2 else None)
                        pe.wait_ge(u_h.sem, u_h.at(q + 4 * j, L))
                        up(q, 1)
                    pe.wait_ge(w_lo.sem, w_lo.at(5 + 4 * j, L))
                    pe.wait_ge(u_cp.sem, u_cp.at(4 + 4 * j, L))
                    up(0, 0, frees=0)
                    down(4, j)
                pe.wait_ge(u_h.sem, u_h.at(4 * NG, L))
                up(0, 1)
                pe.wait_ge(w_lo.sem, w_lo.at(FC, L))
                pe.wait_ge(u_cp.sem, u_cp.at(FC - 1, L))
                up(1, 0)
                pe.wait_ge(u_h.sem, u_h.at(FC - 1, L))
                up(1, 1)
                down(2, NG, frees=2)
                for c in range(FC):
                    if c >= 2:
                        pe.wait_ge(ul_c.sem, ul_c.at(c - 1, L))
                    tr(ps[c % 2][0:18, 0:128], uLast[:, c, :], ident).then_inc(ul_t.sem, 1)
                pe.drain().then_inc(stage_done, 1)
                pe.wait_ge(stage_done, stage_end(15, L))
                stand_alone(pe)

            norm_sums(dict(sq=final_sq, used=final_used))
            pe.wait_ge(final_xn.sem, final_xn.at(KC))
            for n in range(10):
                t, hf = n // 2, n % 2
                M = 128 if t < 4 else TS
                if n >= 4:
                    pe.wait_ge(final_copy.sem, final_copy.at(n - 3))
                for k in range(4):
                    ins = tr(ps[4 + n % 4][0:M, 128 * k:128 * k + 128], xnT[:, 4 * hf + k, 128 * t:128 * t + M], ident)
                ins.then_inc(final_tr.sem, 1)

        def bc(ap, axis, n):
            a = ap.unsqueeze(axis)
            shape = list(a.shape)
            shape[axis] = n
            return a.to_broadcast(shape)

        @block.scalar
        def _(act):
            A_ = nc.scalar.activation
            drain = act.drain
            act.wait_ge(load_in, PRO_LOADS)
            A_(crow[0:9, :], crow[0:9, :], ACT.Silu).then_inc(pro_silu, 1)
            for k in range(KC):
                act.wait_ge(pro_xt, k + 1)
                A_(xT[:, k, 0:SEQ], ps[2 * (k % 3)][:, :], ACT.Copy).then_inc(pro_copy_p, 1)

            def norm_act(S, L=0):
                for k in range(KC):
                    if k >= 2:
                        act.wait_ge(S["used"].sem, S["used"].at(k - 1, L))
                    A_(sq[:, k % 2, :], xT[:, k, :], ACT.Square).then_inc(S["sq"].sem, 1)
                act.wait_ge(S["var"].sem, S["var"].at(1, L))
                A_(rstd[:, :], rstd[:, :], ACT.Sqrt).then_inc(S["root"].sem, 1)

            def modulate(S, shift, L):
                for k in range(KC):
                    act.wait_ge(S["xr"].sem, S["xr"].at(k + 1, L))
                    A_(xnT[:, k, 0:SEQ], xnT[:, k, 0:SEQ], ACT.Identity, bias=modT[:, shift + k, 0:1],
                       scale=scale_n[:, k, 0:1])

            with act.Fori(0, DEPTH) as L:
                act.drain().then_inc(stage_done, 1)
                act.wait_ge(stage_done, stage_end(1, L))
                stand_alone(act)
                with act.Fori(0, 4) as j:
                    for i in range(3):
                        act.wait_ge(mod_acc.sem, mod_acc.at(i + 1, L, j))
                        A_(modp[:, i, :], ps[i][:, :], ACT.Copy).then_inc(mod_copy.sem, 1)
                act.drain().then_inc(stage_done, 1)
                act.wait_ge(stage_done, stage_end(2, L))
                stand_alone(act)
                norm_act(NRM["n1"], L)
                modulate(NRM["n1"], 0, L)

                def split_in(i):
                    n = 8 * IN_SLABS[i][1]
                    act.wait_ge(slab_in[i % 2], slab_loads("in", IN_AT[i], L))
                    if i >= 2:
                        act.wait_ge(in_acc.sem, in_acc.at(5 * (i - 1), L))
                    A_(fr(hiW[i % 2][:, 0:n]), slab[i % 2][:, 0:n], ACT.Copy).then_inc(d_hi.sem, 1)

                split_in(0)
                act.drain().then_inc(stage_done, 1)
                act.wait_ge(stage_done, stage_end(3, L))
                stand_alone(act)
                for k in range(KC):
                    A_(fr(hiXi[:, k, :]), xnT[:, k, :], ACT.Copy).then_inc(x_hi.sem, 1)
                for i, (c0, cw) in enumerate(IN_SLABS):
                    if i + 1 < 6:
                        split_in(i + 1)
                    for t in range(5):
                        n = 5 * i + t
                        if n % 2 == 0:
                            M = 128 if t < 4 else TS
                            dst = proj[:, t, c0:c0 + cw] if t < 4 else proj_s[:, c0:c0 + cw]
                            act.wait_ge(in_acc.sem, in_acc.at(n + 1, L))
                            A_(dst, ps[n % 8][0:M, 0:cw], ACT.Copy).then_inc(in_act.sem, 1)
                act.drain().then_inc(stage_done, 1)
                act.wait_ge(stage_done, stage_end(4, L))
                stand_alone(act)
                A_(proj[:, :, C_MK:C_MK + 256], proj[:, :, C_MK:C_MK + 256], ACT.Copy, scale=DK ** -0.5)
                A_(proj_s[:, C_MK:C_MK + 256], proj_s[:, C_MK:C_MK + 256], ACT.Copy, scale=DK ** -0.5).then_inc(k_scaled.sem, 1)
                for n in range(3):
                    act.wait_ge(mt_tr.sem, mt_tr.at(n + 1, L))
                    A_(mqk[0:64, n, :], ps[4 + n % 2][0:64, :], ACT.Copy).then_inc(mt_cp.sem, 1)
                A_(gates[:, :, :], proj[:, :, C_G:C_G + 24], ACT.Sigmoid)
                A_(gates_s[:, :], proj_s[:, C_G:C_G + 24], ACT.Sigmoid)
                A_(proj[:, :, C_MO:C_MO + 512], proj[:, :, C_MO:C_MO + 512], ACT.Sigmoid)
                A_(proj_s[:, C_MO:C_MO + 512], proj_s[:, C_MO:C_MO + 512], ACT.Sigmoid)
                for n in range(3, 9):
                    act.wait_ge(mt_tr.sem, mt_tr.at(n + 1, L))
                    if n < 8:
                        A_(mqk[0:64, n, :], ps[4 + n % 2][0:64, :], ACT.Copy).then_inc(mt_cp.sem, 1)
                    else:
                        A_(mqks[:, :, :].rearrange("p n t -> p (n t)"), ps[4][0:64, 0:256], ACT.Copy).then_inc(mt_cp.sem, 1)
                act.wait_ge(ml_abs.sem, ml_abs.at(1, L))
                A_(rr[:, 5, :], rr[:, 4, :], ACT.Exp, scale=-1.0)
                drain()
                A_(rr[:, 5, :], rr[:, 5, :], ACT.Ln, bias=1.0).then_inc(ml_ln.sem, 1)
                act.wait_ge(ml_rows.sem, ml_rows.at(1, L))
                A_(rr[:, 1, :], rr[:, 1, :], ACT.Exp)
                A_(rr[:, 2, :], rr[:, 2, :], ACT.Exp, scale=-1.0)
                A_(rr[:, 3, :], rr[:, 3, :], ACT.Exp).then_inc(ml_exp.sem, 1)
                act.drain().then_inc(stage_done, 1)
                act.wait_ge(stage_done, stage_end(5, L))
                stand_alone(act)
                wo = [0, 512, 896, 1152]
                for h in range(MH):
                    act.wait_ge(ml_diag.sem, ml_diag.at(h + 1, L))
                    for i in range(PT_):
                        g = RT[:, i, 0, h:h + 1]
                        ins = A_(E[:, wo[i]:wo[i] + 128], E[:, wo[i]:wo[i] + 128], ACT.Exp, bias=g)
                        if i < 3:
                            n = 128 * (3 - i)
                            ins = A_(E[:, wo[i] + 128:wo[i] + 128 + n], ps[0][:, 128 * (i + 1):SEQ], ACT.Exp, bias=g)
                        ins.then_inc(ml_E.sem, 1)
                    act.wait_ge(ml_num.sem, ml_num.at(h + 1, L))
                    A_(Cp[0:64, h, :], ps[5][0:64, 0:DV + 1], ACT.Copy).then_inc(ml_Cc.sem, 1)
                act.wait_ge(d_cm.sem, d_cm.at(NB, L))
                A_(KmTd[:, :, :].rearrange("p b n -> p (b n)"), ps[6][:, 0:128], ACT.Copy)
                A_(Vmd[:, :, :].rearrange("p g d -> p (g d)"), ps[7][0:64, 256:512], ACT.Copy)
                act.wait_ge(h_var.sem, h_var.at(1, L))
                A_(hvar, hvar, ACT.Sqrt).then_inc(h_root.sem, 1)
                act.drain().then_inc(stage_done, 1)
                act.wait_ge(stage_done, stage_end(6, L))
                stand_alone(act)
                for n in range(0, 12, 2):
                    act.wait_ge(th_tr.sem, th_tr.at(n + 1, L))
                    A_(TH[0:64, n, :], ps[n % 4][0:64, :], ACT.Copy, scale=HD ** -0.5 if n < 8 else 1.0).then_inc(th_act.sem, 1)
                act.wait_ge(cm_sub.sem, cm_sub.at(1, L))
                A_(cS, cS, ACT.Exp).then_inc(cm_exp.sem, 1)
                act.wait_ge(cm_o.sem, cm_o.at(1, L))
                for t in range(PT_):
                    A_(proj[:, t, 0:512], ps[t][:, :], ACT.Copy)
                act.drain().then_inc(stage_done, 1)
                act.wait_ge(stage_done, stage_end(7, L))
                stand_alone(act)
                with act.Fori(0, 4) as j:
                    def exp(u):
                        nk = 128 * (u % 4) + 128
                        act.wait_ge(a_max.sem, a_max.at(u + 1, L, j))
                        if u >= 2:
                            act.wait_ge(a_t.sem, a_t.at(u - 1, L, j))
                        A_(Pb[:, u % 2, 0:nk], ps[SBANK[u % 4]][:, 0:nk], ACT.Exp, bias=nmax[:, u:u + 1],
                                     accum_out=den[:, u:u + 1]).then_inc(a_exp.sem, 1)

                    def copy(u):
                        nk = 128 * (u % 4) + 128
                        act.wait_ge(a_t.sem, a_t.at(u + 1, L, j))
                        if u >= 2:
                            act.wait_ge(a_pv.sem, a_pv.at(u - 1, L, j))
                        A_(PTb[:, u % 2, 0:nk], ps[3 + u % 2][:, 0:nk], ACT.Copy).then_inc(a_tc.sem, 1)

                    A_(qs[0:64, 0, :], TH[0:64, bass.ds(j, 1), :].squeeze(1), ACT.Copy)
                    A_(qs[0:64, 1, :], TH[0:64, bass.ds(j + 4, 1), :].squeeze(1), ACT.Copy).then_inc(q_stage.sem, 1)
                    exp(0)
                    for u in range(U):
                        if u + 1 < U:
                            exp(u + 1)
                        copy(u)
                act.drain().then_inc(stage_done, 1)
                act.wait_ge(stage_done, stage_end(8, L))
                stand_alone(act)
                for n in range(8):
                    act.wait_ge(mx_t.sem, mx_t.at(n + 1, L))
                    A_(xnT[:, n, 0:SEQ], ps[n % 4][:, :], ACT.Copy).then_inc(mx_c.sem, 1)
                act.drain().then_inc(stage_done, 1)
                act.wait_ge(stage_done, stage_end(9, L))
                stand_alone(act)
                for j in range(2):
                    act.wait_ge(d_csub.sem, d_csub.at(1, L, j))
                    A_(imp[:, 0:16], ps[4][:, 0:16], ACT.Exp, bias=small[:, 0:1], accum_out=small[:, 1:2]).then_inc(d_cexp.sem, 1)
                    for n in range(8):
                        act.wait_ge(d_kt.sem, d_kt.at(n + 1, L, j))
                        A_(KT[:, n // 2 % 2, 512 * (n % 2):512 * (n % 2) + 512], ps[n % 2][:, :], ACT.Copy).then_inc(d_ktc.sem, 1)
                    act.wait_ge(d_ct.sem, d_ct.at(1, L, j))
                    A_(PTc[0:64, :], ps[3][0:64, 0:128], ACT.Copy).then_inc(d_ctc.sem, 1)
                    for br in range(2):
                        nt = (8, 4)[br]
                        if br == 1:
                            for n in range(8, 12):
                                act.wait_ge(d_kt.sem, d_kt.at(n + 1, L, j))
                                A_(KT[:, n % 2, 0:512], ps[n % 2][:, :], ACT.Copy).then_inc(d_ktc.sem, 1)
                        act.wait_ge(d_max.sem, d_max.at(br + 1, L, j))
                        wd = 128 * nt + TS
                        A_(Ssb[:, 0:wd], Ssb[:, 0:wd], ACT.Exp, bias=small[:, 2 + br:3 + br],
                                     accum_out=small[:, 4 + br:5 + br]).then_inc(d_exp.sem, 1)
                        act.wait_ge(d_pt.sem, d_pt.at(br + 1, L, j))
                        for q in range(nt // 4):
                            A_(PTs[:, 4 * q:4 * q + 4, :].rearrange("p a b -> p (a b)"), ps[q][:, :], ACT.Copy)
                        A_(PTs[0:TS, 8, :], ps[3][0:TS, 128:256], ACT.Copy).then_inc(d_ptc.sem, 1)
                act.drain().then_inc(stage_done, 1)
                act.wait_ge(stage_done, stage_end(10, L))
                stand_alone(act)

                def split_out(i):
                    act.wait_ge(slab_in[i], slab_loads("out", i, L))
                    A_(fr(hiO[i]), slab[i][:, :].rearrange("p (k n) -> p k n", k=8), ACT.Copy).then_inc(d_hi.sem, 1)

                for h in range(MH):
                    act.wait_ge(ms_E.sem, ms_E.at(h + 1, L))
                    A_(Es[0:TS, :], Es[0:TS, :], ACT.Exp, bias=RT[0:TS, 4, 0, h:h + 1]).then_inc(ms_W.sem, 1)
                    if h == 1:
                        split_out(0)
                act.wait_ge(hs_var.sem, hs_var.at(1, L))
                A_(h_small[0:TS, 8:12], h_small[0:TS, 8:12], ACT.Sqrt).then_inc(hs_root.sem, 1)
                act.drain().then_inc(stage_done, 1)
                act.wait_ge(stage_done, stage_end(11, L))
                stand_alone(act)
                act.drain().then_inc(stage_done, 1)
                act.wait_ge(stage_done, stage_end(12, L))
                stand_alone(act)
                for k in range(KC):
                    A_(fr(hiX[:, k, :]), xnT[:, k, :], ACT.Copy).then_inc(x_hi.sem, 1)
                split_out(1)
                act.drain().then_inc(stage_done, 1)
                act.wait_ge(stage_done, stage_end(13, L))
                stand_alone(act)
                norm_act(NRM["n2"], L)
                modulate(NRM["n2"], 24, L)
                def split_w(q, cd, wait=True):
                    src = slab[(2, 0)[q % 4 // 2]][:, :].rearrange("p (k h n) -> p k h n", k=8, h=2)
                    cc = 128 * (q % 2)
                    if wait:
                        act.wait_ge(g_acc.sem, g_acc.at(cd - 1, L))
                    A_(fr(hiU[:, q % 2, :, :, :]), src[:, :, :, cc:cc + 128], ACT.Copy).then_inc(w_hi.sem, 1)

                act.wait_ge(slab_in[2], slab_loads("ffn", 2, L))
                split_w(0, 0, False)
                act.drain().then_inc(stage_done, 1)
                act.wait_ge(stage_done, stage_end(14, L))
                stand_alone(act)

                def u_chunk(s, cd):
                    act.wait_ge(u_acc.sem, u_acc.at(cd + 1, L))
                    act.wait_ge(u_cv.sem, u_cv.at(cd - 1, L))
                    A_(up[:, s, 2:2 + HALF], ps[0][:, 0:HALF], ACT.Copy)
                    A_(up[:, s, 2 + HALF:2 + SEQ], ps[1][:, 0:SEQ - HALF], ACT.Copy)
                    A_(up[:, s, 2 + SEQ:UPW].rearrange("p (b t) -> p b t", b=NB)[:, :, 2:],
                       ps[1][:, SEQ - HALF:HALF].rearrange("p (b t) -> p b t", b=NB), ACT.Copy).then_inc(u_cp.sem, 1)
                    act.wait_ge(u_cv.sem, u_cv.at(cd + 1, L))
                    A_(cv[:, s, 0:UPW - 2], cv[:, s, 0:UPW - 2], ACT.Silu, bias=cbias[:, s:s + 1]).then_inc(u_si.sem, 1)

                def split_h(q, cd):
                    act.wait_ge(u_h.sem, u_h.at(cd + 1, L))
                    A_(fr(hiH[:, q, :]), hid[:, q, :], ACT.Copy).then_inc(h_hi.sem, 1)

                def split_down(part, n_k):
                    A_(fr(hiD[:, n_k * part:n_k * part + n_k, :]),
                       slab[1][:, n_k * D * part:n_k * D * (part + 1)].rearrange("p (k n) -> p k n", k=n_k), ACT.Copy
                       ).then_inc(d_hi.sem, 1)

                for k in range(KC):
                    A_(fr(hiX[:, k, :]), xnT[:, k, :], ACT.Copy).then_inc(x_hi.sem, 1)
                split_w(1, 1, False)
                with act.Fori(0, NG) as j:
                    for q in range(4):
                        cd = j * 4 + q
                        u_chunk(q % 2, cd)
                        if q % 2 == 0:
                            i = (0, 5)[q // 2]
                            act.wait_ge(slab_in[i % NSLAB], slab_loads("ffn", i, L, j))
                        split_w(q + 2, cd + 2)
                        split_h(q, cd)
                        if q == 1:
                            act.wait_ge(slab_in[1], slab_loads("ffn", 1, L, j))
                        if q in (1, 2):
                            split_down(q - 1, 2)
                for q in range(2):
                    u_chunk(q, 4 * NG + q)
                    if q == 0:
                        act.wait_ge(slab_in[1], slab_loads("ffn", 16, L))
                        for part in range(2):
                            split_down(part, 1)
                    split_h(q, 4 * NG + q)
                for c in range(FC):
                    act.wait_ge(ul_t.sem, ul_t.at(c + 1, L))
                    A_(ulrow[0:18, 128 * c:128 * c + 128], ps[c % 2][0:18, 0:128], ACT.Copy).then_inc(ul_c.sem, 1)
                act.drain().then_inc(stage_done, 1)
                act.wait_ge(stage_done, stage_end(15, L))
                stand_alone(act)

            norm_act(dict(sq=final_sq, used=final_used, var=final_var, root=final_sqrt))
            for n in range(10):
                M = 128 if n < 8 else TS
                act.wait_ge(final_tr.sem, final_tr.at(n + 1))
                A_(ybuf[0:M, n, :], ps[4 + n % 4][0:M, :], ACT.Copy).then_inc(final_copy.sem, 1)

        @block.vector
        def _(dve):
            V = nc.vector
            tt, ts_, stt, cp, red = V.tensor_tensor, V.tensor_scalar, V.scalar_tensor_tensor, V.tensor_copy, V.tensor_reduce
            drain = dve.drain
            for s in (u_cv, u_h, y_add):
                dve.sem_inc(s.sem, s.credit)
            V.memset(cT[:, :, :], 0.0)
            drain()
            dve.wait_ge(pro_ct, 1)
            cp(cT[:, :, 0:9], ps[7][:, 0:72].rearrange("p (k r) -> p k r", k=KC))
            for k in range(KC):
                dve.wait_ge(pro_xt, k + 1)
                cp(xT[:, k, SEQ:TT], ps[2 * (k % 3) + 1][:, 0:TS]).then_inc(pro_copy_s, 1)

            def low(dst, hi):
                return tt(fr(dst), dst, fr(hi).bitcast(F), ALU.subtract)

            def norm_rstd(S, L=0):
                dve.wait_ge(S["used"].sem, S["used"].at(KC, L))
                ts_(rstd[:, 0:HALF], ps[0][:, 0:HALF], 1.0 / D, EPS, ALU.mult, ALU.add)
                ts_(rstd[:, HALF:TT], ps[1][:, 0:HALF], 1.0 / D, EPS, ALU.mult, ALU.add).then_inc(S["var"].sem, 1)
                dve.wait_ge(S["root"].sem, S["root"].at(1, L))
                V.reciprocal(rstd[:, :], rstd[:, :])
                drain()

            def norm_dve(S, norm, scale, shift, L):
                stt(scale_n[:, :, :], modT[:, scale:scale + KC, :], 1.0, bc(colsA[:, norm:norm + KC], 2, 9), ALU.add, ALU.mult)
                norm_rstd(S, L)
                for k in range(KC):
                    tt(xnT[:, k, :], xT[:, k, :], rstd[:, :], ALU.mult).then_inc(S["xr"].sem, 1)
                drain()
                d = xnT[:, :, SEQ:TT].rearrange("p k (b t) -> p k b t", b=NB)
                tt(d, d, bc(scale_n[:, :, 1:9], 3, NT), ALU.mult)
                drain()
                tt(d, d, bc(modT[:, shift:shift + KC, 1:9], 3, NT), ALU.add)

            with dve.Fori(0, DEPTH) as L:
                dve.drain().then_inc(stage_done, 1)
                dve.wait_ge(stage_done, stage_end(1, L))
                stand_alone(dve)
                dve.wait_ge(rows_tr.sem, rows_tr.at(1, L))
                cp(colsA[:, :], ps[6][:, 0:64])
                cp(colsB[:, :], ps[6][:, 64:160])
                dve.drain().then_inc(stage_done, 1)
                dve.wait_ge(stage_done, stage_end(2, L))
                stand_alone(dve)
                tt(modT[:, :, :], ps[7][:, 0:432].rearrange("p (c r) -> p c r", c=48), bc(colsA[:, 16:64], 2, 9), ALU.add)
                drain()
                norm_dve(NRM["n1"], 0, 8, 0, L)

                def low_in(i):
                    n = 8 * IN_SLABS[i][1]
                    dve.wait_ge(d_hi.sem, d_hi.at(i + 1, L))
                    low(slab[i % 2][:, 0:n], hiW[i % 2][:, 0:n]).then_inc(d_lo.sem, 1)

                low_in(0)
                dve.drain().then_inc(stage_done, 1)
                dve.wait_ge(stage_done, stage_end(3, L))
                stand_alone(dve)
                for k in range(KC):
                    dve.wait_ge(x_hi.sem, x_hi.at(k + 1, L))
                    low(xnT[:, k, :], hiXi[:, k, :]).then_inc(x_lo.sem, 1)
                for i, (c0, cw) in enumerate(IN_SLABS):
                    if i + 1 < 6:
                        low_in(i + 1)
                    for t in range(5):
                        n = 5 * i + t
                        if n % 2 == 1:
                            M = 128 if t < 4 else TS
                            dst = proj[:, t, c0:c0 + cw] if t < 4 else proj_s[:, c0:c0 + cw]
                            dve.wait_ge(in_acc.sem, in_acc.at(n + 1, L))
                            cp(dst, ps[n % 8][0:M, 0:cw]).then_inc(in_dve.sem, 1)
                dve.drain().then_inc(stage_done, 1)
                dve.wait_ge(stage_done, stage_end(4, L))
                stand_alone(dve)
                bif = rows_bc[:, 512:520]
                tt(proj[:, :, C_IF:C_IF + 8], proj[:, :, C_IF:C_IF + 8], bc(bif, 1, PT_), ALU.add)
                tt(proj_s[:, C_IF:C_IF + 8], proj_s[:, C_IF:C_IF + 8], rows_bc[0:TS, 512:520], ALU.add).then_inc(if_ready.sem, 1)
                dve.wait_ge(if_tr.sem, if_tr.at(1, L))
                cp(rr[:, 0, 0:SEQ], ps[0][0:MH, :])
                cp(row8[:, 0:SEQ], ps[1][0:MH, :])
                cp(rr[:, 0, SEQ:TT], ps[2][0:MH, 0:TS])
                cp(row8[:, SEQ:TT], ps[2][0:MH, TS:2 * TS])
                V.memset(rr[:, 6, 0:SEQ], 0.0)
                cp(rr[:, 6, SEQ:TT].rearrange("p (b t) -> p b t", b=NB), bc(m0s[:, :], 2, NT))
                drain()
                stt(rr[:, 4, :], row8[:, :], -1.0, row8[:, :], ALU.mult, ALU.max).then_inc(ml_abs.sem, 1)

                dve.wait_ge(ml_ln.sem, ml_ln.at(1, L))
                stt(rr[:, 4, :], row8[:, :], 0.0, rr[:, 5, :], ALU.min, ALU.subtract)
                drain()
                V.tensor_tensor_scan(rr[:, 5, :], seqc[:, 0, :], rr[:, 4, :], 0.0, ALU.mult, ALU.add)
                drain()
                tt(rr[:, 0, :], rr[:, 0, :], rr[:, 5, :], ALU.subtract)
                drain()
                tt(rr[:, 4, :], rr[:, 0, :], rr[:, 6, :], ALU.max)
                drain()
                V.tensor_tensor_scan(row8[:, :], seqc[:, 1, :], rr[:, 4, :], 0.0, ALU.add, ALU.max)
                drain()
                tt(rr[:, 2, :], rr[:, 5, :], row8[:, :], ALU.add)
                tt(rr[:, 4, :], rr[:, 5, :], row8[:, :], ALU.add)
                ts_(rr[:, 7, :], row8[:, :], -1.0, None, ALU.mult)
                ts_(negG_s[:, :], row8[:, SEQ:TT], -1.0, None, ALU.mult)
                ts_(rr[:, 1, 0:SEQ], rr[:, 0, 0:SEQ], row8[:, SEQ - 1:SEQ], None, ALU.subtract)
                gb = row8[:, SEQ:TT].rearrange("p (b t) -> p b t", b=NB)[:, :, NT - 1]
                tt(rr[:, 1, SEQ:TT].rearrange("p (b t) -> p b t", b=NB), rr[:, 0, SEQ:TT].rearrange("p (b t) -> p b t", b=NB),
                   bc(gb, 2, NT), ALU.subtract)
                tt(rr[:, 3, :], rr[:, 6, :], row8[:, :], ALU.subtract)
                dve.drain().then_inc(ml_rows.sem, 1)
                dve.wait_ge(ml_colt.sem, ml_colt.at(1, L))
                cp(RT[:, 0:4, :, :].rearrange("p t q h -> p (t q h)"), ps[3][:, 0:64])
                cp(RT[0:TS, 4, :, :].rearrange("p q h -> p (q h)"), ps[3][0:TS, 64:80])
                dve.drain().then_inc(stage_done, 1)
                dve.wait_ge(stage_done, stage_end(5, L))
                stand_alone(dve)
                tt(kw[:, :, :].rearrange("p t (h d) -> p t h d", h=MH),
                             proj[:, :, C_MK:C_MK + 256].rearrange("p t (h d) -> p t h d", h=MH),
                             bc(RT[:, 0:4, 1, :], 3, DK), ALU.mult).then_inc(ml_kw.sem, 1)

                def rope(x, P, nh, c, s_, nt):
                    x1, x2 = x[:, :, :, 0:32], x[:, :, :, 32:64]
                    n = nt * nh * 32
                    t = [rope_t[0:P, r, 0:n].rearrange("p (t h d) -> p t h d", t=nt, h=nh) for r in range(4)]
                    cb, sb_ = bc(c, 2, nh), bc(s_, 2, nh)
                    tt(t[0], x1, cb, ALU.mult)
                    tt(t[1], x2, sb_, ALU.mult)
                    tt(t[2], x1, sb_, ALU.mult)
                    tt(t[3], x2, cb, ALU.mult)
                    drain()
                    tt(x1, t[0], t[1], ALU.subtract)
                    tt(x2, t[2], t[3], ALU.add)
                    drain()

                def rope_prompt(c, nh, t0, t1):
                    rope(proj[:, t0:t1, c:c + 64 * nh].rearrange("p t (h d) -> p t h d", h=nh), 128, nh, cos[:, t0:t1, :],
                         sin[:, t0:t1, :], t1 - t0)

                def rope_decode(c, nh):
                    rope(proj_s[:, c:c + 64 * nh].rearrange("p (t h d) -> p t h d", t=1, h=nh), TS, nh, cos[0:TS, 4:5, :],
                         sin[0:TS, 4:5, :], 1)

                def rotations(h):
                    if h == 0:
                        rope_prompt(C_KC, 2, 0, PT_)
                        rope_prompt(C_KS, 2, 0, PT_)
                        rope_decode(C_KC, 2)
                        rope_decode(C_KS, 2)
                    if h == 1:
                        rope_prompt(C_KW, 2, 0, PT_)
                        rope_decode(C_KW, 2)
                        dve.drain().then_inc(roped.sem, 1)
                        rope_prompt(C_Q, 8, 0, 1)
                    if h == 2:
                        rope_prompt(C_Q, 8, 1, 2)
                        rope_prompt(C_Q, 8, 2, 3)
                    if h == 3:
                        rope_prompt(C_Q, 8, 3, 4)
                        rope_decode(C_Q, 8)

                wo = [0, 512, 896, 1152]
                for h in range(MH):
                    dve.wait_ge(ml_g.sem, ml_g.at(h + 1, L))
                    for i in range(PT_):
                        ins = tt(E[:, wo[i]:wo[i] + 128], ps[0][:, 128 * i:128 * i + 128], K["causalT"], ALU.add)
                    ins.then_inc(ml_diag.sem, 1)
                    if h:
                        dve.wait_ge(ml_num.sem, ml_num.at(h, L))
                    for i in range(PT_):
                        n = 128 * (PT_ - i)
                        dve.wait_ge(ml_qk.sem, ml_qk.at(4 * h + i + 1, L))
                        dve.wait_ge(ml_E.sem, ml_E.at(4 * h + i + 1, L))
                        tt(W[:, wo[i]:wo[i] + n], E[:, wo[i]:wo[i] + n], ps[1 + i % 2][:, 0:n], ALU.mult).then_inc(ml_W.sem, 1)
                    rotations(h)
                    dve.wait_ge(ml_num.sem, ml_num.at(h + 1, L))
                    ts_(hden, ps[4][:, 0:4], -1.0, None, ALU.mult)
                    drain()
                    tt(hden, hden, ps[4][:, 0:4], ALU.max)
                    drain()
                    tt(hden, hden, RT[:, 0:4, 2, h], ALU.max)
                    drain()
                    V.reciprocal(hden, hden)
                    drain()
                    tt(proj[:, :, C_MV + DV * h:C_MV + DV * h + DV],
                                   ps[3][:, :].rearrange("p (t d) -> p t d", t=PT_), bc(hden, 2, DV), ALU.mult).then_inc(ml_numc.sem, 1)
                drain()
                Hv = proj[:, :, C_MV:C_MV + 512].rearrange("p t (h d) -> p t h d", h=MH)
                Hsq = work[:, 0:2048].rearrange("p (t h d) -> p t h d", t=PT_, h=MH)
                tt(Hsq, Hv, Hv, ALU.mult)
                drain()
                red(hvar.rearrange("p (t h) -> p t h", t=PT_), Hsq, X, ALU.add)
                drain()
                ts_(hvar, hvar, 1.0 / DV, EPS, ALU.mult, ALU.add).then_inc(h_var.sem, 1)
                dve.wait_ge(h_root.sem, h_root.at(1, L))
                V.reciprocal(hvar, hvar)
                drain()
                tt(Hv, Hv, bc(hvar.rearrange("p (t h) -> p t h", t=PT_), 3, DV), ALU.mult)
                drain()
                hflat = proj[:, :, C_MV:C_MV + 512]
                tt(hflat, hflat, bc(rows_bc[:, 0:512], 1, PT_), ALU.mult)
                drain()
                tt(proj[:, :, C_MO:C_MO + 512], proj[:, :, C_MO:C_MO + 512], hflat, ALU.mult)
                dve.drain().then_inc(stage_done, 1)
                dve.wait_ge(stage_done, stage_end(6, L))
                stand_alone(dve)
                for n in range(1, 12, 2):
                    dve.wait_ge(th_tr.sem, th_tr.at(n + 1, L))
                    ts_(TH[0:64, n, :], ps[n % 4][0:64, :], HD ** -0.5 if n < 8 else 1.0, None, ALU.mult).then_inc(th_dve.sem, 1)
                dve.wait_ge(cm_mean.sem, cm_mean.at(1, L))
                cp(KmT[0:64, :], ps[4][0:64, 0:16])
                vr = bc(ps[5][0:64, 0:128].rearrange("p (k d) -> p k d", k=KV), 2, AG)
                tt(VmBD[0:64, :].rearrange("p (k g d) -> p k g d", k=KV, g=AG), vr,
                                bc(K["hmask"][0:64, :].rearrange("p (k g) -> p k g", k=KV), 3, HD), ALU.mult).then_inc(cm_meanc.sem, 1)
                dve.wait_ge(cm_s.sem, cm_s.at(1, L))
                c4 = cS.rearrange("p (t h n) -> p t h n", t=PT_, h=AH)
                smv = sm[:, 0:32].rearrange("p (t h) -> p t h", t=PT_)
                tt(c4, ps[6][:, 0:256].rearrange("p (t h n) -> p t h n", t=PT_, h=AH),
                   bc(view("cmpadd", "p (t n) -> p t n", t=PT_), 2, AH), ALU.add)
                drain()
                red(smv, c4, X, ALU.max)
                drain()
                tt(c4, c4, bc(smv, 3, 8), ALU.subtract).then_inc(cm_sub.sem, 1)
                dve.wait_ge(cm_exp.sem, cm_exp.at(1, L))
                tt(c4, c4, bc(view("cmp01", "p (t n) -> p t n", t=PT_), 2, AH), ALU.mult)
                drain()
                red(smv, c4, X, ALU.add)
                drain()
                ts_(sm[:, 32:64], sm[:, 0:32], 0.5, None, ALU.max)
                drain()
                V.reciprocal(sm[:, 64:96], sm[:, 32:64])
                drain()
                gv = gates[:, :, :].rearrange("p t (h b) -> p t h b", b=3)
                tt(smv, sm[:, 64:96].rearrange("p (t h) -> p t h", t=PT_), gv[:, :, :, 0], ALU.mult)
                drain()
                tt(c4, c4, bc(smv, 3, 8), ALU.mult).then_inc(cm_p.sem, 1)
                dve.wait_ge(cm_t.sem, cm_t.at(1, L))
                cp(PTb[0:64, 0, :], ps[7][0:64, :]).then_inc(cm_tc.sem, 1)
                dve.drain().then_inc(stage_done, 1)
                dve.wait_ge(stage_done, stage_end(7, L))
                stand_alone(dve)
                with dve.Fori(0, 4) as j:
                    def maxed(u):
                        t = u % 4
                        s = ps[SBANK[u % 4]]
                        dve.wait_ge(a_s.sem, a_s.at(u + 1, L, j))
                        tt(s[:, 128 * t:128 * t + 128], s[:, 128 * t:128 * t + 128], K["causal"], ALU.add)
                        drain()
                        red(nmax[:, u:u + 1], s[:, 0:128 * t + 128], X, ALU.max, negate=True).then_inc(a_max.sem, 1)

                    def added(u):
                        hh, br, t = u // 8, u // 4 % 2, u % 4
                        dve.wait_ge(a_pv.sem, a_pv.at(u + 1, L, j))
                        V.reciprocal(rg[:, 0:1], den[:, u:u + 1])
                        drain()
                        tt(rg[:, 1:2], rg[:, 0:1], gnow[:, t, hh, br:br + 1], ALU.mult)
                        drain()
                        o_ = proj[:, t, bass.ds(j * 64 + 256 * hh, HD)]
                        stt(o_, ps[5 + u % 2][:, 0:HD], rg[:, 1:2], o_, ALU.mult, ALU.add).then_inc(a_acc.sem, 1)

                    ggv = gates[:, :, :].rearrange("p t (k g b) -> p t k g b", k=KV, g=AG)
                    for hh in range(2):
                        ins = cp(gnow[:, :, hh, :], ggv[:, :, hh, bass.ds(j, 1), 1:3].squeeze(2))
                    ins.then_inc(g_stage.sem, 1)
                    drain()
                    maxed(0)
                    maxed(1)
                    maxed(2)
                    for u in range(U):
                        if u + 3 < U:
                            maxed(u + 3)
                        if u >= 1:
                            added(u - 1)
                    added(U - 1)
                    drain()
                dve.drain().then_inc(stage_done, 1)
                dve.wait_ge(stage_done, stage_end(8, L))
                stand_alone(dve)
                cp(Ssb[0:TS, 0:512].rearrange("p (g k d) -> p g k d", g=AG, k=KV),
                              proj_s[:, 0:512].rearrange("p (k g d) -> p g k d", k=KV, g=AG)).then_inc(d_pair.sem, 1)
                dve.wait_ge(d_tr.sem, d_tr.at(1, L))
                ts_(qTs[:, :, :].rearrange("p a b -> p (a b)"), ps[4][:, 0:128], HD ** -0.5, None, ALU.mult)
                cp(KN[:, :, :].rearrange("p a b -> p (a b)"), ps[4][:, 128:192])
                for g in range(2):
                    pr = ps[5][:, 24 * g:24 * g + 24].rearrange("p (h b) -> p b h", b=3)
                    gt_ = small[:, 0:24].rearrange("p (b h) -> p b h", b=3)
                    tt(gt_, pr, bc(K["hsel"], 1, 3), ALU.mult)
                    drain()
                    red(gq[:, g, :], gt_, X, ALU.add)
                    drain()
                V.memset(aTs[:, :, :], 0.0)
                V.memset(Qbd[:, :, :], 0.0)
                V.memset(P4, 0.0)
                dve.drain().then_inc(stage_done, 1)
                dve.wait_ge(stage_done, stage_end(9, L))
                stand_alone(dve)
                for j in range(2):
                    for k in range(KV):
                        src = qTs[64 * k:64 * k + 64, :, bass.ds(j * 16, 16)].rearrange("p g (b t) -> p b g t", b=4)
                        cp(Qbd[64 * k:64 * k + 64, :, 16 * k:16 * k + 16].rearrange("p b (g t) -> p b g t", g=AG), src)
                    cp(rownow.rearrange("p h t -> p (h t)"), K["rowtok"][:, bass.ds(j * 256, 256)])
                    cp(gq_now[:, :], gq[:, bass.ds(j, 1), :].squeeze(1))
                    dve.drain().then_inc(d_q.sem, 1)
                    dve.wait_ge(d_cs.sem, d_cs.at(1, L, j))
                    red(small[:, 0:1], ps[4][:, 0:16], X, ALU.max, negate=True).then_inc(d_csub.sem, 1)
                    dve.wait_ge(d_cexp.sem, d_cexp.at(1, L, j))
                    V.reciprocal(small[:, 6:7], small[:, 1:2])
                    drain()
                    ts_(imp[:, 0:16], imp[:, 0:16], small[:, 6:7], None, ALU.mult)
                    drain()
                    for b in range(4):
                        r = slice(32 * b, 32 * b + 32)
                        ins = ts_(P4[r, 16 * b:16 * b + 16], imp[r, 0:16], gq_now[r, 0:1], None, ALU.mult)
                    ins.then_inc(d_cp.sem, 1)
                    dve.wait_ge(d_imp.sem, d_imp.at(1, L, j))
                    red(small[:, 7:8], ps[2][:, 1:16], X, ALU.min)
                    drain()
                    ts_(small[:, 16:31], ps[2][:, 1:16], small[:, 7:8], None, ALU.is_equal)
                    drain()
                    tt(small[:, 16:31], small[:, 16:31], K["iota"], ALU.mult)
                    drain()
                    red(small[:, 8:9], small[:, 16:31], X, ALU.max)
                    V.memset(small[:, 32:33], 0.0)
                    drain()
                    ts_(small[:, 33:48], K["iota"], small[:, 8:9], NEG, ALU.is_equal, ALU.mult)
                    drain()
                    newa = K["newadd"][:, bass.ds(j * TS, TS)]
                    for br in range(2):
                        nt = (8, 4)[br]
                        wd = 128 * nt + TS
                        dve.wait_ge(d_s.sem, d_s.at(br + 1, L, j))
                        if br == 0:
                            for q in range(2):
                                tt(Ssb[:, 512 * q:512 * q + 512].rearrange("p (n d) -> p n d", n=8),
                                   ps[5 + q][:, :].rearrange("p (n d) -> p n d", n=8),
                                   bc(small[:, 32 + 8 * q:40 + 8 * q], 2, BLK), ALU.add)
                        else:
                            dve.wait_ge(d_pt.sem, d_pt.at(1, L, j))
                            cp(Ssb[:, 0:512], ps[5][:, :])
                            drain()
                            f4 = Ssb[:, 0:512].rearrange("p (n d) -> p n d", n=4)[:, :, 0]
                            tt(f4, f4, K["winadd"], ALU.add)
                        tt(Ssb[:, 128 * nt:wd], ps[7][:, 0:TS], newa, ALU.add)
                        drain()
                        red(small[:, 2 + br:3 + br], Ssb[:, 0:wd], X, ALU.max, negate=True).then_inc(d_max.sem, 1)
                    dve.wait_ge(d_pv.sem, d_pv.at(2, L, j))
                    V.reciprocal(small[:, 9:11], small[:, 4:6])
                    cp(cmb, ps[4][:, 128:256])
                    drain()
                    tt(small[:, 11:13], small[:, 9:11], gq_now[:, 1:3], ALU.mult)
                    drain()
                    stt(cmb, ps[4][:, 256:384], small[:, 11:12], cmb, ALU.mult, ALU.add)
                    drain()
                    stt(cmb, ps[2][:, 128:256], small[:, 12:13], cmb, ALU.mult, ALU.add).then_inc(d_cmb.sem, 1)
                    dve.wait_ge(d_out.sem, d_out.at(1, L, j))
                    tt(aTs[:, :, :].rearrange("p a b -> p (a b)"), aTs[:, :, :].rearrange("p a b -> p (a b)"),
                                 ps[3][:, 256:384], ALU.add).then_inc(d_add.sem, 1)
                    drain()
                dve.drain().then_inc(stage_done, 1)
                dve.wait_ge(stage_done, stage_end(10, L))
                stand_alone(dve)
                def low_out(i):
                    dve.wait_ge(d_hi.sem, d_hi.at(6 + i + 1, L))
                    low(slab[i][:, :].rearrange("p (k n) -> p k n", k=8), hiO[i]).then_inc(d_lo.sem, 1)

                tt(kws.rearrange("p (h d) -> p h d", h=MH), proj_s[:, C_MK:C_MK + 256].rearrange("p (h d) -> p h d", h=MH),
                   bc(RT[0:TS, 4, 1, :], 2, DK), ALU.mult)
                drain()
                tt(awl[0:TS, :, :], bc(K["lastT"][0:TS, :], 2, MH), bc(RT[0:TS, 4, 3, :], 1, NB), ALU.mult).then_inc(ms_kq.sem, 1)
                dve.wait_ge(ms_dec.sem, ms_dec.at(1, L))
                cp(decayb[0:64, :], ps[6][0:64, 0:NB * MH])
                dve.wait_ge(st_in, L * 32 + 32)
                Cv = Cst[0:64, :, :].rearrange("p (b h) d -> p b h d", h=MH)
                Cn = Cnew[0:64, :, :].rearrange("p (b h) d -> p b h d", h=MH)
                dv_, nv, nn = [a[0:64, :].rearrange("p (b h) -> p b h", h=MH) for a in (decayb, nst, nnew)]
                for h in range(MH):
                    if h:
                        dve.wait_ge(ms_C.sem, ms_C.at(2 * h, L))
                    tt(Qm[0:64, :, :], bc(mqks[:, h, :], 1, NB), view("inbatch", "p (b t) -> p b t", b=NB)[0:64], ALU.mult)
                    tt(kwb[0:TS, :, :], bc(kws[:, DK * h:DK * h + DK], 1, NB), bc(K["inbatchT"][0:TS, :], 2, DK),
                                ALU.mult).then_inc(ms_q.sem, 1)
                    dve.wait_ge(ms_g.sem, ms_g.at(h + 1, L))
                    tt(Es[0:TS, :], ps[0][0:TS, 0:TS], K["samebatch"][0:TS, :], ALU.add).then_inc(ms_E.sem, 1)
                    dve.wait_ge(ms_W.sem, ms_W.at(h + 1, L))
                    tt(Ws[0:TS, :], Es[0:TS, :], ps[1][0:TS, 0:TS], ALU.mult).then_inc(ms_Wd.sem, 1)
                    tt(Cn[:, :, h, :], Cv[:, :, h, :], bc(dv_[:, :, h], 2, DV), ALU.mult)
                    tt(nn[:, :, h], nv[:, :, h], dv_[:, :, h], ALU.mult)
                    if h == 2:
                        low_out(0)
                    dve.wait_ge(ms_num.sem, ms_num.at(h + 1, L))
                    cp(hs2[0:TS, 0:DV + 1], ps[2][0:TS, 0:DV + 1])
                    drain()
                    stt(nd[0:TS, :], ps[3][0:TS, 0:DV + 1], RT[0:TS, 4, 3, h:h + 1], hs2[0:TS, 0:DV + 1], ALU.mult, ALU.add)
                    drain()
                    d1 = h_small[0:TS, 0:1]
                    stt(d1, nd[0:TS, DV:DV + 1], -1.0, nd[0:TS, DV:DV + 1], ALU.mult, ALU.max)
                    drain()
                    tt(d1, d1, RT[0:TS, 4, 2, h:h + 1], ALU.max)
                    drain()
                    V.reciprocal(d1, d1)
                    drain()
                    ts_(hs[0:TS, DV * h:DV * h + DV], nd[0:TS, 0:DV], d1, None, ALU.mult).then_inc(ms_numc.sem, 1)
                    for half in range(2):
                        r = slice(4 * half, 4 * half + 4)
                        dve.wait_ge(ms_C.sem, ms_C.at(2 * h + half + 1, L))
                        tt(Cn[:, r, h, :], Cn[:, r, h, :], ps[4 + half][0:64, :].rearrange("p (b d) -> p b d", b=4), ALU.add)
                        tt(nn[:, r, h], nn[:, r, h], ps[6 + half][0:64, 0:4], ALU.add).then_inc(ms_Cc.sem, 1)
                drain()
                h3 = hs[0:TS, :].rearrange("p (h d) -> p h d", h=MH)
                tt(hs2[0:TS, :], hs[0:TS, :], hs[0:TS, :], ALU.mult)
                drain()
                red(h_small[0:TS, 4:8], hs2[0:TS, :].rearrange("p (h d) -> p h d", h=MH), X, ALU.add)
                drain()
                ts_(h_small[0:TS, 8:12], h_small[0:TS, 4:8], 1.0 / DV, EPS, ALU.mult, ALU.add).then_inc(hs_var.sem, 1)
                dve.wait_ge(hs_root.sem, hs_root.at(1, L))
                V.reciprocal(h_small[0:TS, 12:16], h_small[0:TS, 8:12])
                drain()
                tt(h3, h3, bc(h_small[0:TS, 12:16], 2, DV), ALU.mult)
                drain()
                tt(hs[0:TS, :], hs[0:TS, :], rows_bc[0:TS, 0:512], ALU.mult)
                drain()
                tt(hs[0:TS, :], hs[0:TS, :], proj_s[:, C_MO:C_MO + 512], ALU.mult)
                dve.drain().then_inc(stage_done, 1)
                dve.wait_ge(stage_done, stage_end(11, L))
                stand_alone(dve)
                dve.wait_ge(ms_t.sem, ms_t.at(1, L))
                cp(xnT[:, 4:8, SEQ:TT], ps[0][:, 0:128].rearrange("p (c t) -> p c t", c=4))
                cp(xnT[:, 0:4, SEQ:TT], aTs[:, :, :])
                dve.drain().then_inc(stage_done, 1)
                dve.wait_ge(stage_done, stage_end(12, L))
                stand_alone(dve)

                def residual(cx, lo, hi, mod):
                    x_ = xT[:, cx, :].squeeze(1) if not isinstance(cx, int) else xT[:, cx, :]
                    gp = modT[:, mod, 0:1] if isinstance(cx, int) else modT[:, mod, 0:1].squeeze(1)
                    gs = modT[:, mod, 1:9] if isinstance(cx, int) else modT[:, mod, 1:9].squeeze(1)
                    tmp = tail_g
                    tt(tmp.rearrange("p (b t) -> p b t", b=NB), hi[:, SEQ - HALF:HALF].rearrange("p (b t) -> p b t", b=NB),
                       bc(gs, 2, NT), ALU.mult)
                    stt(x_[:, 0:HALF], lo[:, 0:HALF], gp, x_[:, 0:HALF], ALU.mult, ALU.add)
                    stt(x_[:, HALF:SEQ], hi[:, 0:SEQ - HALF], gp, x_[:, HALF:SEQ], ALU.mult, ALU.add)
                    drain()
                    return tt(x_[:, SEQ:TT], x_[:, SEQ:TT], tmp, ALU.add)

                for k in range(KC):
                    dve.wait_ge(x_hi.sem, x_hi.at(KC + k + 1, L))
                    low(xnT[:, k, :], hiX[:, k, :]).then_inc(x_lo.sem, 1)
                low_out(1)
                for c in range(8):
                    dve.wait_ge(o_acc.sem, o_acc.at(c + 1, L))
                    residual(c, ps[2 * (c % 4)], ps[2 * (c % 4) + 1], 16 + c).then_inc(o_add.sem, 1)
                    drain()
                dve.drain().then_inc(stage_done, 1)
                dve.wait_ge(stage_done, stage_end(13, L))
                stand_alone(dve)
                norm_dve(NRM["n2"], 8, 32, 24, L)
                V.memset(up[:, :, 0:2], 0.0)
                dve.wait_ge(cv_t.sem, cv_t.at(1, L))
                cp(convS[:, :, :].rearrange("p c n -> p (c n)"), ps[2][:, 0:16 * FC])

                def split_w(q, cd):
                    src = slab[(2, 0)[q % 4 // 2]][:, :].rearrange("p (k h n) -> p k h n", k=8, h=2)
                    cc = 128 * (q % 2)
                    dve.wait_ge(w_hi.sem, w_hi.at(cd + 1, L))
                    low(src[:, :, :, cc:cc + 128], hiU[:, q % 2, :, :, :]).then_inc(w_lo.sem, 1)

                split_w(0, 0)
                dve.drain().then_inc(stage_done, 1)
                dve.wait_ge(stage_done, stage_end(14, L))
                stand_alone(dve)

                def conv(s, cd):
                    one = isinstance(cd, int)
                    cix = cd if one else bass.ds(cd, 1)
                    hist = convS[:, cix, :] if one else convS[:, cix, :].squeeze(1)
                    cp(up[:, s, 2 + SEQ:UPW].rearrange("p (b t) -> p b t", b=NB)[:, :, 0:2],
                       hist.rearrange("p (b t) -> p b t", b=NB))
                    for w_ in range(3):
                        cp(cwt[:, 3 * s + w_:3 * s + w_ + 1], colsB[:, bass.ds(cd + FC * w_, 1)])
                    cp(cbias[:, s:s + 1], colsB[:, bass.ds(cd + 66, 1)])
                    drain()
                    dve.wait_ge(u_cp.sem, u_cp.at(cd + 1, L))
                    n = UPW - 2
                    ts_(cv[:, s, 0:n], up[:, s, 0:n], cwt[:, 3 * s:3 * s + 1], None, ALU.mult)
                    drain()
                    stt(cv[:, s, 0:n], up[:, s, 1:1 + n], cwt[:, 3 * s + 1:3 * s + 2], cv[:, s, 0:n], ALU.mult, ALU.add)
                    ul = uLast[:, cix, :] if one else uLast[:, cix, :].squeeze(1)
                    cp(ul[:, 0:2], up[:, s, SEQ:SEQ + 2])
                    cp(ul[:, 2:18].rearrange("p (b t) -> p b t", b=NB),
                       up[:, s, 2 + SEQ:UPW].rearrange("p (b t) -> p b t", b=NB)[:, :, 4:6])
                    drain()
                    stt(cv[:, s, 0:n], up[:, s, 2:2 + n], cwt[:, 3 * s + 2:3 * s + 3], cv[:, s, 0:n], ALU.mult,
                        ALU.add).then_inc(u_cv.sem, 1)

                def hidden(q, cd):
                    s = q % 2
                    dve.wait_ge(u_si.sem, u_si.at(cd + 1, L))
                    dve.wait_ge(g_acc.sem, g_acc.at(cd + 1, L))
                    tt(hid[:, q, 0:HALF], ps[2][:, 0:HALF], cv[:, s, 0:HALF], ALU.mult)
                    tt(hid[:, q, HALF:SEQ], ps[3][:, 0:SEQ - HALF], cv[:, s, HALF:SEQ], ALU.mult)
                    tt(hid[:, q, SEQ:TT].rearrange("p (b t) -> p b t", b=NB),
                       ps[3][:, SEQ - HALF:HALF].rearrange("p (b t) -> p b t", b=NB),
                       cv[:, s, 2 + SEQ:UPW].rearrange("p (b t) -> p b t", b=NB)[:, :, 0:4], ALU.mult).then_inc(u_h.sem, 1)

                def split_h(q, cd):
                    dve.wait_ge(h_hi.sem, h_hi.at(cd + 1, L))
                    low(hid[:, q, :], hiH[:, q, :]).then_inc(h_lo.sem, 1)

                def split_down(part, n_k, g):
                    dve.wait_ge(d_hi.sem, d_hi.at(2 * g + part + 9, L))
                    low(slab[1][:, n_k * D * part:n_k * D * (part + 1)].rearrange("p (k n) -> p k n", k=n_k),
                        hiD[:, n_k * part:n_k * part + n_k, :]).then_inc(d_lo.sem, 1)

                def add_y(g):
                    for c in range(8):
                        dve.wait_ge(y_acc.sem, y_acc.at(8 * g + c + 1, L))
                        b = 4 + 2 * (c % 2)
                        residual(c, ps[b], ps[b + 1], 40 + c).then_inc(y_add.sem, 1)
                        drain()

                for k in range(KC):
                    dve.wait_ge(x_hi.sem, x_hi.at(2 * KC + k + 1, L))
                    low(xnT[:, k, :], hiX[:, k, :]).then_inc(x_lo.sem, 1)
                split_w(1, 1)
                with dve.Fori(0, NG) as j:
                    for q in range(4):
                        cd = j * 4 + q
                        conv(q % 2, cd)
                        hidden(q, cd)
                        split_w(q + 2, cd + 2)
                        split_h(q, cd)
                        if q in (1, 2):
                            split_down(q - 1, 2, j)
                    add_y(j)
                for q in range(2):
                    conv(q, 4 * NG + q)
                    if q == 0:
                        for part in range(2):
                            split_down(part, 1, NG)
                    hidden(q, 4 * NG + q)
                    split_h(q, 4 * NG + q)
                add_y(NG)
                dve.drain().then_inc(stage_done, 1)
                dve.wait_ge(stage_done, stage_end(15, L))
                stand_alone(dve)

            norm_rstd(dict(used=final_used, var=final_var, root=final_sqrt))
            for k in range(KC):
                stt(xnT[:, k, :], xT[:, k, :], colsB[:, 88 + k:89 + k], rstd[:, :], ALU.mult, ALU.mult).then_inc(final_xn.sem, 1)

        @block.gpsimd
        def _(pool):
            ld = pool.dma_start
            pool.dma_start(cst[:, :], A["shape_constants"][:, 0:sum(_WIDTHS)]).then_inc(load_in, 16)
            ld(xrow[:, :, :], A["x_prompt"][0].rearrange("(t p) d -> p t d", p=128)).then_inc(load_in, 16)
            ld(crow2[0:TS, :], A["x_sample"].rearrange("b t d -> (b t) d")).then_inc(load_in, 16)
            ld(crow[0:1, :], A["c_prompt"]).then_inc(load_in, 16)
            ld(crow[1:9, :], A["c_sample"]).then_inc(load_in, 16)
            ld(pages_sb[:, :], A["page_table"].rearrange("b n -> (b n)").unsqueeze(0)).then_inc(load_in, 16)
            pool.wait_ge(load_in, PRO_LOADS)
            n_st = [0]
            ST_ALL = 16 * (3 + 2 + NB + 1 + NB + 2 + 16 + 2 + 2)

            with pool.Fori(0, DEPTH) as L:
                def put(dst, src):
                    n_st[0] += 16
                    return pool.dma_start(dst, src).then_inc(stored, 16)

                def all_stored():
                    pool.wait_ge(stored, L * ST_ALL + n_st[0])
                    stand_alone(pool)

                pool.drain().then_inc(stage_done, 1)

                pool.wait_ge(stage_done, stage_end(1, L))

                stand_alone(pool)
                r8 = lambda a: a.rearrange("(k n) -> k n", n=128)
                row = lambda name: A[name][L, :]
                for dst, src in ((rowsA[0:8, :], r8(row("norm1_g"))), (rowsA[8:16, :], r8(row("norm2_g"))),
                                 (rowsA[16:64, :], r8(row("b_mod"))),
                                 (rowsB[0:66, :], A["w_conv"][L, :, :].rearrange("w (k n) -> (w k) n", n=128)),
                                 (rowsB[66:88, :], r8(row("b_conv"))), (rowsB[88:96, :], r8(A["final_g"])),
                                 (rows_bc[:, 0:512], row("mlstm_norm_g").partition_broadcast(128)),
                                 (rows_bc[:, 512:520], row("b_if").partition_broadcast(128)),
                                 (seqc, A["shape_constants"][0:MH, sum(_WIDTHS):].rearrange("p (a n) -> p a n", a=2)),
                                 (m0s[:, :], A["state_mlstm_m"][L, :, :].rearrange("b h -> h b"))):
                    pool.dma_start(dst, src, allow_slow_non_contiguous=True).then_inc(rows_in, 16)
                pool.wait_ge(rows_in, L * ROWS_PER_LAYER + ROWS_PER_LAYER)
                stand_alone(pool)
                for n in (2, 3, 4):
                    pool.drain().then_inc(stage_done, 1)
                    pool.wait_ge(stage_done, stage_end(n, L))
                    stand_alone(pool)
                pool.wait_ge(ml_rows.sem, ml_rows.at(1, L))
                stand_alone(pool)
                put(p_m[L].rearrange("o h -> h o"), rr[:, 4, SEQ - 1:SEQ])
                for b in range(NB):
                    put(s_m[L][b].unsqueeze(1), rr[:, 4, SEQ + NT * b + NT - 1:SEQ + NT * b + NT])
                pool.drain().then_inc(stage_done, 1)
                pool.wait_ge(stage_done, stage_end(5, L))
                stand_alone(pool)
                pool.wait_ge(roped.sem, roped.at(1, L))
                stand_alone(pool)
                for o_p, o_s, c in ((p_cmp, s_cmp, C_KC), (p_sel, s_sel, C_KS), (p_win, s_win, C_KW)):
                    put(o_p[L].rearrange("o (t p) a k d -> p (o t) (a k d)", p=128), proj[:, :, c:c + 256])
                    if c == C_KW:
                        for b in range(NB):
                            put(o_s[L][b, WINDOW - NT:WINDOW].rearrange("t a k d -> t (a k d)"), proj_s[NT * b:NT * b + NT, c:c + 256])
                    else:
                        put(o_s[L].rearrange("b t a k d -> (b t) (a k d)"), proj_s[:, c:c + 256])
                pool.wait_ge(ml_Cc.sem, ml_Cc.at(MH, L))
                stand_alone(pool)
                put(p_C[L].rearrange("o h k v -> k (o h) v"), Cp[0:64, :, 0:DV])
                pool.dma_start(p_n[L].rearrange("o h k -> k (o h)"), Cp[0:64, :, DV], allow_slow_non_contiguous=True).then_inc(stored, 16)
                n_st[0] += 16
                all_stored()
                for n in (6, 7, 8):
                    pool.drain().then_inc(stage_done, 1)
                    pool.wait_ge(stage_done, stage_end(n, L))
                    stand_alone(pool)
                pool.drain().then_inc(stage_done, 1)
                pool.wait_ge(mx_t.sem, mx_t.at(8, L))
                stand_alone(pool)
                by_part = lambda a: a.rearrange("(p i) a k d -> p (i a k d)", i=4)
                for b in range(NB):
                    pool.dma_start(wpg[b].rearrange("p i c -> p (i c)"), by_part(A["cache_win_kv"][L][b])).then_inc(wpg_in[b // 4], 16)
                pool.wait_ge(stage_done, stage_end(9, L))
                stand_alone(pool)
                for b in range(NB):
                    if b % 4 == 0:
                        pool.wait_ge(wpg_in[b // 4], L * 64 + 64)
                        stand_alone(pool)
                    ob = by_part(s_win[L][b][0:WINDOW - NT])
                    for lo, hi in ((1, 113), (113, 128)):
                        put(ob[lo - 1:hi - 1], wpg[b][lo:hi].rearrange("p i c -> p (i c)"))
                all_stored()
                pool.wait_ge(d_pv.sem, d_pv.at(1, L, 1))
                stand_alone(pool)
                pool.dma_start(Cst[0:64, :, :], A["state_mlstm_C"][L].rearrange("b h k v -> k (b h) v")).then_inc(st_in, 16)
                pool.dma_start(nst[0:64, :], A["state_mlstm_n"][L].rearrange("b h k -> k (b h)"), allow_slow_non_contiguous=True).then_inc(st_in, 16)
                pool.wait_ge(st_in, L * 32 + 32)
                stand_alone(pool)
                pool.drain().then_inc(stage_done, 1)
                pool.wait_ge(stage_done, stage_end(10, L))
                stand_alone(pool)
                pool.drain().then_inc(stage_done, 1)
                pool.wait_ge(stage_done, stage_end(11, L))
                stand_alone(pool)
                put(s_C[L].rearrange("b h k v -> k (b h) v"), Cnew[0:64, :, :])
                pool.dma_start(s_n[L].rearrange("b h k -> k (b h)"), nnew[0:64, :], allow_slow_non_contiguous=True).then_inc(stored, 16)
                n_st[0] += 16
                pool.drain().then_inc(stage_done, 1)
                pool.wait_ge(stage_done, stage_end(12, L))
                stand_alone(pool)
                pool.dma_start(csrow[0:16, :], A["state_ffn_conv"][L].rearrange("b j f -> (b j) f")).then_inc(cv_in, 16)
                all_stored()
                pool.drain().then_inc(stage_done, 1)
                pool.wait_ge(stage_done, stage_end(13, L))
                stand_alone(pool)
                pool.drain().then_inc(stage_done, 1)
                pool.wait_ge(stage_done, stage_end(14, L))
                stand_alone(pool)
                pool.drain().then_inc(stage_done, 1)
                pool.wait_ge(stage_done, stage_end(15, L))
                stand_alone(pool)
                put(p_conv[L].rearrange("o j f -> (o j) f"), ulrow[0:2, :])
                put(s_conv[L].rearrange("b j f -> (b j) f"), ulrow[2:18, :])
                all_stored()
                assert n_st[0] == ST_ALL, (n_st[0], ST_ALL)
            for n in range(10):
                t, hf = n // 2, n % 2
                pool.wait_ge(final_copy.sem, final_copy.at(n + 1))
                dst = y_p[0, 128 * t:128 * t + 128, 512 * hf:512 * hf + 512] if t < 4 else \
                    y_s.rearrange("b t d -> (b t) d")[:, 512 * hf:512 * hf + 512]
                pool.dma_start(dst, ybuf[0:128 if t < 4 else TS, n, :]).then_inc(stored, 16)
            pool.wait_ge(stored, DEPTH * ST_ALL + 160)


_INS = ["x_prompt", "x_sample", "cache_cmp_kv", "cache_sel_kv", "cache_win_kv", "state_mlstm_C", "state_mlstm_n",
        "state_mlstm_m", "state_ffn_conv", "page_table", "c_prompt", "c_sample", "norm1_g", "norm2_g", "w_mod", "b_mod",
        "w_in", "b_if", "mlstm_norm_g", "w_out", "w_up", "w_conv", "b_conv", "w_down", "final_g"]
_KVS = (2, KV, HD)
_OUTS = [(1, SEQ, D), (NB, NT, D), (DEPTH, 1, SEQ) + _KVS, (DEPTH, 1, SEQ) + _KVS, (DEPTH, 1, SEQ) + _KVS,
         (DEPTH, 1, MH, DK, DV), (DEPTH, 1, MH, DK), (DEPTH, 1, MH), (DEPTH, 1, 2, FF),
         (DEPTH, NB, NT) + _KVS, (DEPTH, NB, NT) + _KVS, (DEPTH, NB, WINDOW) + _KVS,
         (DEPTH, NB, MH, DK, DV), (DEPTH, NB, MH, DK), (DEPTH, NB, MH), (DEPTH, NB, 2, FF)]


def kernel(**inputs):
    import numpy as _np
    import concourse.bacc as _bacc
    from concourse import mybir as _mybir
    from concourse.bass_utils import run_bass_kernel_spmd as _run

    nc = _bacc.Bacc("TRN2", target_bir_lowering=False, num_devices=1)
    arrays, args = {}, {}
    for name in _INS:
        a = _np.ascontiguousarray(inputs[name])
        arrays[f"in_{name}"] = a
        args[name] = nc.dram_tensor(f"in_{name}", a.shape, _mybir.dt.from_np(a.dtype), kind="ExternalInput").ap()
    c = _np.ascontiguousarray(_np.concatenate(shape_constants(), axis=1))
    arrays["in_shape_constants"] = c
    args["shape_constants"] = nc.dram_tensor("in_shape_constants", c.shape, _mybir.dt.float32, kind="ExternalInput").ap()
    outs = [nc.dram_tensor(f"out_{i}", s, _mybir.dt.float32, kind="ExternalOutput").ap() for i, s in enumerate(_OUTS)]
    trunk_program(nc, args, outs)
    r = _run(nc, [arrays], core_ids=[0])
    return tuple(r.results[0][f"out_{i}"] for i in range(len(_OUTS)))
```
